# Optimizing a Trainium2 kernel written in Bass

```python
import math
import jax, jax.numpy as jnp
from jax import lax
import numpy as np

D_MODEL = 1024
BATCH = 1
SEQ = 512
DEPTH = 2

CHUNK = 64
Q_BLOCK = 128
HEAD_DIM = 64
N_GROUP_HEADS = 4
GROUP_WIDTH = N_GROUP_HEADS * HEAD_DIM
N_GROUPS = 4
D_MIX = N_GROUPS * GROUP_WIDTH
ROPE_THETA = 500000.0
RET_THETA = 10000.0
KV_RANK = 128
IDX_HEADS = 8
IDX_DIM = 64
TOPK_MAX = 256
DIFF_HALF = HEAD_DIM // 2
EPS = 1e-6

IN_SIZES = (
    GROUP_WIDTH, KV_RANK, IDX_HEADS * IDX_DIM, IDX_DIM, IDX_HEADS, GROUP_WIDTH,
    GROUP_WIDTH, GROUP_WIDTH, GROUP_WIDTH, GROUP_WIDTH,
    GROUP_WIDTH, GROUP_WIDTH, GROUP_WIDTH, GROUP_WIDTH,
    GROUP_WIDTH, GROUP_WIDTH, GROUP_WIDTH, GROUP_WIDTH,
)
D_IN = 14 * GROUP_WIDTH + KV_RANK + IDX_HEADS * IDX_DIM + IDX_DIM + IDX_HEADS

kernel_name = 'hybrid_head_group_streaming_encoder'

def _rms(x, g=None):
    xf = x.astype(jnp.float32)
    y = xf * lax.rsqrt(jnp.mean(xf * xf, axis=-1, keepdims=True) + EPS)
    if g is not None:
        y = y * g.astype(jnp.float32)
    return y.astype(x.dtype)

def _rope(x, pos, theta, rot_dim):
    half = rot_dim // 2
    inv = theta ** (-jnp.arange(half, dtype=jnp.float32) * 2.0 / rot_dim)
    ang = pos.astype(jnp.float32)[..., None] * inv
    cos = jnp.cos(ang)[:, :, None, :]
    sin = jnp.sin(ang)[:, :, None, :]
    xr = x[..., :rot_dim].astype(jnp.float32)
    x1, x2 = xr[..., :half], xr[..., half:]
    rot = jnp.concatenate([x1 * cos - x2 * sin, x2 * cos + x1 * sin], axis=-1)
    return jnp.concatenate([rot.astype(x.dtype), x[..., rot_dim:]], axis=-1)

def _split(t, sizes):
    return jnp.split(t, np.cumsum(sizes)[:-1].tolist(), axis=-1)

def _qslice(t, i):
    return lax.dynamic_slice_in_dim(t, i * Q_BLOCK, Q_BLOCK, axis=1)

def _sweep(block_fn, S):
    out = lax.map(block_fn, jnp.arange(S // Q_BLOCK))
    nb, B, qb, H, e = out.shape
    return jnp.moveaxis(out, 0, 1).reshape(B, nb * qb, H, e)

def _chunk_mask(tq, S):
    end = (tq // CHUNK + 1) * CHUNK
    return jnp.arange(S)[None, :] < end[:, None], end

def _dsa(q, k, v, q_idx, k_idx, w_idx):
    S = q.shape[1]
    topk = min(TOPK_MAX, S // 4)
    ts = jnp.arange(S)
    idx_scale = (IDX_HEADS * IDX_DIM) ** -0.5

    def block(i):
        tq = i * Q_BLOCK + jnp.arange(Q_BLOCK)
        _, end = _chunk_mask(tq, S)
        rel = jax.nn.relu(jnp.einsum('bqhd,bsd->bqhs', _qslice(q_idx, i), k_idx).astype(jnp.float32))
        score = jnp.einsum('bqhs,bqh->bqs', rel, _qslice(w_idx, i).astype(jnp.float32)) * idx_scale
        score = jnp.where(ts[None, None, :] < end[None, :, None], score, -jnp.inf)
        _, sel = lax.top_k(score, topk)
        valid = sel < end[None, :, None]
        k_sel = jax.vmap(lambda kb, ib: kb[ib])(k, sel)
        v_sel = jax.vmap(lambda vb, ib: vb[ib])(v, sel)
        logits = jnp.einsum('bqhd,bqkd->bqhk', _qslice(q, i), k_sel).astype(jnp.float32) * HEAD_DIM ** -0.5
        logits = jnp.where(valid[:, :, None, :], logits, -jnp.inf)
        p = jax.nn.softmax(logits, axis=-1)
        return jnp.einsum('bqhk,bqkd->bqhd', p.astype(v.dtype), v_sel)

    return _sweep(block, S)

def _retention(q, k, v, g):
    B, S, H, d = q.shape
    e = v.shape[-1]
    nc = S // CHUNK
    log_gamma = jnp.log1p(-(2.0 ** (-5.0 - jnp.arange(H, dtype=jnp.float32))))
    pos_c = jnp.arange(CHUNK, dtype=jnp.float32)
    intra_decay = jnp.exp(log_gamma[:, None, None] * jnp.abs(pos_c[:, None] - pos_c[None, :]))
    k_decay = jnp.exp(log_gamma[:, None] * (CHUNK - 1 - pos_c))
    q_decay = jnp.exp(log_gamma[:, None] * (pos_c + 1.0))
    chunk_decay = jnp.exp(log_gamma * CHUNK)
    qc = q.astype(jnp.float32).reshape(B, nc, CHUNK, H, d)
    kc = k.astype(jnp.float32).reshape(B, nc, CHUNK, H, d) * d ** -0.5
    vc = v.astype(jnp.float32).reshape(B, nc, CHUNK, H, e)
    s_intra = jnp.einsum('bnihd,bnjhd->bnhij', qc, kc) * intra_decay
    y = jnp.einsum('bnhij,bnjhe->bnihe', s_intra, vc)
    kv = jnp.einsum('bnjhd,bnjhe,hj->nbhde', kc, vc, k_decay)

    def step(state, kv_n):
        return chunk_decay[None, :, None, None] * state + kv_n, state

    _, states = lax.scan(step, jnp.zeros((B, H, d, e), jnp.float32), kv)
    y = y + jnp.einsum('bnihd,nbhde,hi->bnihe', qc, states, q_decay)
    y = y.reshape(B, S, H, e)
    mu = jnp.mean(y, axis=-1, keepdims=True)
    var = jnp.mean(jnp.square(y - mu), axis=-1, keepdims=True)
    y = ((y - mu) * lax.rsqrt(var + EPS)).reshape(B, S, H * e) * g.astype(jnp.float32)
    return y.astype(v.dtype)

def _diff_attn(q1, q2, k1, k2, v, lam):
    S = q1.shape[1]
    scale = DIFF_HALF ** -0.5

    def block(i):
        tq = i * Q_BLOCK + jnp.arange(Q_BLOCK)
        mask, _ = _chunk_mask(tq, S)

        def probs(qh, kh):
            s = jnp.einsum('bqhd,bshd->bhqs', _qslice(qh, i), kh).astype(jnp.float32) * scale
            return jax.nn.softmax(jnp.where(mask, s, -jnp.inf), axis=-1)

        a = probs(q1, k1) - lam * probs(q2, k2)
        return jnp.einsum('bhqs,bshe->bqhe', a.astype(v.dtype), v)

    return _sweep(block, S)

def _stick_breaking(q, k, v):
    S = q.shape[1]
    ts = jnp.arange(S)

    def block(i):
        tq = i * Q_BLOCK + jnp.arange(Q_BLOCK)
        strict = ts[None, :] < tq[:, None]
        z = jnp.einsum('bqhd,bshd->bhqs', _qslice(q, i), k).astype(jnp.float32) * HEAD_DIM ** -0.5
        log_1m = jnp.where(strict, jax.nn.log_sigmoid(-z), 0.0)
        log_rest = lax.cumsum(log_1m, axis=3, reverse=True) - log_1m
        a = jnp.where(strict, jnp.exp(jax.nn.log_sigmoid(z) + log_rest), 0.0)
        return jnp.einsum('bhqs,bshe->bqhe', a.astype(v.dtype), v)

    return _sweep(block, S)

def setup_inputs(seed: int = 0) -> dict:
    key = jax.random.key(seed)
    ks = jax.random.split(key, 20)
    f32 = jnp.float32

    def nrm(k, shape, scale):
        return jax.random.normal(k, shape, f32) * scale

    def gain(k, shape):
        return 1.0 + 0.02 * jax.random.normal(k, shape, f32)

    x = jax.random.normal(ks[0], (BATCH, SEQ, D_MODEL), f32)
    offs = jax.random.randint(ks[1], (BATCH, 1), 0, 4096, dtype=jnp.int32)
    positions = (jnp.arange(SEQ, dtype=jnp.int32)[None, :] + offs).astype(jnp.int32)
    return {
        'x': x,
        'positions': positions,
        'norm_g': gain(ks[2], (DEPTH, D_MODEL)),
        'w_in': nrm(ks[3], (DEPTH, D_MODEL, D_IN), D_MODEL ** -0.5),
        'kv_norm_g': gain(ks[4], (DEPTH, KV_RANK)),
        'w_kv_up': nrm(ks[5], (DEPTH, KV_RANK, 2 * HEAD_DIM), KV_RANK ** -0.5),
        'q_norm_a': gain(ks[6], (DEPTH, HEAD_DIM)),
        'k_norm_a': gain(ks[7], (DEPTH, HEAD_DIM)),
        'ret_norm_g': gain(ks[8], (DEPTH, GROUP_WIDTH)),
        'q_norm_c': gain(ks[9], (DEPTH, DIFF_HALF)),
        'k_norm_c': gain(ks[10], (DEPTH, DIFF_HALF)),
        'lam_q1': nrm(ks[11], (DEPTH, DIFF_HALF), 0.1),
        'lam_k1': nrm(ks[12], (DEPTH, DIFF_HALF), 0.1),
        'lam_q2': nrm(ks[13], (DEPTH, DIFF_HALF), 0.1),
        'lam_k2': nrm(ks[14], (DEPTH, DIFF_HALF), 0.1),
        'subln_g': gain(ks[15], (DEPTH, HEAD_DIM)),
        'w_out': nrm(ks[16], (DEPTH, D_MIX, D_MODEL), D_MIX ** -0.5),
    }

def reference(x, positions, norm_g, w_in, kv_norm_g, w_kv_up, q_norm_a, k_norm_a, ret_norm_g,
              q_norm_c, k_norm_c, lam_q1, lam_k1, lam_q2, lam_k2, subln_g, w_out):
    B, S, _ = x.shape

    def heads(t, d):
        return t.reshape(B, S, -1, d)

    for l in range(DEPTH):
        h = _rms(x, norm_g[l])
        proj = jnp.einsum('bsd,df->bsf', h, w_in[l])
        (qa, ckv, qidx, kidx, widx, ga,
         qb, kb, vb, gb,
         qc, kc, vc, gc,
         qd, kd, vd, gd) = _split(proj, IN_SIZES)

        kv_a = jnp.einsum('bsr,rf->bsf', _rms(ckv, kv_norm_g[l]), w_kv_up[l])
        k_a, v_a = kv_a[..., :HEAD_DIM], kv_a[..., HEAD_DIM:]
        q_a = _rope(_rms(heads(qa, HEAD_DIM), q_norm_a[l]), positions, ROPE_THETA, HEAD_DIM // 4)
        k_a = _rope(_rms(k_a, k_norm_a[l])[:, :, None, :], positions, ROPE_THETA, HEAD_DIM // 4)[:, :, 0, :]
        q_i = _rope(heads(qidx, IDX_DIM), positions, ROPE_THETA, IDX_DIM // 4)
        k_i = _rope(_rms(kidx)[:, :, None, :], positions, ROPE_THETA, IDX_DIM // 4)[:, :, 0, :]
        y_a = _dsa(q_a, k_a, v_a, q_i, k_i, widx).reshape(B, S, GROUP_WIDTH)

        q_b = _rope(heads(qb, HEAD_DIM), positions, RET_THETA, HEAD_DIM)
        k_b = _rope(heads(kb, HEAD_DIM), positions, RET_THETA, HEAD_DIM)
        y_b = _retention(q_b, k_b, heads(vb, HEAD_DIM), ret_norm_g[l])

        qc4 = heads(qc, 2 * DIFF_HALF)
        kc4 = heads(kc, 2 * DIFF_HALF)
        prep_q = lambda t: _rope(_rms(t, q_norm_c[l]), positions, ROPE_THETA, DIFF_HALF // 4)
        prep_k = lambda t: _rope(_rms(t, k_norm_c[l]), positions, ROPE_THETA, DIFF_HALF // 4)
        q1, q2 = prep_q(qc4[..., :DIFF_HALF]), prep_q(qc4[..., DIFF_HALF:])
        k1, k2 = prep_k(kc4[..., :DIFF_HALF]), prep_k(kc4[..., DIFF_HALF:])
        lam_init = 0.8 - 0.6 * math.exp(-0.3 * l)
        lam = (jnp.exp(jnp.sum(lam_q1[l].astype(jnp.float32) * lam_k1[l].astype(jnp.float32)))
               - jnp.exp(jnp.sum(lam_q2[l].astype(jnp.float32) * lam_k2[l].astype(jnp.float32)))
               + lam_init)
        y_c = _diff_attn(q1, q2, k1, k2, heads(vc, HEAD_DIM), lam)
        y_c = (_rms(y_c, subln_g[l]) * (1.0 - lam_init)).reshape(B, S, GROUP_WIDTH)

        y_d = _stick_breaking(heads(qd, HEAD_DIM), heads(kd, HEAD_DIM), heads(vd, HEAD_DIM)).reshape(B, S, GROUP_WIDTH)

        y = jnp.concatenate([
            y_a * jax.nn.silu(ga),
            y_b * jax.nn.silu(gb),
            y_c * jax.nn.silu(gc),
            y_d * jax.nn.silu(gd),
        ], axis=-1)
        x = x + jnp.einsum('bsf,fd->bsd', y, w_out[l])
    return x


_drawn_inputs = setup_inputs


def setup_inputs(seed=0):
    import zlib

    import numpy as np

    out = dict(_drawn_inputs(seed))
    spreads = {}
    factors = {'kv_norm_g': 8.0,
     'q_norm_a': 8.0,
     'k_norm_a': 8.0,
     'ret_norm_g': 6.845,
     'q_norm_c': 8.0,
     'k_norm_c': 7.89,
     'lam_k1': 2.752,
     'lam_q2': 4.357,
     'lam_k2': 6.69,
     'subln_g': 8.0}
    for name, (base, spread) in spreads.items():
        noise = np.random.default_rng([zlib.crc32(name.encode()), seed]).standard_normal(out[name].shape)
        drawn = base * np.exp(spread * noise) if base else spread * noise
        out[name] = __import__('jax').numpy.asarray(drawn.astype(out[name].dtype))
    for name, factor in factors.items():
        out[name] = (out[name] * factor).astype(out[name].dtype)
    return out
```

```python
import math
from contextlib import ExitStack

import numpy as np
import concourse.bass as bass
from concourse import mybir

SEQ, D_MODEL, DEPTH, CHUNK, P = 512, 1024, 2, 64, 128
HEAD, HEADS, WIDTH = 64, 4, 256
KV_RANK, IDX_HEADS, DIFF_HALF, TOPK = 128, 8, 32, 128
EPS = 1e-6
TILES = SEQ // P
KT = D_MODEL // P
ROPE_THETA, RET_THETA = 500000.0, 10000.0

F_A, F_C, F_B = 8, 4, 32
ROT_A, ROT_C, ROT_B = slice(0, 8), slice(8, 12), slice(12, 44)
FREQS = F_A + F_C + F_B

GROUPS = [
    ("A0", [(0, 256), (896, 960)]),
    ("A1", [(256, 384), (960, 968)]),
    ("A2", [(384, 896)]),
    ("C0", [(2248, 2760)]),
    ("C1", [(2760, 3272)]),
    ("D0", [(3272, 3784)]),
    ("D1", [(3784, 4296)]),
    ("B0", [(1224, 1736)]),
    ("B1", [(1736, 2248)]),
    ("A3", [(968, 1224)]),
    ("O0", 512),
    ("O1", 512),
]
NAMES = [n for n, _ in GROUPS]
COLS = [c if isinstance(c, int) else sum(b - a for a, b in c) for _, c in GROUPS]
OFFSETS = [KT * sum(COLS[:g]) for g in range(len(GROUPS) + 1)]
SLOTS = 2
PER_SLOT = len(GROUPS) // SLOTS

VECS = {}
for _name, _n in (("kv_norm_g", 128), ("q_norm_a", 64), ("k_norm_a", 64), ("ret_norm_g", 256),
                  ("q_norm_c", 32), ("k_norm_c", 32), ("lam_q1", 32), ("lam_k1", 32),
                  ("lam_q2", 32), ("lam_k2", 32), ("subln_g", 64), ("lam_init", 1), ("one_minus", 1)):
    _at = max((b for _, b in VECS.values()), default=0)
    VECS[_name] = (_at, _at + _n)
N_VEC = VECS["one_minus"][1]

CONSTS = {}
for _name, _n in (("ident", P), ("decay", HEADS * P), ("tri", P), ("neg_ones", P), ("chunk_bias", SEQ),
                  ("k_decay", HEADS), ("q_decay", HEADS), ("state_decay", 2), ("freq", FREQS)):
    _at = max((b for _, b in CONSTS.values()), default=0)
    CONSTS[_name] = (_at, _at + _n)
N_CONST = CONSTS["freq"][1]

RSQ = {}
for _name, _n in (("h", 4), ("a", 24), ("k", 4), ("c", 64), ("y", 16), ("b", 16)):
    _at = max((b for _, b in RSQ.values()), default=0)
    RSQ[_name] = (_at, _at + _n)

MASKED = -1e30
INVALID = -3.0e38
TAKEN = -3.4e38
WORK_AT = {1: 0, 2: 256, 3: 640}
D_AT = {0: 0, 1: 512, 2: 896, 3: 1152}


def schedule():
    s = [("h_stats",), ("rsq", "h"), ("xn", 0), ("lam",)]
    for t in range(TILES):
        if t + 1 < TILES:
            s.append(("xn", t + 1))
        s += [("xT", t), ("proj", "A0", t)]
    s += [("proj", "A1", t) for t in range(TILES)]
    s += [("a_sq",), ("rsq", "a"), ("proj", "A2", 0), ("proj", "A2", 1), ("a_norm",), ("proj", "A2", 2),
          ("ckvT",), ("proj", "A2", 3), ("kv_up",), ("rsq", "k"), ("proj", "C0", 0), ("qi_rope",), ("k_norm",),
          ("proj", "C0", 1), ("a_rope",), ("proj", "C0", 2), ("proj", "C0", 3), ("c_sq",), ("rsq", "c")]
    s += [("proj", "C1", 0), ("AT", 0), ("AT", 1), ("c_norm",), ("proj", "C1", 1), ("AT", 2), ("AT", 3),
          ("c_rope",)]
    idx = [("idx", t, h) for t in (1, 2, 3) for h in range(IDX_HEADS)]
    top = [("top", t, r) for t in (1, 2, 3) for r in range(TOPK // 8)]
    s += idx[:4] + [("proj", "C1", 2)] + idx[4:8] + [("gate0",), ("proj", "C1", 3)]
    s += [("gate", "C")]
    s += idx[8:12] + [("CT", 0), ("CT", 1)] + idx[12:16] + [("CT", 2), ("CT", 3)] + idx[16:]
    units = [("C", t, hp) for t in range(TILES) for hp in range(2)]
    projs = ([("proj", "D0", f) for f in range(4)] + [("proj", "D1", t) for t in range(4)])
    att = []
    for i, u in enumerate(units):
        att.append([("att_s", *u)] + ([("att_pv", *units[i - 1])] if i else []))
    att.append([("att_pv", *units[-1])])
    for i, a in enumerate(att):
        s += [a[0]]
        s += [top.pop(0) for _ in range(2)]
        if i < len(projs):
            s.append(projs[i])
        s += a[1:]
    s += [("y_sq",), ("rsq", "y"), ("gate", "D")]
    projs = [("proj", g, t) for g in ("B0", "B1") for t in range(TILES)]
    dsteps = []
    for h in range(HEADS):
        dsteps += [("dz", h, 3), ("dz", h, 2), ("da", h, 3), ("dz", h, 1), ("da", h, 2), ("dz", h, 0),
                   ("da", h, 1), ("da", h, 0), ("dpv", h)]
    late = [[], [("c_post",)], [], [], [("b_rope",)], [("BT", 0), ("BT", 1)], [("BT", 2), ("BT", 3)], []]
    n = len(dsteps)
    for i in range(8):
        s.append(projs[i])
        s += late[i]
        for st in dsteps[i * n // 8:(i + 1) * n // 8]:
            s.append(st)
            if top:
                s.append(top.pop(0))
    s += top
    s += [("gate", "B"), ("proj", "A3", 0), ("proj", "A3", 1), ("bkv", 0), ("bs", 0), ("bs", 1), ("bkv", 1),
          ("by", 0), ("proj", "A3", 2), ("bkv", 2), ("bs", 2), ("by", 1), ("proj", "A3", 3), ("bs", 3), ("by", 2),
          ("by", 3), ("gate", "A"), ("b_sq",), ("rsq", "b")]
    a_units = [("A", t, 0) for t in range(TILES)]
    s += [("att_s", *a_units[0]), ("att_s", *a_units[1]), ("b_post",), ("att_pv", *a_units[0]),
          ("att_s", *a_units[2]), ("att_pv", *a_units[1]), ("att_s", *a_units[3]), ("att_pv", *a_units[2]),
          ("yT", 0), ("att_pv", *a_units[3]), ("yT", 1)]
    s += [("proj", "O0", 0), ("yT", 2), ("proj", "O0", 1), ("yT", 3), ("proj", "O0", 2), ("proj", "O0", 3)]
    s += [("proj", "O1", t) for t in range(TILES)]
    return [x for x in s if x[0] != "gate0"]


SCHEDULE = schedule()

RINGS = {"proj": (0, 1), "turn": (2, 3), "score": (4, 5), "hold": (6, 7)}


def fills_of(step):
    k = step[0]
    if k == "proj":
        return [("proj", step)]
    if k in ("xT", "AT", "yT"):
        return [("turn", (*step, j)) for j in range(2)]
    if k in ("CT", "BT", "ckvT", "kv_up", "dpv"):
        return [("turn", step)]
    if k == "idx":
        return [("score", step)]
    if k == "bs":
        return [("score", (*step, par)) for par in range(2)]
    if k == "att_s":
        return [("score", (*step, m)) for m in range(4)]
    if k == "att_pv":
        return [("hold", step)] + [("turn", (*step, m)) for m in (range(4) if step[1] == "A" else (0, 2))]
    if k in ("bkv", "by", "dz"):
        return [("hold", step)]
    return []


def turns():
    used = {b: 0 for ring in RINGS.values() for b in ring}
    told = dict(used)
    at = {r: 0 for r in RINGS}
    out = {}
    for step in SCHEDULE:
        for ring, key in fills_of(step):
            b = RINGS[ring][at[ring] % len(RINGS[ring])]
            told[b] += key[0] != "att_pv" or key != step
            out[key] = (b, used[b], told[b])
            at[ring] += 1
            used[b] += 1
    return out


TURN = turns()
UNITS = [s[1:] for s in SCHEDULE if s[0] == "att_pv"]
PT_AT = {}
for _u in UNITS:
    for _m in (range(4) if _u[0] == "A" else (0, 2)):
        PT_AT[(_u, _m)] = len(PT_AT)
GATES = [s[1] for s in SCHEDULE if s[0] == "gate"]
IDX = [s for s in SCHEDULE if s[0] == "idx"]
DZ = {s[1:]: n for n, s in enumerate([s for s in SCHEDULE if s[0] == "dz"])}
DA = {s[1:]: n for n, s in enumerate([s for s in SCHEDULE if s[0] == "da"])}
RSQ_AT = {s[1]: n for n, s in enumerate([s for s in SCHEDULE if s[0] == "rsq"])}
Y_AT = {"A": 0, "B": 256, "C": 512, "D": 768}
V_AT = {"C": 0, "D": 1, "B": 2}


def encoder(nc, x, pos, w, norm_g, vecs, w_kv, consts, out):
    f32, i32 = mybir.dt.float32, mybir.dt.int32
    ACT, ALU, AX = mybir.ActivationFunctionType, mybir.AluOpType, mybir.AxisListType.X
    ctx = ExitStack()
    with ctx:
        def sb(name, *shape, dt=f32):
            return ctx.enter_context(nc.sbuf_tensor(name, [P, *shape], dt))

        def sem(name):
            return ctx.enter_context(nc.semaphore(name))

        X = sb("X", TILES, D_MODEL)
        hT = sb("hT", KT, SEQ)
        W = [sb(f"W{i}", KT * 512) for i in range(SLOTS)]
        AH = sb("AH", TILES, 15, HEAD)
        CW = sb("CW", TILES, KV_RANK + IDX_HEADS)
        CKT = sb("CKT", TILES, P)
        VA = sb("VA", TILES, HEAD)
        AT = sb("AT", 8, SEQ)
        QK = sb("QK", TILES, 512)
        QKT = sb("QKT", 4, SEQ)
        V = sb("V", 3, TILES, WIDTH)
        G = sb("G", TILES, D_MODEL)
        L = sb("L", 2, 4, SEQ)
        PT = sb("PT", 2, TILES, P)
        DL = sb("DL", 2, 1280)
        WORK = sb("WORK", 1152)
        T = sb("T", 2, SEQ)
        GE = sb("GE", TILES, WIDTH)
        SQY = sb("SQY", TILES, WIDTH)
        C = sb("C", N_CONST)
        VEC = sb("VEC", N_VEC)
        NG = sb("NG", KT)
        WKV = sb("WKV", 2 * HEAD)
        COS = sb("COS", TILES, FREQS)
        SIN = sb("SIN", TILES, FREQS)
        SS = sb("SS", 128)
        VAR = sb("VAR", 128)
        RS = sb("RS", 128)
        NEWT = sb("NEWT", 128)
        M8 = sb("M8", 8)
        MX = sb("MX", 2, 4)
        NM = sb("NM", 2, 4)
        SUM = sb("SUM", 2, 4)
        RINV = sb("RINV", 2, 4)
        RHO = sb("RHO", 2, 2)
        LAM = sb("LAM", 8)
        SG = sb("SG", HEAD)
        MU = sb("MU", 16)
        YT = sb("YT", WIDTH)
        STATE = sb("STATE", 3, 2, 2 * HEAD)
        DT = AT[:, 4:8, :]
        DAT = AH[:, :, :, :].rearrange("p t h d -> p (t h d)")[:, 0:2560].rearrange("p (b n) -> p b n", b=2)
        YC = AH[:, :, :, :].rearrange("p t h d -> p (t h d)")[:, 2560:3584].rearrange("p (t n) -> p t n", t=TILES)
        XN = L[:, :, :, :].rearrange("p a b n -> p (a b n)")[:, 0:2048].rearrange("p (a n) -> p a n", a=2)
        SQ = L[:, :, :, :].rearrange("p a b n -> p (a b n)")[:, 2048:4096]
        R = DL[:, :, 0:SEQ]
        SD = DL[:, :, 0:SEQ].rearrange("p b (h q) -> p b h q", h=HEADS)
        KS = T[:, :, :].rearrange("p a n -> p (a n)").rearrange("p (t h d) -> p t h d", t=TILES, h=HEADS)
        YB = QK[:, :, :].rearrange("p t n -> p (t n)")[:, 0:1024].rearrange("p (t n) -> p t n", t=TILES)
        early = SQY[:, :, :].rearrange("p t n -> p (t n)")
        ANG, TURNS_ = (early[:, a:a + TILES * FREQS].rearrange("p (t f) -> p t f", t=TILES) for a in (0, 256))
        POS = early[:, 512:516]
        POS_I = early[:, 516:520].bitcast(i32)
        PS = [ctx.enter_context(nc.psum_tensor(f"PS{b}", [P, 512], f32)) for b in range(8)]

        def const(name):
            a, b = CONSTS[name]
            return C[:, a:b]

        def vec(name):
            a, b = VECS[name]
            return VEC[:, a:b]

        IDENT = const("ident")

        x_in = [sem(f"x_in{t}") for t in range(TILES)]
        const_in = sem("const_in")
        setup_dve = sem("setup_dve")
        setup_act = sem("setup_act")
        tables_ready = sem("tables_ready")
        states_zeroed = sem("states_zeroed")
        weights_in = [sem(f"weights_in{i}") for i in range(SLOTS)]
        slot_free = [sem(f"slot_free{i}") for i in range(SLOTS)]
        layer_done = sem("layer_done")
        layer_cleared = sem("layer_cleared")
        layer_over = sem("layer_over")
        stored = sem("stored")
        bank_filled = [sem(f"bank_filled{b}") for b in range(8)]
        bank_drained = [sem(f"bank_drained{b}") for b in range(8)]
        vecs_in = sem("vecs_in")
        dve_step = sem("dve_step")
        act_step = sem("act_step")
        pool_step = sem("pool_step")
        squares = sem("squares")
        var_ready = sem("var_ready")
        rsq_guess = sem("rsq_guess")
        xn_ready = sem("xn_ready")
        lam_sums = sem("lam_sums")
        lam_exps = sem("lam_exps")
        cn_ready = sem("cn_ready")
        a_normed = sem("a_normed")
        a_roped = sem("a_roped")
        c_normed = sem("c_normed")
        c_roped = sem("c_roped")
        b_roped = sem("b_roped")
        ks_ready = sem("ks_ready")
        idx_added = sem("idx_added")
        max_ready = sem("max_ready")
        probs_ready = sem("probs_ready")
        combined = sem("combined")
        pt_used = sem("pt_used")
        gate_exp = sem("gate_exp")
        gate_rcp = sem("gate_rcp")
        gate_ready = sem("gate_ready")
        softplus_log = sem("softplus_log")
        softplus_ready = sem("softplus_ready")
        softplus_masked = sem("softplus_masked")
        d_args = sem("d_args")
        d_masked = sem("d_masked")
        centred = sem("centred")
        y_normed = sem("y_normed")
        ya_ready = sem("ya_ready")
        y_ready = sem("y_ready")
        in_layer = range(bank_filled[0].num, y_ready.num + 1)

        def tok(t, n=1):
            return slice(t * P, (t + n) * P)

        def wait_filled(e, key):
            b, _, f = TURN[key]
            e.wait_ge(bank_filled[b], f)
            return PS[b]

        def wait_copied(e, key):
            b, n, _ = TURN[key]
            e.wait_ge(bank_drained[b], n + 1)

        def drains(ins, key):
            ins.then_inc(bank_drained[TURN[key][0]], 1)

        def wait_projected(e, name):
            for t in range(TILES) if name != "D0" else range(4):
                wait_copied(e, ("proj", name, t))

        def chain(e, s):
            count = [0]

            def note(ins):
                count[0] += 1
                ins.then_inc(s, 1)

            def settle():
                if count[0]:
                    e.wait_ge(s, count[0])

            def link(ins):
                note(ins)
                settle()
            return link, note, settle

        def head_view(a, b):
            return AH[:, :, a:b, :]

        def map_operands(kind, t, hp, m):
            n = (t + 1) * P
            if kind == "C":
                rows = slice(32 * m, 32 * m + 32)
                return QKT[rows, hp, tok(t)], QKT[rows, 2 + hp, 0:n], n
            base = 64 * (m % 2)
            rows = slice(base, base + 64)
            return AT[rows, m // 2, tok(t)], AT[rows, 3 if base == 0 else 2, 0:n], n

        def maps_of(kind):
            return range(4) if kind == "A" else (0, 2)

        def probs_counts(u):
            return 4 * (ATT_S.index(u) + 1)

        ATT_S = [s[1:] for s in SCHEDULE if s[0] == "att_s"]
        SETUP = 11

        block = ctx.enter_context(nc.Block())

        @block.sync
        def _(sp):
            sp.dma_start(C[:, :], consts).then_inc(const_in, 16)
            sp.dma_start(POS_I[:, :], pos).then_inc(const_in, 16)
            for t in range(TILES):
                sp.dma_start(X[:, t, :], x[tok(t), :]).then_inc(x_in[t], 16)
            for i in range(SLOTS):
                sp.sem_inc(slot_free[i], 1)
            with sp.Fori(0, DEPTH) as l:
                for g in range(len(GROUPS)):
                    i, n = g % SLOTS, g // SLOTS
                    sp.wait_ge(slot_free[i], l * PER_SLOT + (n + 1))
                    sp.dma_start(W[i][:, 0:KT * COLS[g]], w[l][:, OFFSETS[g]:OFFSETS[g + 1]]) \
                        .then_inc(weights_in[i], 16)
            sp.wait_ge(layer_done, 4 * DEPTH)
            for t in range(TILES):
                sp.dma_start(out[tok(t), :], X[:, t, :]).then_inc(stored, 16)
            sp.wait_ge(stored, 16 * TILES)

        @block.tensor
        def _(pe):
            def bank(key):
                b, n, _ = TURN[key]
                if n:
                    pe.wait_ge(bank_drained[b], n)
                return PS[b]

            def filled(ins, key):
                ins.then_inc(bank_filled[TURN[key][0]], 1)

            pe.wait_ge(const_in, 32)
            with pe.Fori(0, DEPTH) as l:
                for step in SCHEDULE:
                    kind = step[0]
                    if kind == "xT":
                        t = step[1]
                        pe.wait_ge(xn_ready, t + 1)
                        for j in range(2):
                            ps = bank((*step, j))
                            for i in range(4):
                                ins = pe.transpose(ps[:, tok(i)], XN[:, t % 2, 4 * j + i::KT], IDENT)
                            filled(ins, (*step, j))
                    elif kind == "proj":
                        _, name, t = step
                        g = NAMES.index(name)
                        if t == 0:
                            pe.wait_ge(weights_in[g % SLOTS], (l * PER_SLOT + (g // SLOTS + 1)) * 16)
                        if name[0] == "O":
                            wait_copied(pe, ("yT", t, 0))
                            wait_copied(pe, ("yT", t, 1))
                        elif name == "A0":
                            wait_copied(pe, ("xT", t, 0))
                            wait_copied(pe, ("xT", t, 1))
                        ps = bank(step)
                        n = COLS[g]
                        wg = W[g % SLOTS][:, 0:KT * n].rearrange("p (k n) -> p k n", k=KT)
                        for k in range(KT):
                            if name == "D0":
                                ins = pe.matmul(ps[:, :], wg[:, k, tok(t)], hT[:, k, :], start=k == 0, stop=k == KT - 1)
                            else:
                                ins = pe.matmul(ps[:, 0:n], hT[:, k, tok(t)], wg[:, k, :], start=k == 0,
                                                stop=k == KT - 1)
                        filled(ins, step)
                    elif kind == "ckvT":
                        pe.wait_ge(cn_ready, 1)
                        ps = bank(step)
                        for t in range(TILES):
                            ins = pe.transpose(ps[:, tok(t)], CW[:, t, 0:KV_RANK], IDENT)
                        filled(ins, step)
                    elif kind == "kv_up":
                        wait_copied(pe, ("ckvT",))
                        pe.wait_ge(vecs_in, 48)
                        ps = bank(step)
                        for t in range(TILES):
                            ins = pe.matmul(ps[:, tok(t)], CKT[:, t, :], WKV[:, :], start=True, stop=True)
                        filled(ins, step)
                    elif kind == "AT":
                        t = step[1]
                        pe.wait_ge(a_roped, 3)
                        for j in range(2):
                            ps = bank((*step, j))
                            for i, h in enumerate(((0, 2, 4, 5), (7, 9, 11, 13))[j]):
                                ins = pe.transpose(ps[:, tok(i)],
                                                   AH[:, t, h:h + 2, :].rearrange("p h d -> p (h d)"), IDENT)
                            filled(ins, (*step, j))
                    elif kind in ("CT", "BT"):
                        t = step[1]
                        pe.wait_ge(*((c_roped, 1) if kind == "CT" else (b_roped, 2)))
                        ps = bank(step)
                        for i in range(4):
                            ins = pe.transpose(ps[:, tok(i)], QK[:, t, tok(i)], IDENT)
                        filled(ins, step)
                    elif kind == "idx":
                        _, t, h = step
                        if h == 0:
                            for u in range(t + 1):
                                wait_copied(pe, ("AT", u, 0))
                                wait_copied(pe, ("AT", u, 1))
                        ps = bank(step)
                        rows = slice(64 * (h % 2), 64 * (h % 2) + 64)
                        filled(pe.matmul(ps[:, 0:(t + 1) * P], AT[rows, 4 + h // 2, tok(t)],
                                         AT[rows, 3 if h % 2 else 2, 0:(t + 1) * P], start=True, stop=True), step)
                    elif kind == "att_s":
                        _, g, t, hp = step
                        if g == "C":
                            wait_copied(pe, ("CT", t))
                        for m in range(4):
                            q, k, n = map_operands(g, t, hp, m)
                            ps = bank((*step, m))
                            filled(pe.matmul(ps[:, 0:n], q, k, start=True, stop=True), (*step, m))
                    elif kind == "att_pv":
                        u = step[1:]
                        g, t, hp = u
                        maps = list(maps_of(g))
                        lb = ATT_S.index(u) % 2

                        def turn_over(m):
                            ps = bank((*step, m))
                            for j in range(t + 1):
                                ins = pe.transpose(ps[:, tok(j)], L[:, lb, m, tok(j)], IDENT)
                            filled(ins, (*step, m))

                        def times_v(i):
                            pt = PT_AT[(u, maps[i])]
                            wait_copied(pe, (*step, maps[i]))
                            for j in range(t + 1):
                                v = VA[:, j, :] if g == "A" else V[:, V_AT["C"], j, (2 * hp + i) * 64:(2 * hp + i + 1) * 64]
                                ins = pe.matmul(po[:, 64 * i:64 * i + 64], PT[:, pt % 2, j, :], v,
                                                start=j == 0, stop=j == t)
                            ins.then_inc(pt_used, 1)

                        if g == "A":
                            pe.wait_ge(probs_ready, probs_counts(u))
                        else:
                            pe.wait_ge(combined, 2 * (1 + [v for v in UNITS if v[0] == "C"].index(u)))
                            wait_projected(pe, "C1")
                        po = bank(step)
                        turn_over(maps[0])
                        for i in range(len(maps)):
                            if i + 1 < len(maps):
                                turn_over(maps[i + 1])
                            times_v(i)
                    elif kind == "dz":
                        _, h, j = step
                        if h == 0 and j == 3:
                            wait_projected(pe, "D0")
                        rows = slice(64 * (h % 2), 64 * (h % 2) + 64)
                        ps = bank(step)
                        filled(pe.matmul(ps[:, 0:(4 - j) * P], DT[rows, 2 + h // 2, tok(j)],
                                         DT[rows, h // 2, j * P:SEQ], start=True, stop=True), step)
                    elif kind == "da":
                        _, h, j = step
                        ps = PS[TURN[("dz", h, j)][0]]
                        pe.wait_ge(softplus_masked, DZ[(h, j)] + 1)
                        n = (4 - j) * P
                        ins = pe.matmul(ps[:, 0:n], const("tri"), DL[:, h % 2, D_AT[j]:D_AT[j] + n],
                                        start=False, stop=True, skip_group_check=True)
                        for i in range(j + 1, TILES):
                            n = (4 - i) * P
                            ins = pe.matmul(ps[:, (i - j) * P:(i - j) * P + n], const("neg_ones"),
                                            DL[:, h % 2, D_AT[i]:D_AT[i] + n], start=False, stop=True,
                                            skip_group_check=True)
                        ins.then_inc(d_args, 1)
                    elif kind == "dpv":
                        h = step[1]
                        pe.wait_ge(d_masked, 4 * (h + 1))
                        if h == 0:
                            wait_projected(pe, "D1")
                        ps = bank(step)
                        for i in range(TILES):
                            for j in range(i + 1):
                                a = D_AT[j] + (i - j) * P
                                ins = pe.matmul(ps[:, 64 * i:64 * i + 64], DAT[:, h % 2, a:a + P],
                                                V[:, V_AT["D"], j, 64 * h:64 * h + 64], start=j == 0, stop=j == i)
                        filled(ins, step)
                    elif kind == "bs":
                        t = step[1]
                        wait_copied(pe, ("BT", t))
                        for par in range(2):
                            ps = bank((*step, par))
                            rows = slice(64 * par, 64 * par + 64)
                            for pair in range(2):
                                ins = pe.matmul(ps[:, tok(pair)], QKT[rows, 2 + pair, tok(t)], QKT[rows, pair, tok(t)],
                                                start=True, stop=True)
                            filled(ins, (*step, par))
                    elif kind == "bkv":
                        t = step[1]
                        pe.wait_ge(ks_ready, 1)
                        if t == 0:
                            wait_projected(pe, "B1")
                        ps = bank(step)
                        for h in range(HEADS):
                            r = 64 * (h % 2)
                            ins = pe.matmul(ps[r:r + 64, 64 * h:64 * h + 64], KS[:, t, h, :],
                                            V[:, V_AT["B"], t, 64 * h:64 * h + 64], start=True, stop=True)
                        filled(ins, step)
                    elif kind == "by":
                        t = step[1]
                        wait_copied(pe, ("bs", t, 0))
                        wait_copied(pe, ("bs", t, 1))
                        if t:
                            wait_copied(pe, ("bkv", t - 1))
                        ps = bank(step)
                        for pair in range(2):
                            if t:
                                pe.matmul(ps[:, tok(pair)], QKT[:, pair, tok(t)], STATE[:, t - 1, pair, :],
                                          start=True, stop=True)
                            for h in (2 * pair, 2 * pair + 1):
                                ins = pe.matmul(ps[:, 64 * h:64 * h + 64], SD[:, t % 2, h, :],
                                                V[:, V_AT["B"], t, 64 * h:64 * h + 64], start=t == 0, stop=True,
                                                skip_group_check=t > 0)
                        filled(ins, step)
                    elif kind == "yT":
                        t = step[1]
                        pe.wait_ge(y_ready, 2)
                        for h in range(HEADS):
                            wait_copied(pe, ("dpv", h))
                        pe.wait_ge(ya_ready, t + 1)
                        for j in range(2):
                            ps = bank((*step, j))
                            for i in range(4):
                                ins = pe.transpose(ps[:, tok(i)], G[:, t, 4 * j + i::KT], IDENT)
                            filled(ins, (*step, j))
                pe.drain().then_inc(layer_done, 1)
                pe.wait_ge(layer_cleared, l + 1)

        @block.scalar
        def _(act):
            act.wait_ge(setup_dve, SETUP)
            nc.scalar.activation(SIN[:, :, :], ANG[:, :, :], ACT.Sin).then_inc(tables_ready, 1)
            nc.scalar.activation(COS[:, :, :], TURNS_[:, :, :], ACT.Sin).then_inc(tables_ready, 1)
            with act.Fori(0, DEPTH) as l:
                link, note, settle = chain(act, act_step)
                act.dma_start(NG[:, :], norm_g[l].rearrange("(p k) -> p k", k=KT)).then_inc(vecs_in, 16)
                act.dma_start(VEC[:, :], vecs[l].partition_broadcast(P)).then_inc(vecs_in, 16)
                act.dma_start(WKV[:, :], w_kv[l]).then_inc(vecs_in, 16)

                def copy_out(key, dst, src, scale=1.0):
                    drains(nc.scalar.activation(dst, src, ACT.Copy, scale=scale), key)

                for step in SCHEDULE:
                    kind = step[0]
                    if kind == "h_stats":
                        for t in range(2):
                            act.wait_ge(x_in[t], 16)
                            nc.scalar.activation(G[:, t, :], X[:, t, :], ACT.Square, accum_out=SS[:, t:t + 1]) \
                                .then_inc(squares, 1)
                    elif kind == "rsq":
                        a, b = RSQ[step[1]]
                        act.wait_ge(var_ready, RSQ_AT[step[1]] + 1)
                        link(nc.scalar.activation(RS[:, a:b], VAR[:, a:b], ACT.Ln))
                        nc.scalar.activation(RS[:, a:b], RS[:, a:b], ACT.Exp, scale=-0.5).then_inc(rsq_guess, 1)
                    elif kind == "lam":
                        act.wait_ge(lam_sums, 2)
                        nc.scalar.activation(LAM[:, 2:4], LAM[:, 0:2], ACT.Exp).then_inc(lam_exps, 1)
                    elif kind == "proj" and step[1][0] != "O":
                        _, name, t = step
                        g = NAMES.index(name)
                        if name == "D0" and t == 0:
                            wait_copied(act, IDX[-1])
                        if name == "B0" and t == 0:
                            wait_filled(act, ("CT", TILES - 1))
                        ps = wait_filled(act, step)
                        if t == 3:
                            act.sem_inc(slot_free[g % SLOTS], 1)
                        if name == "A0":
                            copy_out(step, AH[:, t, 0:5, :].rearrange("p h d -> p (h d)"), ps[:, 0:320])
                        elif name == "A1":
                            copy_out(step, CW[:, t, :], ps[:, 0:136])
                        elif name == "A2":
                            copy_out(step, AH[:, t, 7:15, :].rearrange("p h d -> p (h d)"), ps[:, :])
                        elif name in ("C0", "B0"):
                            copy_out(step, QK[:, t, :], ps[:, :])
                        elif name == "D0":
                            copy_out(step, DT[:, t, :], ps[:, :], HEAD ** -0.5 if t < 2 else 1.0)
                        elif name == "A3":
                            copy_out(step, G[:, t, 0:256], ps[:, 0:256])
                        else:
                            note(nc.scalar.activation(V[:, V_AT[name[0]], t, :], ps[:, 0:256], ACT.Copy))
                            y = Y_AT[name[0]]
                            copy_out(step, G[:, t, y:y + 256], ps[:, 256:512])
                    elif kind == "proj" and step[2] == 3:
                        g = NAMES.index(step[1])
                        wait_filled(act, step)
                        act.sem_inc(slot_free[g % SLOTS], 1)
                    elif kind == "a_sq":
                        wait_projected(act, "A0")
                        wait_projected(act, "A1")
                        note(nc.scalar.activation(SQ[:, 0:1280].rearrange("p (t h d) -> p t h d", t=TILES, h=5),
                                                  head_view(0, 5), ACT.Square))
                        nc.scalar.activation(SQ[:, 1280:1792].rearrange("p (t n) -> p t n", t=TILES),
                                             CW[:, :, 0:KV_RANK], ACT.Square).then_inc(squares, 1)
                    elif kind == "ckvT":
                        ps = wait_filled(act, step)
                        copy_out(step, CKT[:, :, :], ps[:, :].rearrange("p (t n) -> p t n", t=TILES))
                    elif kind == "kv_up":
                        ps = wait_filled(act, step)
                        kv = ps[:, :].rearrange("p (t n) -> p t n", t=TILES)
                        note(nc.scalar.activation(VA[:, :, :], kv[:, :, 64:128], ACT.Copy))
                        copy_out(step, AH[:, :, 5, :], kv[:, :, 0:64])
                        wait_copied(act, step)
                        act.wait_ge(var_ready, RSQ_AT["a"] + 1)
                        nc.scalar.activation(SQ[:, 0:256].rearrange("p (t n) -> p t n", t=TILES), AH[:, :, 5, :],
                                             ACT.Square).then_inc(squares, 1)
                    elif kind == "AT":
                        ps = wait_filled(act, (*step, 0))
                        copy_out((*step, 0), AT[:, 0:4, tok(step[1])], ps[:, :].rearrange("p (s n) -> p s n", s=4))
                    elif kind in ("CT", "BT"):
                        if kind == "BT" and step[1] == 0:
                            wait_filled(act, ("att_s", "C", TILES - 1, 1, 3))
                            wait_filled(act, ("att_s", "C", TILES - 1, 1, 2))
                        ps = wait_filled(act, step)
                        copy_out(step, QKT[:, :, tok(step[1])], ps[:, :].rearrange("p (s n) -> p s n", s=4))
                    elif kind == "idx":
                        i = IDX.index(step)
                        ps = wait_filled(act, step)
                        if i >= 2:
                            act.wait_ge(idx_added, i - 1)
                        n = (step[1] + 1) * P
                        drains(nc.scalar.activation(R[:, i % 2, 0:n], ps[:, 0:n], ACT.Relu), step)
                    elif kind == "c_sq":
                        wait_projected(act, "C0")
                        act.wait_ge(var_ready, RSQ_AT["k"] + 1)
                        nc.scalar.activation(SQ[:, :], QK[:, :, :].rearrange("p t n -> p (t n)"), ACT.Square) \
                            .then_inc(squares, 1)
                    elif kind == "att_s":
                        u = step[1:]
                        g, t, hp = u
                        i = ATT_S.index(u)
                        n = (t + 1) * P
                        scale = (HEAD if g == "A" else DIFF_HALF) ** -0.5
                        act.wait_ge(max_ready, i + 1)
                        for m in range(4):
                            nc.scalar.activation(L[:, i % 2, m, 0:n], L[:, i % 2, m, 0:n], ACT.Exp,
                                                 bias=NM[:, i % 2, m:m + 1], scale=scale,
                                                 accum_out=SUM[:, i % 2, m:m + 1]).then_inc(probs_ready, 1)
                    elif kind == "att_pv":
                        u = step[1:]
                        n = (u[1] + 1) * P
                        for m in maps_of(u[0]):
                            pt = PT_AT[(u, m)]
                            ps = wait_filled(act, (*step, m))
                            if pt >= 2:
                                act.wait_ge(pt_used, pt - 1)
                            copy_out((*step, m), PT[:, pt % 2, :, :].rearrange("p j n -> p (j n)")[:, 0:n],
                                     ps[:, 0:n])
                    elif kind == "gate":
                        y = Y_AT[step[1]]
                        i = GATES.index(step[1])
                        wait_projected(act, {"A": "A3", "B": "B1", "C": "C1", "D": "D1"}[step[1]])
                        if i:
                            act.wait_ge(gate_ready, i)
                        nc.scalar.activation(GE[:, :, :], G[:, :, y:y + 256], ACT.Exp, scale=-1.0) \
                            .then_inc(gate_exp, 1)
                    elif kind == "y_sq":
                        for u in [u for u in UNITS if u[0] == "C"]:
                            wait_copied(act, ("att_pv", *u))
                        nc.scalar.activation(SQY[:, :, :], YC[:, :, :], ACT.Square).then_inc(squares, 1)
                    elif kind == "b_sq":
                        act.wait_ge(centred, 1)
                        nc.scalar.activation(SQY[:, :, :], YB[:, :, :], ACT.Square).then_inc(squares, 1)
                    elif kind == "dz":
                        _, h, j = step
                        a = DAT[:, h % 2, D_AT[j]:D_AT[j] + (4 - j) * P]
                        ps = wait_filled(act, step)
                        if h == 0 and j == 3:
                            wait_filled(act, ("AT", TILES - 1, 1))
                        if h >= 2 and j == 3:
                            wait_filled(act, ('dpv', h - 2))
                        link(nc.scalar.activation(a, ps[:, 0:(4 - j) * P], ACT.Abs))
                        link(nc.scalar.activation(a, a, ACT.Exp, scale=-1.0))
                        nc.scalar.activation(a, a, ACT.Ln, bias=1.0).then_inc(softplus_log, 1)
                    elif kind == "da":
                        _, h, j = step
                        act.wait_ge(d_args, DA[(h, j)] + 1)
                        act.wait_ge(softplus_ready, DZ[(h, j)] + 1)
                        drains(nc.scalar.activation(DAT[:, h % 2, D_AT[j]:D_AT[j] + (4 - j) * P],
                                                    PS[TURN[("dz", h, j)][0]][:, 0:(4 - j) * P], ACT.Exp),
                               ("dz", h, j))
                    elif kind == "yT":
                        t = step[1]
                        ps = wait_filled(act, (*step, 0))
                        copy_out((*step, 0), hT[:, 0:4, tok(t)], ps[:, :].rearrange("p (s n) -> p s n", s=4))
                act.drain().then_inc(layer_done, 1)
                act.wait_ge(layer_cleared, l + 1)

        @block.vector
        def _(dve):
            v = nc.vector
            link, note, settle = chain(dve, setup_dve)
            two_pi = 2.0 * math.pi
            c1 = 6.28125
            c2 = float(np.float32(round((two_pi - c1) * 2 ** 20) / 2 ** 20))
            c3 = two_pi - c1 - c2
            pi = 3.1415925
            magic = 1.5 * 2 ** 23
            dve.wait_ge(const_in, 32)
            link(v.tensor_copy(POS[:, :], POS_I[:, :]))
            link(v.tensor_tensor(ANG[:, :, :], POS[:, :].unsqueeze(2).broadcast_to([P, TILES, FREQS]),
                                 const("freq").unsqueeze(1).broadcast_to([P, TILES, FREQS]), ALU.mult))
            link(v.tensor_scalar(TURNS_[:, :, :], ANG[:, :, :], 1.0 / two_pi, magic, ALU.mult, ALU.add))
            link(v.tensor_scalar(TURNS_[:, :, :], TURNS_[:, :, :], magic, None, ALU.subtract))
            for c in (c1, c2, c3):
                link(v.scalar_tensor_tensor(ANG[:, :, :], TURNS_[:, :, :], -c, ANG[:, :, :], ALU.mult, ALU.add))
            link(v.tensor_scalar(COS[:, :, :], ANG[:, :, :], pi / 2, -two_pi, ALU.is_gt, ALU.mult))
            link(v.scalar_tensor_tensor(TURNS_[:, :, :], ANG[:, :, :], math.pi / 2, COS[:, :, :], ALU.add, ALU.add))
            link(v.tensor_scalar(TURNS_[:, :, :], TURNS_[:, :, :], pi, -pi, ALU.min, ALU.max))
            note(v.tensor_scalar(ANG[:, :, :], ANG[:, :, :], pi, -pi, ALU.min, ALU.max))

            with dve.Fori(0, DEPTH) as l:
                link, note, settle = chain(dve, dve_step)

                def reduce_groups(use, src, lo, hi, n):
                    a = RSQ[use][0]
                    link(v.tensor_reduce(SS[:, a + lo:a + hi], src, op=ALU.add, axis=AX))
                    return v.tensor_scalar(VAR[:, a + lo:a + hi], SS[:, a + lo:a + hi], 1.0 / n, EPS, ALU.mult, ALU.add)

                def newton(use):
                    a, b = RSQ[use]
                    dve.wait_ge(rsq_guess, RSQ_AT[use] + 1)
                    link(v.tensor_tensor(NEWT[:, a:b], RS[:, a:b], RS[:, a:b], ALU.mult))
                    link(v.tensor_tensor(NEWT[:, a:b], NEWT[:, a:b], VAR[:, a:b], ALU.mult))
                    link(v.tensor_scalar(NEWT[:, a:b], NEWT[:, a:b], -0.5, 1.5, ALU.mult, ALU.add))
                    link(v.tensor_tensor(RS[:, a:b], RS[:, a:b], NEWT[:, a:b], ALU.mult))

                def rs(use, lo=0, hi=None):
                    a, b = RSQ[use]
                    return RS[:, a + lo:(b if hi is None else a + hi)]

                for step in SCHEDULE:
                    kind = step[0]
                    if kind == "h_stats":
                        for t in range(2, TILES):
                            dve.wait_ge(x_in[t], 16)
                            link(v.tensor_tensor_reduce(out=G[:, t, :], in0=X[:, t, :], in1=X[:, t, :], scale=1.0,
                                                        scalar=0.0, op0=ALU.mult, op1=ALU.add,
                                                        accum_out=SS[:, t:t + 1]))
                        dve.wait_ge(squares, 2)
                        v.tensor_scalar(VAR[:, 0:4], SS[:, 0:4], 1.0 / D_MODEL, EPS, ALU.mult, ALU.add) \
                            .then_inc(var_ready, 1)
                    elif kind == "xn":
                        t = step[1]
                        if t == 0:
                            newton("h")
                        if t >= 2:
                            wait_filled(dve, ("xT", t - 2, 1))
                        v.tensor_scalar(XN[:, t % 2, :], X[:, t, :], RS[:, t:t + 1], None, ALU.mult) \
                            .then_inc(xn_ready, 1)
                    elif kind == "lam":
                        dve.wait_ge(vecs_in, 48)
                        for i in range(2):
                            v.tensor_tensor_reduce(out=YT[:, 32 * i:32 * i + 32], in0=vec(f"lam_q{i + 1}"),
                                                   in1=vec(f"lam_k{i + 1}"), scale=1.0, scalar=0.0, op0=ALU.mult,
                                                   op1=ALU.add, accum_out=LAM[:, i:i + 1]).then_inc(lam_sums, 1)
                        note(v.tensor_scalar(SG[:, :], vec("subln_g"), vec("one_minus"), None, ALU.mult))
                    elif kind == "xT":
                        t = step[1]
                        dve.wait_ge(vecs_in, 48)
                        for j in range(2):
                            ps = wait_filled(dve, (*step, j))
                            drains(v.tensor_tensor(hT[:, 4 * j:4 * j + 4, tok(t)],
                                                   ps[:, :].rearrange("p (s n) -> p s n", s=4),
                                                   NG[:, 4 * j:4 * j + 4].unsqueeze(2).broadcast_to([P, 4, P]),
                                                   ALU.mult), (*step, j))
                    elif kind == "a_sq":
                        dve.wait_ge(squares, 3)
                        note(reduce_groups("a", SQ[:, 0:1280].rearrange("p (g d) -> p g d", d=HEAD), 0, 20, HEAD))
                        reduce_groups("a", SQ[:, 1280:1792].rearrange("p (g d) -> p g d", d=KV_RANK), 20, 24,
                                      KV_RANK).then_inc(var_ready, 1)
                    elif kind == "a_norm":
                        newton("a")
                        ckv = CW[:, :, 0:KV_RANK]
                        link(v.tensor_tensor(ckv, ckv, rs("a", 20, 24).unsqueeze(2).broadcast_to([P, TILES, KV_RANK]),
                                             ALU.mult))
                        v.tensor_tensor(ckv, ckv, vec("kv_norm_g").unsqueeze(1).broadcast_to([P, TILES, KV_RANK]),
                                        ALU.mult).then_inc(cn_ready, 1)
                        link(v.tensor_tensor(head_view(0, 5), head_view(0, 5),
                                             rs("a", 0, 20).rearrange("p (t h) -> p t h", t=TILES).unsqueeze(3)
                                             .broadcast_to([P, TILES, 5, HEAD]), ALU.mult))
                        note(v.tensor_tensor(head_view(0, 4), head_view(0, 4),
                                             vec("q_norm_a").unsqueeze(1).unsqueeze(1)
                                             .broadcast_to([P, TILES, 4, HEAD]), ALU.mult))
                        note(v.tensor_scalar(CW[:, :, KV_RANK:], CW[:, :, KV_RANK:], (IDX_HEADS * HEAD) ** -0.5, None,
                                             ALU.mult))
                    elif kind == "kv_up":
                        dve.wait_ge(squares, 4)
                        reduce_groups("k", SQ[:, 0:256].rearrange("p (g d) -> p g d", d=HEAD), 0, 4, HEAD) \
                            .then_inc(var_ready, 1)
                    elif kind == "k_norm":
                        newton("k")
                        k = AH[:, :, 5, :]
                        link(v.tensor_tensor(k, k, rs("k").unsqueeze(2).broadcast_to([P, TILES, HEAD]), ALU.mult))
                        v.tensor_tensor(k, k, vec("k_norm_a").unsqueeze(1).broadcast_to([P, TILES, HEAD]), ALU.mult) \
                            .then_inc(a_normed, 1)
                    elif kind == "c_sq":
                        dve.wait_ge(squares, 5)
                        reduce_groups("c", SQ[:, :].rearrange("p (g d) -> p g d", d=DIFF_HALF), 0, 64, DIFF_HALF) \
                            .then_inc(var_ready, 1)
                    elif kind == "c_norm":
                        newton("c")
                        q = QK[:, :, :].rearrange("p t n -> p (t n)").rearrange("p (g d) -> p g d", d=DIFF_HALF)
                        link(v.tensor_tensor(q, q, rs("c").unsqueeze(2).broadcast_to([P, 64, DIFF_HALF]), ALU.mult))
                        for i, name in enumerate(("q_norm_c", "k_norm_c")):
                            q = QK[:, :, 256 * i:256 * i + 256].rearrange("p t (g d) -> p t g d", d=DIFF_HALF)
                            v.tensor_tensor(q, q, vec(name).unsqueeze(1).unsqueeze(1)
                                            .broadcast_to([P, TILES, 8, DIFF_HALF]), ALU.mult).then_inc(c_normed, 1)
                    elif kind == "AT":
                        ps = wait_filled(dve, (*step, 1))
                        drains(v.tensor_copy(AT[:, 4:8, tok(step[1])], ps[:, :].rearrange("p (s n) -> p s n", s=4)),
                               (*step, 1))
                    elif kind == "idx":
                        _, t, h = step
                        i = IDX.index(step)
                        n = (t + 1) * P
                        s = WORK[:, WORK_AT[t]:WORK_AT[t] + n]
                        wait_copied(dve, step)
                        w_h = CW[:, t, KV_RANK + h:KV_RANK + h + 1]
                        if h == 0:
                            settle()
                            v.tensor_scalar(s, R[:, i % 2, 0:n], w_h, None, ALU.mult).then_inc(idx_added, 1)
                        else:
                            dve.wait_ge(idx_added, i)
                            v.scalar_tensor_tensor(s, R[:, i % 2, 0:n], w_h, s, ALU.mult, ALU.add) \
                                .then_inc(idx_added, 1)
                        if h == IDX_HEADS - 1:
                            dve.wait_ge(idx_added, i + 1)
                            a = WORK_AT[t] + n - CHUNK
                            link(v.memset(WORK[0:CHUNK, a:a + CHUNK], INVALID))
                    elif kind == "top":
                        _, t, r = step
                        s = WORK[:, WORK_AT[t]:WORK_AT[t] + (t + 1) * P]
                        link(v.max(M8[:, :], s))
                        link(v.match_replace(s, M8[:, :], s, TAKEN))
                        if r == TOPK // 8 - 1:
                            link(v.tensor_scalar(s, s, TAKEN, MASKED, ALU.not_equal, ALU.mult))
                    elif kind == "att_s":
                        u = step[1:]
                        g, t, hp = u
                        i = ATT_S.index(u)
                        lb = i % 2
                        n = (t + 1) * P
                        scale = (HEAD if g == "A" else DIFF_HALF) ** -0.5
                        if i >= 2:
                            prev = ("att_pv", *ATT_S[i - 2])
                            wait_filled(dve, (*prev, list(maps_of(prev[1]))[-1]))
                            wait_filled(dve, (*prev, list(maps_of(prev[1]))[-2]))
                        bias = WORK[:, WORK_AT[t]:WORK_AT[t] + n] if g == "A" and t else const("chunk_bias")[:, SEQ - n:]
                        for m in range(4):
                            ps = wait_filled(dve, (*step, m))
                            drains(v.tensor_tensor_reduce(out=L[:, lb, m, 0:n], in0=ps[:, 0:n], in1=bias, scale=1.0,
                                                          scalar=-3.0e38, op0=ALU.add, op1=ALU.max,
                                                          accum_out=MX[:, lb, m:m + 1]), (*step, m))
                        wait_copied(dve, (*step, 2))
                        wait_copied(dve, (*step, 3))
                        v.tensor_scalar(NM[:, lb, :], MX[:, lb, :], -scale, None, ALU.mult).then_inc(max_ready, 1)
                    elif kind == "att_pv":
                        u = step[1:]
                        g, t, hp = u
                        lb = ATT_S.index(u) % 2
                        b = TURN[step][0]
                        dve.wait_ge(probs_ready, probs_counts(u))
                        link(v.reciprocal(RINV[:, lb, :], SUM[:, lb, :]))
                        if g == "C":
                            dve.wait_ge(lam_exps, 1)
                            if u == ("C", 0, 0):
                                link(v.tensor_tensor(LAM[:, 4:5], LAM[:, 3:4], LAM[:, 2:3], ALU.subtract))
                                link(v.tensor_tensor(LAM[:, 5:6], LAM[:, 4:5], vec("lam_init"), ALU.subtract))
                            link(v.tensor_tensor(RHO[:, lb, :], SUM[:, lb, 0::2], RINV[:, lb, 1::2], ALU.mult))
                            link(v.tensor_scalar(RHO[:, lb, :], RHO[:, lb, :], LAM[:, 5:6], None, ALU.mult))
                            for i in range(2):
                                v.scalar_tensor_tensor(L[:, lb, 2 * i, 0:(t + 1) * P], L[:, lb, 2 * i + 1, 0:(t + 1) * P],
                                                       RHO[:, lb, i:i + 1], L[:, lb, 2 * i, 0:(t + 1) * P], ALU.mult,
                                                       ALU.add).then_inc(combined, 1)
                            dve.wait_ge(pt_used, PT_AT[(u, 2)] + 1)
                            drains(v.tensor_tensor(YC[:, t, 128 * hp:128 * hp + 128].rearrange("p (h d) -> p h d", h=2),
                                                   PS[b][:, 0:128].rearrange("p (h d) -> p h d", h=2),
                                                   RINV[:, lb, 0::2].unsqueeze(2).broadcast_to([P, 2, HEAD]), ALU.mult),
                                   step)
                        else:
                            dve.wait_ge(pt_used, PT_AT[(u, 3)] + 1)
                            drains(v.tensor_tensor(YT[:, :].rearrange("p (h d) -> p h d", h=4),
                                                   PS[b][:, 0:256].rearrange("p (h d) -> p h d", h=4),
                                                   RINV[:, lb, :].unsqueeze(2).broadcast_to([P, 4, HEAD]), ALU.mult),
                                   step)
                            wait_copied(dve, step)
                            dve.wait_ge(gate_ready, GATES.index("A") + 1)
                            v.tensor_tensor(G[:, t, 0:256], G[:, t, 0:256], YT[:, :], ALU.mult).then_inc(ya_ready, 1)
                    elif kind == "gate":
                        dve.wait_ge(gate_exp, GATES.index(step[1]) + 1)
                        link(v.tensor_scalar(GE[:, :, :], GE[:, :, :], 1.0, None, ALU.add))
                        v.reciprocal(GE[:, :, :], GE[:, :, :]).then_inc(gate_rcp, 1)
                    elif kind == "y_sq":
                        dve.wait_ge(squares, 6)
                        reduce_groups("y", SQY[:, :, :].rearrange("p t n -> p (t n)").rearrange("p (g d) -> p g d", d=HEAD), 0, 16, HEAD) \
                            .then_inc(var_ready, 1)
                    elif kind == "c_post":
                        newton("y")
                        y = YC.rearrange("p t (h d) -> p t h d", h=HEADS)
                        link(v.tensor_tensor(y, y, rs("y").rearrange("p (t h) -> p t h", t=TILES).unsqueeze(3)
                                             .broadcast_to([P, TILES, HEADS, HEAD]), ALU.mult))
                        v.tensor_tensor(y, y, SG[:, :].unsqueeze(1).unsqueeze(1)
                                        .broadcast_to([P, TILES, HEADS, HEAD]), ALU.mult).then_inc(y_normed, 1)
                    elif kind == "dz":
                        _, h, j = step
                        n = (4 - j) * P
                        dve.wait_ge(softplus_log, DZ[(h, j)] + 1)
                        if h >= 2 and j == 3:
                            dve.wait_ge(d_args, 4 * (h - 1))
                        if h == 0 and j == 3:
                            dve.wait_ge(idx_added, len(IDX))
                        v.scalar_tensor_tensor(DL[:, h % 2, D_AT[j]:D_AT[j] + n], PS[TURN[step][0]][:, 0:n], 0.0,
                                               DAT[:, h % 2, D_AT[j]:D_AT[j] + n], ALU.max, ALU.add) \
                            .then_inc(softplus_ready, 1)
                    elif kind == "dpv":
                        h = step[1]
                        y = Y_AT["D"] + 64 * h
                        ps = wait_filled(dve, step)
                        dve.wait_ge(gate_ready, GATES.index("D") + 1)
                        drains(v.tensor_tensor(G[:, :, y:y + 64], ps[:, 0:256].rearrange("p (t d) -> p t d", t=TILES),
                                               G[:, :, y:y + 64], ALU.mult), step)
                    elif kind == "bs":
                        t = step[1]
                        if t == 0:
                            dve.wait_ge(d_args, 16)
                        if t >= 2:
                            wait_filled(dve, ("by", t - 2))
                        for par in range(2):
                            ps = wait_filled(dve, (*step, par))
                            drains(v.tensor_tensor(SD[:, t % 2, par::2, :],
                                                   ps[:, 0:256].rearrange("p (h q) -> p h q", h=2),
                                                   const("decay").rearrange("p (h q) -> p h q", h=HEADS)[:, par::2, :],
                                                   ALU.mult), (*step, par))
                    elif kind == "bkv":
                        t = step[1]
                        ps = wait_filled(dve, step)
                        a = CONSTS["state_decay"][0]
                        if t == 0:
                            dve.wait_ge(states_zeroed, 1)
                        else:
                            wait_copied(dve, ("bkv", t - 1))
                        for h in range(HEADS):
                            rows = slice(64 * (h % 2), 64 * (h % 2) + 64)
                            kv = ps[rows, 64 * h:64 * h + 64]
                            new = STATE[rows, t, h // 2, rows]
                            if t == 0:
                                ins = v.tensor_copy(new, kv)
                            else:
                                ins = v.scalar_tensor_tensor(new, STATE[rows, t - 1, h // 2, rows],
                                                             C[rows, a + h // 2:a + h // 2 + 1], kv, ALU.mult, ALU.add)
                            (note(ins) if h < HEADS - 1 else drains(ins, step))
                    elif kind == "by":
                        t = step[1]
                        ps = wait_filled(dve, step)
                        if t == 0:
                            dve.wait_ge(ks_ready, 1)
                            wait_filled(dve, ("BT", TILES - 1))
                        drains(v.tensor_tensor(YB[:, t, :].rearrange("p (h d) -> p h d", h=HEADS),
                                               ps[:, 0:256].rearrange("p (h d) -> p h d", h=HEADS),
                                               const("q_decay").unsqueeze(2).broadcast_to([P, HEADS, HEAD]), ALU.mult),
                               step)
                    elif kind == "b_sq":
                        y = QK[:, :, :].rearrange("p t n -> p (t n)")[:, 0:1024].rearrange("p (g d) -> p g d", d=HEAD)
                        for t in range(TILES):
                            wait_copied(dve, ("by", t))
                        link(v.tensor_reduce(MU[:, :], y, op=ALU.add, axis=AX))
                        link(v.tensor_scalar(MU[:, :], MU[:, :], 1.0 / HEAD, None, ALU.mult))
                        v.tensor_tensor(y, y, MU[:, :].unsqueeze(2).broadcast_to([P, 16, HEAD]), ALU.subtract) \
                            .then_inc(centred, 1)
                        dve.wait_ge(squares, 7)
                        reduce_groups("b", SQY[:, :, :].rearrange("p t n -> p (t n)").rearrange("p (g d) -> p g d", d=HEAD), 0, 16, HEAD) \
                            .then_inc(var_ready, 1)
                    elif kind == "b_post":
                        newton("b")
                        y = QK[:, :, :].rearrange("p t n -> p (t n)")[:, 0:1024].rearrange("p (g d) -> p g d", d=HEAD)
                        link(v.tensor_tensor(y, y, rs("b").unsqueeze(2).broadcast_to([P, 16, HEAD]), ALU.mult))
                        v.tensor_tensor(YB[:, :, :], YB[:, :, :],
                                        vec("ret_norm_g").unsqueeze(1).broadcast_to([P, TILES, WIDTH]), ALU.mult) \
                            .then_inc(y_normed, 1)
                    elif kind == "yT":
                        t = step[1]
                        ps = wait_filled(dve, (*step, 1))
                        drains(v.tensor_copy(hT[:, 4:8, tok(t)], ps[:, :].rearrange("p (s n) -> p s n", s=4)),
                               (*step, 1))
                    elif kind == "proj" and step[1][0] == "O":
                        _, name, t = step
                        half = X[:, t, 512 * int(name[1]):512 * int(name[1]) + 512]
                        ps = wait_filled(dve, step)
                        drains(v.tensor_tensor(half, ps[:, :], half, ALU.add), step)
                dve.drain().then_inc(layer_done, 1)
                dve.wait_ge(layer_cleared, l + 1)

        @block.gpsimd
        def _(pool):
            p = nc.gpsimd
            p.memset(STATE[:, :, :, :], 0.0).then_inc(states_zeroed, 1)
            pool.wait_ge(tables_ready, 2)
            with pool.Fori(0, DEPTH) as l:
                link, note, settle = chain(pool, pool_step)

                def rope(x1, x2, rot, heads, done):
                    f = rot.stop - rot.start
                    n = TILES * heads * f

                    def scratch(i):
                        return T[:, i, 0:n].rearrange("p (t h f) -> p t h f", t=TILES, h=heads)

                    cos = COS[:, :, rot].unsqueeze(2).broadcast_to([P, TILES, heads, f])
                    sin = SIN[:, :, rot].unsqueeze(2).broadcast_to([P, TILES, heads, f])
                    settle()
                    note(p.tensor_tensor(scratch(0), x1, sin, ALU.mult))
                    link(p.tensor_tensor(scratch(1), x2, sin, ALU.mult))
                    note(p.tensor_tensor(x1, x1, cos, ALU.mult))
                    link(p.tensor_tensor(x2, x2, cos, ALU.mult))
                    note(p.tensor_tensor(x1, x1, scratch(1), ALU.subtract))
                    p.tensor_tensor(x2, x2, scratch(0), ALU.add).then_inc(*done)

                for step in SCHEDULE:
                    kind = step[0]
                    if kind == "qi_rope":
                        wait_projected(pool, "A2")
                        rope(AH[:, :, 7:15, 0:8], AH[:, :, 7:15, 8:16], ROT_A, 8, (a_roped, 1))
                    elif kind == "a_rope":
                        pool.wait_ge(a_normed, 1)
                        pool.wait_ge(a_roped, 1)
                        rope(AH[:, :, 0:6, 0:8], AH[:, :, 0:6, 8:16], ROT_A, 6, (a_roped, 1))
                        pool.wait_ge(a_roped, 2)
                        p.tensor_copy(AH[:, :, 6, :], AH[:, :, 4, :]).then_inc(a_roped, 1)
                    elif kind == "c_rope":
                        pool.wait_ge(c_normed, 2)
                        pool.wait_ge(a_roped, 3)
                        q = QK[:, :, :].rearrange("p t (g d) -> p t g d", d=DIFF_HALF)
                        rope(q[:, :, :, 0:4], q[:, :, :, 4:8], ROT_C, 16, (c_roped, 1))
                    elif kind == "b_rope":
                        wait_projected(pool, "B0")
                        pool.wait_ge(c_roped, 1)
                        for i in range(2):
                            q = QK[:, :, 256 * i:256 * i + 256].rearrange("p t (h d) -> p t h d", d=HEAD)
                            if i:
                                pool.wait_ge(b_roped, 1)
                            rope(q[:, :, :, 0:32], q[:, :, :, 32:64], ROT_B, HEADS, (b_roped, 1))
                        pool.wait_ge(b_roped, 2)
                        for t in range(TILES):
                            ins = p.tensor_tensor(KS[:, t, :, :], QK[:, t, 256:512].rearrange("p (h d) -> p h d", d=HEAD),
                                                  const("k_decay").unsqueeze(2).broadcast_to([P, HEADS, HEAD]), ALU.mult)
                            (note(ins) if t < TILES - 1 else ins.then_inc(ks_ready, 1))
                    elif kind == "gate":
                        y = Y_AT[step[1]]
                        pool.wait_ge(gate_rcp, GATES.index(step[1]) + 1)
                        p.tensor_tensor(G[:, :, y:y + 256], G[:, :, y:y + 256], GE[:, :, :], ALU.mult) \
                            .then_inc(gate_ready, 1)
                    elif kind in ("c_post", "b_post"):
                        y = Y_AT["C" if kind == "c_post" else "B"]
                        pool.wait_ge(y_normed, 1 if kind == "c_post" else 2)
                        pool.wait_ge(gate_ready, GATES.index("C" if kind == "c_post" else "B") + 1)
                        p.tensor_tensor(G[:, :, y:y + 256], G[:, :, y:y + 256],
                                        (YC if kind == "c_post" else YB)[:, :, :], ALU.mult).then_inc(y_ready, 1)
                    elif kind == "dz":
                        _, h, j = step
                        pool.wait_ge(softplus_ready, DZ[(h, j)] + 1)
                        d = DL[:, h % 2, D_AT[j]:D_AT[j] + P]
                        p.affine_select(out=d, in_=d, compare_op=ALU.is_gt, fill=0.0, base=0, pattern=[[1, P]],
                                        channel_multiplier=-1).then_inc(softplus_masked, 1)
                    elif kind == "da":
                        _, h, j = step
                        wait_copied(pool, ("dz", h, j))
                        d = DAT[:, h % 2, D_AT[j]:D_AT[j] + P]
                        p.affine_select(out=d, in_=d, compare_op=ALU.is_gt, fill=0.0, base=0, pattern=[[1, P]],
                                        channel_multiplier=-1).then_inc(d_masked, 1)
                pool.drain().then_inc(layer_done, 1)
                pool.wait_ge(layer_done, l * 4 + 4)
                pool.sem_inc(layer_over, 1)
                pool.sem_clear(in_layer)
                pool.sem_inc(layer_cleared, 1)


def constants():
    i = np.arange(P, dtype=np.float64)
    c = np.zeros((P, N_CONST), np.float64)

    def put(name, a):
        lo, hi = CONSTS[name]
        c[:, lo:hi] = np.asarray(a).reshape(P, hi - lo)

    log_gamma = np.log1p(-(2.0 ** (-5.0 - np.arange(HEADS))))
    put("ident", np.eye(P))
    seen = ~((i[None, :] < CHUNK) & (i[:, None] >= CHUNK))
    dist = np.abs(i[:, None] - i[None, :]) - (i[None, :] + 1)
    put("decay", np.stack([np.exp(g * dist) * seen * HEAD ** -0.5 for g in log_gamma], 1))
    put("tri", np.where(i[:, None] >= i[None, :], -1.0, 0.0))
    put("neg_ones", np.full((P, P), -1.0))
    bias = np.zeros((P, SEQ))
    bias[:CHUNK, SEQ - CHUNK:] = MASKED
    put("chunk_bias", bias)
    put("k_decay", np.exp(log_gamma[None, :] * (P - 1 - i)[:, None]) * HEAD ** -0.5)
    put("q_decay", np.exp(log_gamma[None, :] * (i + 1)[:, None]))
    put("state_decay", np.exp(log_gamma * P).reshape(2, 2)[:, (i >= 64).astype(int)].T)
    freq = []
    for theta, half, rot in ((ROPE_THETA, F_A, 16), (ROPE_THETA, F_C, 8), (RET_THETA, F_B, 64)):
        freq.append(np.float32(theta) ** (-np.arange(half, dtype=np.float32) * np.float32(2.0) / np.float32(rot)))
    put("freq", np.tile(np.concatenate(freq), (P, 1)))
    return c.astype(np.float32)


def kernel(**inputs):
    import concourse.bacc as bacc
    from concourse.bass_utils import run_bass_kernel_spmd

    a = {k: np.asarray(v) for k, v in inputs.items()}
    parts = []
    for name, cols in GROUPS:
        if isinstance(cols, int):
            half = int(name[1])
            g = a["w_out"][:, :, 512 * half:512 * half + 512]
        else:
            g = np.concatenate([a["w_in"][:, :, lo:hi] for lo, hi in cols], axis=2)
        parts.append(g.reshape(DEPTH, P, -1))
    lam_init = [0.8 - 0.6 * math.exp(-0.3 * l) for l in range(DEPTH)]
    rows = {"lam_init": np.array(lam_init, np.float32)[:, None],
            "one_minus": np.array([1.0 - v for v in lam_init], np.float32)[:, None]}
    arrays = {
        "x": np.ascontiguousarray(a["x"][0]),
        "pos": np.ascontiguousarray(a["positions"].reshape(TILES, P).T),
        "w": np.ascontiguousarray(np.concatenate(parts, axis=2)),
        "norm_g": np.ascontiguousarray(a["norm_g"]),
        "vecs": np.ascontiguousarray(np.concatenate([rows.get(n, a.get(n)) for n in VECS], axis=1)),
        "w_kv": np.ascontiguousarray(a["w_kv_up"]),
        "consts": constants(),
    }
    nc = bacc.Bacc("TRN2", target_bir_lowering=False, num_devices=1)
    args = [nc.dram_tensor(f"in_{n}", v.shape, mybir.dt.from_np(v.dtype), kind="ExternalInput").ap()
            for n, v in arrays.items()]
    out = nc.dram_tensor("out", (SEQ, D_MODEL), mybir.dt.float32, kind="ExternalOutput").ap()
    encoder(nc, *args, out)
    r = run_bass_kernel_spmd(nc, [{f"in_{n}": v for n, v in arrays.items()}], core_ids=[0])
    return r.results[0]["out"].reshape(1, SEQ, D_MODEL)
```

```python
import math
from contextlib import ExitStack

import numpy as np
import concourse.bass as bass
from concourse import mybir

SEQ, D_MODEL, DEPTH, CHUNK, P = 512, 1024, 2, 64, 128
HEAD, HEADS, WIDTH = 64, 4, 256
KV_RANK, IDX_HEADS, DIFF_HALF, TOPK = 128, 8, 32, 128
EPS = 1e-6
TILES = SEQ // P
KT = D_MODEL // P
ROPE_THETA, RET_THETA = 500000.0, 10000.0

F_A, F_C, F_B = 8, 4, 32
ROT_A, ROT_C, ROT_B = slice(0, 8), slice(8, 12), slice(12, 44)
FREQS = F_A + F_C + F_B

GROUPS = [
    ("A0", [(0, 256), (896, 960)]),
    ("A1", [(256, 384), (960, 968)]),
    ("A2", [(384, 896)]),
    ("C0", [(2248, 2760)]),
    ("C1", [(2760, 3272)]),
    ("D0", [(3272, 3784)]),
    ("D1", [(3784, 4296)]),
    ("B0", [(1224, 1736)]),
    ("B1", [(1736, 2248)]),
    ("A3", [(968, 1224)]),
    ("O0", 512),
    ("O1", 512),
]
NAMES = [n for n, _ in GROUPS]
COLS = [c if isinstance(c, int) else sum(b - a for a, b in c) for _, c in GROUPS]
OFFSETS = [KT * sum(COLS[:g]) for g in range(len(GROUPS) + 1)]
SLICES = [(g, k) for g in range(len(GROUPS)) for k in range(KT)]
RAW = 3
SPLIT = 3
PAIRS = len(SLICES) // 2
PER_SLOT = PAIRS // RAW

VECS = {}
for _name, _n in (("kv_norm_g", 128), ("q_norm_a", 64), ("k_norm_a", 64), ("ret_norm_g", 256),
                  ("q_norm_c", 32), ("k_norm_c", 32), ("lam_q1", 32), ("lam_k1", 32),
                  ("lam_q2", 32), ("lam_k2", 32), ("subln_g", 64), ("lam_init", 1), ("one_minus", 1)):
    _at = max((b for _, b in VECS.values()), default=0)
    VECS[_name] = (_at, _at + _n)
N_VEC = VECS["one_minus"][1]

CONSTS = {}
for _name, _n in (("ident", P), ("decay", HEADS * P), ("tri", P), ("neg_ones", P), ("chunk_bias", SEQ),
                  ("k_decay", HEADS), ("q_decay", HEADS), ("state_decay", 2), ("freq", FREQS)):
    _at = max((b for _, b in CONSTS.values()), default=0)
    CONSTS[_name] = (_at, _at + _n)
N_CONST = CONSTS["freq"][1]

RSQ = {}
for _name, _n in (("h", 4), ("a", 24), ("k", 4), ("c", 64), ("y", 16), ("b", 16)):
    _at = max((b for _, b in RSQ.values()), default=0)
    RSQ[_name] = (_at, _at + _n)

MASKED = -1e30
INVALID = -3.0e38
TAKEN = -3.4e38
WORK_AT = {1: 0, 2: 256, 3: 640}
D_AT = {0: 0, 1: 512, 2: 896, 3: 1152}


def schedule():
    s = []
    sliced = [0]

    def slices(n):
        for i in range(sliced[0], sliced[0] + n):
            s.append(("slice", i))
            if i + 2 < len(SLICES):
                s.append(("split", i + 2))
        sliced[0] += n

    def group_end(name):
        return (NAMES.index(name) + 1) * KT - sliced[0]

    def weave(steps, name):
        n, done = group_end(name), 0
        for i, step in enumerate(steps):
            while done * len(steps) < n * (i + 1):
                slices(1)
                done += 1
            s.append(step)

    s += [("h_stats",), ("split", 0), ("split", 1), ("rsq", "h"), ("xn", 0), ("xn", 1), ("lam",)]
    for t in range(TILES):
        s.append(("xT", t))
        if t + 2 < TILES:
            s.append(("xn", t + 2))
    slices(16)
    s += [("a_sq",), ("rsq", "a")]
    slices(1)
    s += [("a_norm",)]
    slices(2)
    s += [("ckvT",)]
    slices(2)
    s += [("kv_up",), ("rsq", "k")]
    slices(2)
    s += [("k_norm",)]
    slices(1)
    s += [("qi_rope",), ("a_rope",)]
    slices(6)
    s += [("AT", t) for t in range(TILES)]
    slices(group_end("C0"))
    s += [("c_sq",), ("rsq", "c")]
    idx = [("idx", t, h) for t in (1, 2, 3) for h in range(IDX_HEADS)]
    top = [("top", t, r) for t in (1, 2, 3) for r in range(TOPK // 8)]
    weave(idx[:6] + [("c_norm",), ("c_rope",)] + idx[6:], "C1")
    s += [("gate", "C")] + [("CT", t) for t in range(TILES)]
    units = [("C", t, hp) for t in range(TILES) for hp in range(2)]
    att = []
    for i, u in enumerate(units):
        att += [("att_s", *u), top.pop(0), top.pop(0)] + ([("att_pv", *units[i - 1])] if i else []) + [top.pop(0)]
    att += [("att_pv", *units[-1])]
    weave(att, "D1")
    d = [("y_sq",), ("rsq", "y"), ("gate", "D")]
    for h in range(HEADS):
        d += [("dz", h, 3), ("dz", h, 2), ("da", h, 3), ("dz", h, 1), ("da", h, 2), ("dz", h, 0), ("da", h, 1),
              ("da", h, 0)] + ([("dpv", h - 1)] if h else [])
    d += [("dpv", HEADS - 1)]
    full = []
    for i, step in enumerate(d):
        full.append(step)
        if i == 6:
            full.append(("c_post",))
        if top:
            full.append(top.pop(0))
    full += top
    half = len(full) * 5 // 8
    n = group_end("B0")
    weave(full[:half], "B0")
    s.append(("b_rope",))
    weave(full[half:], "B1")
    s += [("gate", "B")]
    s += [("BT", t) for t in range(TILES)]
    a_units = [("A", t, 0) for t in range(TILES)]
    weave([("bkv", 0), ("bs", 0), ("bs", 1), ("bkv", 1), ("by", 0), ("bkv", 2), ("bs", 2), ("by", 1), ("bs", 3),
           ("by", 2), ("by", 3)], "A3")
    s += [("gate", "A"), ("att_s", *a_units[0]), ("b_sq",), ("rsq", "b"), ("yT", "C"), ("yT", "D")]
    slices(2)
    s += [("att_s", *a_units[1]), ("b_post",), ("att_pv", *a_units[0])]
    slices(1)
    s += [("att_s", *a_units[2]), ("att_pv", *a_units[1])]
    slices(1)
    s += [("att_s", *a_units[3]), ("att_pv", *a_units[2]), ("yT", "B")]
    slices(2)
    s += [("att_pv", *a_units[3]), ("yT", "A")]
    slices(10)
    return s


SCHEDULE = schedule()

FREE_BANKS = (4, 5, 6, 7)
OUT_ORDER = ("C", "D", "B", "A")


def fills_of(step):
    k = step[0]
    if k == "slice" and SLICES[step[1]][1] == 0:
        return [("proj", NAMES[SLICES[step[1]][0]], t) for t in range(TILES)]
    if k == "xT":
        return [(*step, j) for j in range(2)]
    if k == "yT":
        return [(*step, j) for j in range(2)]
    if k == "AT":
        return [(*step, j) for j in range(2)]
    if k in ("CT", "BT", "ckvT", "kv_up", "dpv", "idx", "bkv", "by", "dz"):
        return [step]
    if k == "bs":
        return [(*step, par) for par in range(2)]
    if k == "att_s":
        return [(*step, m) for m in range(4)]
    if k == "att_pv":
        return [step] + [(*step, m) for m in (range(4) if step[1] == "A" else (0, 2))]
    return []


def turns():
    used = {b: 0 for b in range(8)}
    told = dict(used)
    order = list(FREE_BANKS)
    kept = {}
    out = {}
    for step in SCHEDULE:
        if step[0] == "da":
            order.append(kept.pop(("dz", *step[1:])))
        for key in fills_of(step):
            b = key[2] if key[0] == "proj" else order.pop(0)
            told[b] += key[0] != "att_pv" or key != step
            out[key] = (b, used[b], told[b])
            used[b] += 1
            if key[0] == "dz" or (key[0] == "att_pv" and key == step):
                kept[key] = b
            elif key[0] != "proj":
                order.append(b)
        if step[0] == "att_pv":
            order.append(kept.pop(step))
    return out


TURN = turns()
UNITS = [s[1:] for s in SCHEDULE if s[0] == "att_pv"]
PT_AT = {}
for _u in UNITS:
    for _m in (range(4) if _u[0] == "A" else (0, 2)):
        PT_AT[(_u, _m)] = len(PT_AT)
GATES = [s[1] for s in SCHEDULE if s[0] == "gate"]
IDX = [s for s in SCHEDULE if s[0] == "idx"]
DZ = {s[1:]: n for n, s in enumerate([s for s in SCHEDULE if s[0] == "dz"])}
DA = {s[1:]: n for n, s in enumerate([s for s in SCHEDULE if s[0] == "da"])}
RSQ_AT = {s[1]: n for n, s in enumerate([s for s in SCHEDULE if s[0] == "rsq"])}
Y_AT = {"A": 0, "B": 256, "C": 512, "D": 768}
V_AT = {"C": 0, "D": 1, "B": 2}


SPLITS = [s[1] for s in SCHEDULE if s[0] == "split"]
assert SPLITS == list(range(len(SLICES)))


def encoder(nc, x, pos, w, norm_g, vecs, w_kv, consts, out):
    f32, f32r, i32 = mybir.dt.float32, mybir.dt.float32r, mybir.dt.int32
    ACT, ALU, AX = mybir.ActivationFunctionType, mybir.AluOpType, mybir.AxisListType.X
    ctx = ExitStack()
    with ctx:
        def sb(name, *shape, dt=f32):
            return ctx.enter_context(nc.sbuf_tensor(name, [P, *shape], dt))

        def sem(name):
            return ctx.enter_context(nc.semaphore(name))

        X = sb("X", TILES, D_MODEL)
        hT = [sb(f"hT_{part}", KT, SEQ, dt=f32r) for part in ("hi", "lo")]
        WR = sb("WR", RAW, 2 * 512)
        WS = [sb(f"WS_{part}", SPLIT, 512, dt=f32r) for part in ("hi", "lo")]
        AH = sb("AH", TILES, 15, HEAD)
        CW = sb("CW", TILES, KV_RANK + IDX_HEADS)
        VA = sb("VA", TILES, HEAD)
        AT = sb("AT", 8, SEQ)
        QK = sb("QK", TILES, 512)
        QKT = sb("QKT", 4, SEQ)
        V = sb("V", 3, TILES, WIDTH)
        G = sb("G", TILES, D_MODEL)
        L = sb("L", 2, 4, SEQ)
        PT = sb("PT", 2, TILES, P)
        DL = sb("DL", 2, 1280)
        WORK = sb("WORK", 1152)
        T = sb("T", 2, SEQ)
        GE = sb("GE", TILES, WIDTH)
        C = sb("C", N_CONST)
        VEC = sb("VEC", N_VEC)
        NG = sb("NG", KT)
        WKV = sb("WKV", 2 * HEAD)
        COS = sb("COS", TILES, FREQS)
        SIN = sb("SIN", TILES, FREQS)
        SS = sb("SS", 128)
        VAR = sb("VAR", 128)
        RS = sb("RS", 128)
        NEWT = sb("NEWT", 128)
        M8 = sb("M8", 8)
        MX = sb("MX", 2, 4)
        NM = sb("NM", 2, 4)
        SUM = sb("SUM", 2, 4)
        RINV = sb("RINV", 2, 4)
        RHO = sb("RHO", 2, 2)
        LAM = sb("LAM", 8)
        SG = sb("SG", HEAD)
        MU = sb("MU", 16)
        YT = sb("YT", WIDTH)
        DT = AT[:, 4:8, :]
        DAT = AH[:, :, :, :].rearrange("p t h d -> p (t h d)")[:, 0:2560].rearrange("p (b n) -> p b n", b=2)
        YC = AH[:, :, :, :].rearrange("p t h d -> p (t h d)")[:, 2560:3584].rearrange("p (t n) -> p t n", t=TILES)
        XN = L[:, :, :, :].rearrange("p a b n -> p (a b n)")[:, 0:2048].rearrange("p (a n) -> p a n", a=2)
        SQ = L[:, :, :, :].rearrange("p a b n -> p (a b n)")[:, 2048:4096]
        SQY = SQ[:, 0:1024].rearrange("p (t n) -> p t n", t=TILES)
        H32 = PT
        CKT = PT[:, 0, :, :]
        R = DL[:, :, 0:SEQ]
        SD = DL[:, :, 0:SEQ].rearrange("p b (h q) -> p b h q", h=HEADS)
        KS = T[:, :, :].rearrange("p a n -> p (a n)").rearrange("p (t h d) -> p t h d", t=TILES, h=HEADS)
        STATE = QK[:, :, :].rearrange("p t n -> p (t n)")[:, 1024:1792].rearrange("p (t s n) -> p t s n", t=3, s=2)
        YB = QK[:, :, :].rearrange("p t n -> p (t n)")[:, 0:1024].rearrange("p (t n) -> p t n", t=TILES)
        early = SQ
        ANG, TURNS_ = (early[:, a:a + TILES * FREQS].rearrange("p (t f) -> p t f", t=TILES) for a in (0, 256))
        POS = early[:, 512:516]
        POS_I = early[:, 516:520].bitcast(i32)
        PS = [ctx.enter_context(nc.psum_tensor(f"PS{b}", [P, 512], f32)) for b in range(8)]

        def const(name):
            a, b = CONSTS[name]
            return C[:, a:b]

        def vec(name):
            a, b = VECS[name]
            return VEC[:, a:b]

        IDENT = const("ident")

        x_in = [sem(f"x_in{t}") for t in range(TILES)]
        const_in = sem("const_in")
        setup_dve = sem("setup_dve")
        setup_act = sem("setup_act")
        tables_ready = sem("tables_ready")
        weights_in = [sem(f"weights_in{i}") for i in range(RAW)]
        raw_free = sem("raw_free")
        layer_done = sem("layer_done")
        layer_cleared = sem("layer_cleared")
        layer_over = sem("layer_over")
        stored = sem("stored")
        bank_filled = [sem(f"bank_filled{b}") for b in range(8)]
        bank_drained = [sem(f"bank_drained{b}") for b in range(8)]
        vecs_in = sem("vecs_in")
        w_hi_ready = sem("w_hi_ready")
        w_lo_ready = sem("w_lo_ready")
        slice_used = sem("slice_used")
        h_hi_ready = sem("h_hi_ready")
        h_lo_ready = sem("h_lo_ready")
        dve_step = sem("dve_step")
        act_step = sem("act_step")
        pool_step = sem("pool_step")
        squares = sem("squares")
        var_ready = sem("var_ready")
        rsq_guess = sem("rsq_guess")
        xn_ready = sem("xn_ready")
        lam_sums = sem("lam_sums")
        lam_exps = sem("lam_exps")
        cn_ready = sem("cn_ready")
        a_roped = sem("a_roped")
        c_roped = sem("c_roped")
        b_roped = sem("b_roped")
        ks_ready = sem("ks_ready")
        states_zeroed = sem("states_zeroed")
        idx_added = sem("idx_added")
        max_ready = sem("max_ready")
        probs_ready = sem("probs_ready")
        combined = sem("combined")
        pt_used = sem("pt_used")
        gate_clamped = sem("gate_clamped")
        sigmoid_ready = sem("sigmoid_ready")
        gate_ready = sem("gate_ready")
        softplus_log = sem("softplus_log")
        softplus_ready = sem("softplus_ready")
        softplus_masked = sem("softplus_masked")
        d_args = sem("d_args")
        d_masked = sem("d_masked")
        centred = sem("centred")
        y_normed = sem("y_normed")
        ya_ready = sem("ya_ready")
        y_ready = sem("y_ready")
        in_layer = range(bank_filled[0].num, y_ready.num + 1)

        def tok(t, n=1):
            return slice(t * P, (t + n) * P)

        def wait_filled(e, key):
            b, _, f = TURN[key]
            e.wait_ge(bank_filled[b], f)
            return PS[b]

        def wait_copied(e, key):
            b, n, _ = TURN[key]
            e.wait_ge(bank_drained[b], n + 1)

        def drains(ins, key):
            ins.then_inc(bank_drained[TURN[key][0]], 1)

        def wait_projected(e, name):
            for t in range(TILES):
                wait_copied(e, ("proj", name, t))

        def wait_slice_used(e, i):
            g, k = SLICES[i]
            if k == KT - 1:
                wait_filled(e, ("proj", NAMES[g], TILES - 1))
            else:
                e.wait_ge(slice_used, i - g + 1)

        def raw(i):
            n = COLS[SLICES[i][0]]
            return WR[:, i // 2 % RAW, (i % 2) * n:(i % 2 + 1) * n]

        def chain(e, s):
            count = [0]

            def note(ins):
                count[0] += 1
                ins.then_inc(s, 1)

            def settle():
                if count[0]:
                    e.wait_ge(s, count[0])

            def link(ins):
                note(ins)
                settle()
            return link, note, settle

        def head_view(a, b):
            return AH[:, :, a:b, :]

        def map_operands(kind, t, hp, m):
            n = (t + 1) * P
            if kind == "C":
                rows = slice(32 * m, 32 * m + 32)
                return QKT[rows, hp, tok(t)], QKT[rows, 2 + hp, 0:n], n
            base = 64 * (m % 2)
            rows = slice(base, base + 64)
            return AT[rows, m // 2, tok(t)], AT[rows, 3 if base == 0 else 2, 0:n], n

        def maps_of(kind):
            return range(4) if kind == "A" else (0, 2)

        def probs_counts(u):
            return 4 * (ATT_S.index(u) + 1)

        ATT_S = [s[1:] for s in SCHEDULE if s[0] == "att_s"]
        SETUP = 11

        block = ctx.enter_context(nc.Block())

        @block.sync
        def _(sp):
            sp.dma_start(C[:, :], consts).then_inc(const_in, 16)
            sp.dma_start(POS_I[:, :], pos).then_inc(const_in, 16)
            for t in range(TILES):
                sp.dma_start(X[:, t, :], x[tok(t), :]).then_inc(x_in[t], 16)
            sp.sem_inc(raw_free, RAW)
            with sp.Fori(0, DEPTH) as l:
                for j in range(PAIRS):
                    g, k = SLICES[2 * j]
                    n = COLS[g]
                    sp.wait_ge(raw_free, l * PAIRS + (j + 1))
                    sp.dma_start(WR[:, j % RAW, 0:2 * n],
                                 w[l][:, OFFSETS[g] + k * n:OFFSETS[g] + (k + 2) * n]).then_inc(weights_in[j % RAW], 16)
            sp.wait_ge(layer_done, 4 * DEPTH)
            for t in range(TILES):
                sp.dma_start(out[tok(t), :], X[:, t, :]).then_inc(stored, 16)
            sp.wait_ge(stored, 16 * TILES)

        @block.tensor
        def _(pe):
            def bank(key):
                b, n, _ = TURN[key]
                if n:
                    pe.wait_ge(bank_drained[b], n)
                return PS[b]

            def filled(ins, key):
                ins.then_inc(bank_filled[TURN[key][0]], 1)

            pe.wait_ge(const_in, 32)
            with pe.Fori(0, DEPTH) as l:
                for step in SCHEDULE:
                    kind = step[0]
                    if kind == "xT":
                        t = step[1]
                        pe.wait_ge(xn_ready, t + 1)
                        for j in range(2):
                            ps = bank((*step, j))
                            for i in range(4):
                                ins = pe.transpose(ps[:, tok(i)], XN[:, t % 2, 4 * j + i::KT], IDENT)
                            filled(ins, (*step, j))
                    elif kind == "slice":
                        i = step[1]
                        g, k = SLICES[i]
                        name, n = NAMES[g], COLS[g]
                        pe.wait_ge(w_lo_ready, i + 1)
                        if i % 2:
                            pe.sem_inc(raw_free, 1)
                        if i == 0:
                            pe.wait_ge(h_lo_ready, 2 * TILES)
                        if name == "O0" and k % 2 == 0:
                            for j in range(2):
                                wait_copied(pe, ("yT", OUT_ORDER[k // 2], j))
                        for t in range(TILES):
                            key = ("proj", name, t)
                            ps = bank(key) if k == 0 else PS[t]
                            for a, b in ((0, 0), (0, 1), (1, 0)):
                                first, last = (k, a, b) == (0, 0, 0), (k, a, b) == (KT - 1, 1, 0)
                                ws = WS[b][:, i % SPLIT, 0:n]
                                if name == "D0":
                                    ins = pe.matmul(ps[:, :], ws[:, tok(t)], hT[a][:, k, :], start=first, stop=last)
                                else:
                                    ins = pe.matmul(ps[:, 0:n], hT[a][:, k, tok(t)], ws, start=first, stop=last)
                            if k == KT - 1:
                                filled(ins, key)
                        if k < KT - 1:
                            ins.then_inc(slice_used, 1)
                    elif kind == "ckvT":
                        pe.wait_ge(cn_ready, 1)
                        ps = bank(step)
                        for t in range(TILES):
                            ins = pe.transpose(ps[:, tok(t)], CW[:, t, 0:KV_RANK], IDENT)
                        filled(ins, step)
                    elif kind == "kv_up":
                        wait_copied(pe, ("ckvT",))
                        pe.wait_ge(vecs_in, 48)
                        ps = bank(step)
                        for t in range(TILES):
                            ins = pe.matmul(ps[:, tok(t)], CKT[:, t, :], WKV[:, :], start=True, stop=True)
                        filled(ins, step)
                    elif kind == "AT":
                        t = step[1]
                        pe.wait_ge(a_roped, 3)
                        for j in range(2):
                            ps = bank((*step, j))
                            for i, h in enumerate(((0, 2, 4, 5), (7, 9, 11, 13))[j]):
                                ins = pe.transpose(ps[:, tok(i)],
                                                   AH[:, t, h:h + 2, :].rearrange("p h d -> p (h d)"), IDENT)
                            filled(ins, (*step, j))
                    elif kind in ("CT", "BT"):
                        t = step[1]
                        pe.wait_ge(*((c_roped, 1) if kind == "CT" else (b_roped, 2)))
                        ps = bank(step)
                        for i in range(4):
                            ins = pe.transpose(ps[:, tok(i)], QK[:, t, tok(i)], IDENT)
                        filled(ins, step)
                    elif kind == "idx":
                        _, t, h = step
                        if h == 0:
                            for u in range(t + 1):
                                wait_copied(pe, ("AT", u, 0))
                                wait_copied(pe, ("AT", u, 1))
                        ps = bank(step)
                        rows = slice(64 * (h % 2), 64 * (h % 2) + 64)
                        filled(pe.matmul(ps[:, 0:(t + 1) * P], AT[rows, 4 + h // 2, tok(t)],
                                         AT[rows, 3 if h % 2 else 2, 0:(t + 1) * P], start=True, stop=True), step)
                    elif kind == "att_s":
                        _, g, t, hp = step
                        if g == "C":
                            wait_copied(pe, ("CT", t))
                        for m in range(4):
                            q, k, n = map_operands(g, t, hp, m)
                            ps = bank((*step, m))
                            filled(pe.matmul(ps[:, 0:n], q, k, start=True, stop=True), (*step, m))
                    elif kind == "att_pv":
                        u = step[1:]
                        g, t, hp = u
                        maps = list(maps_of(g))
                        lb = ATT_S.index(u) % 2

                        def turn_over(m):
                            ps = bank((*step, m))
                            for j in range(t + 1):
                                ins = pe.transpose(ps[:, tok(j)], L[:, lb, m, tok(j)], IDENT)
                            filled(ins, (*step, m))

                        def times_v(i):
                            pt = PT_AT[(u, maps[i])]
                            wait_copied(pe, (*step, maps[i]))
                            for j in range(t + 1):
                                v = VA[:, j, :] if g == "A" else V[:, V_AT["C"], j, (2 * hp + i) * 64:(2 * hp + i + 1) * 64]
                                ins = pe.matmul(po[:, 64 * i:64 * i + 64], PT[:, pt % 2, j, :], v,
                                                start=j == 0, stop=j == t)
                            ins.then_inc(pt_used, 1)

                        if g == "A":
                            pe.wait_ge(probs_ready, probs_counts(u))
                        else:
                            pe.wait_ge(combined, 2 * (1 + [v for v in UNITS if v[0] == "C"].index(u)))
                            wait_projected(pe, "C1")
                        po = bank(step)
                        turn_over(maps[0])
                        for i in range(len(maps)):
                            if i + 1 < len(maps):
                                turn_over(maps[i + 1])
                            times_v(i)
                    elif kind == "dz":
                        _, h, j = step
                        if h == 0 and j == 3:
                            wait_projected(pe, "D0")
                        rows = slice(64 * (h % 2), 64 * (h % 2) + 64)
                        ps = bank(step)
                        filled(pe.matmul(ps[:, 0:(4 - j) * P], DT[rows, 2 + h // 2, tok(j)],
                                         DT[rows, h // 2, j * P:SEQ], start=True, stop=True), step)
                    elif kind == "da":
                        _, h, j = step
                        ps = PS[TURN[("dz", h, j)][0]]
                        pe.wait_ge(softplus_masked, DZ[(h, j)] + 1)
                        n = (4 - j) * P
                        ins = pe.matmul(ps[:, 0:n], const("tri"), DL[:, h % 2, D_AT[j]:D_AT[j] + n],
                                        start=False, stop=True, skip_group_check=True)
                        for i in range(j + 1, TILES):
                            n = (4 - i) * P
                            ins = pe.matmul(ps[:, (i - j) * P:(i - j) * P + n], const("neg_ones"),
                                            DL[:, h % 2, D_AT[i]:D_AT[i] + n], start=False, stop=True,
                                            skip_group_check=True)
                        ins.then_inc(d_args, 1)
                    elif kind == "dpv":
                        h = step[1]
                        pe.wait_ge(d_masked, 4 * (h + 1))
                        if h == 0:
                            wait_projected(pe, "D1")
                        ps = bank(step)
                        for i in range(TILES):
                            for j in range(i + 1):
                                a = D_AT[j] + (i - j) * P
                                ins = pe.matmul(ps[:, 64 * i:64 * i + 64], DAT[:, h % 2, a:a + P],
                                                V[:, V_AT["D"], j, 64 * h:64 * h + 64], start=j == 0, stop=j == i)
                        filled(ins, step)
                    elif kind == "bs":
                        t = step[1]
                        wait_copied(pe, ("BT", t))
                        for par in range(2):
                            ps = bank((*step, par))
                            rows = slice(64 * par, 64 * par + 64)
                            for pair in range(2):
                                ins = pe.matmul(ps[:, tok(pair)], QKT[rows, 2 + pair, tok(t)], QKT[rows, pair, tok(t)],
                                                start=True, stop=True)
                            filled(ins, (*step, par))
                    elif kind == "bkv":
                        t = step[1]
                        pe.wait_ge(ks_ready, 1)
                        if t == 0:
                            wait_projected(pe, "B1")
                        ps = bank(step)
                        for h in range(HEADS):
                            r = 64 * (h % 2)
                            ins = pe.matmul(ps[r:r + 64, 64 * h:64 * h + 64], KS[:, t, h, :],
                                            V[:, V_AT["B"], t, 64 * h:64 * h + 64], start=True, stop=True)
                        filled(ins, step)
                    elif kind == "by":
                        t = step[1]
                        wait_copied(pe, ("bs", t, 0))
                        wait_copied(pe, ("bs", t, 1))
                        if t:
                            wait_copied(pe, ("bkv", t - 1))
                        ps = bank(step)
                        for pair in range(2):
                            if t:
                                pe.matmul(ps[:, tok(pair)], QKT[:, pair, tok(t)], STATE[:, t - 1, pair, :],
                                          start=True, stop=True)
                            for h in (2 * pair, 2 * pair + 1):
                                ins = pe.matmul(ps[:, 64 * h:64 * h + 64], SD[:, t % 2, h, :],
                                                V[:, V_AT["B"], t, 64 * h:64 * h + 64], start=t == 0, stop=True,
                                                skip_group_check=t > 0)
                        filled(ins, step)
                    elif kind == "yT":
                        g = step[1]
                        if g == "D":
                            for h in range(HEADS):
                                wait_copied(pe, ("dpv", h))
                        elif g == "A":
                            pe.wait_ge(ya_ready, TILES)
                        else:
                            pe.wait_ge(y_ready, 1 if g == "C" else 2)
                        for j in range(2):
                            ps = bank((*step, j))
                            y = Y_AT[g] + j * P
                            for t in range(TILES):
                                ins = pe.transpose(ps[:, tok(t)], G[:, t, y:y + P], IDENT)
                            filled(ins, (*step, j))
                pe.drain().then_inc(layer_done, 1)
                pe.wait_ge(layer_cleared, l + 1)

        @block.scalar
        def _(act):
            act.wait_ge(setup_dve, SETUP)
            nc.scalar.activation(SIN[:, :, :], ANG[:, :, :], ACT.Sin).then_inc(tables_ready, 1)
            nc.scalar.activation(COS[:, :, :], TURNS_[:, :, :], ACT.Sin).then_inc(tables_ready, 1)
            act.preload_act_table_set("natural_log_exp_and_others")
            with act.Fori(0, DEPTH) as l:
                link, note, settle = chain(act, act_step)
                act.dma_start(NG[:, :], norm_g[l].rearrange("(p k) -> p k", k=KT)).then_inc(vecs_in, 16)
                act.dma_start(VEC[:, :], vecs[l].partition_broadcast(P)).then_inc(vecs_in, 16)
                act.dma_start(WKV[:, :], w_kv[l]).then_inc(vecs_in, 16)

                def copy_out(key, dst, src, scale=1.0):
                    drains(nc.scalar.activation(dst, src, ACT.Copy, scale=scale), key)

                for step in SCHEDULE:
                    kind = step[0]
                    if kind == "h_stats":
                        for t in range(2):
                            act.wait_ge(x_in[t], 16)
                            nc.scalar.activation(G[:, t, :], X[:, t, :], ACT.Square, accum_out=SS[:, t:t + 1]) \
                                .then_inc(squares, 1)
                    elif kind == "rsq":
                        a, b = RSQ[step[1]]
                        act.wait_ge(var_ready, RSQ_AT[step[1]] + 1)
                        link(nc.scalar.activation(RS[:, a:b], VAR[:, a:b], ACT.Ln))
                        nc.scalar.activation(RS[:, a:b], RS[:, a:b], ACT.Exp, scale=-0.5).then_inc(rsq_guess, 1)
                    elif kind == "lam":
                        act.wait_ge(lam_sums, 2)
                        nc.scalar.activation(LAM[:, 2:4], LAM[:, 0:2], ACT.Exp).then_inc(lam_exps, 1)
                    elif kind == "split":
                        i = step[1]
                        g, k = SLICES[i]
                        if i % 2 == 0:
                            act.wait_ge(weights_in[i // 2 % RAW], (l * PER_SLOT + (i // 2 // RAW + 1)) * 16)
                        if i >= SPLIT:
                            wait_slice_used(act, i - SPLIT)
                        nc.scalar.activation(WS[0][:, i % SPLIT, 0:COLS[g]], raw(i), ACT.Copy).then_inc(w_hi_ready, 1)
                    elif kind == "xT":
                        t = step[1]
                        for j in range(2):
                            wait_copied(act, (*step, j))
                            nc.scalar.activation(hT[0][:, 4 * j:4 * j + 4, tok(t)], H32[:, j, :, :], ACT.Copy) \
                                .then_inc(h_hi_ready, 1)
                    elif kind == "slice" and SLICES[step[1]][1] == KT - 1:
                        name = NAMES[SLICES[step[1]][0]]
                        if name[0] == "O":
                            continue
                        if name == "D0":
                            wait_copied(act, IDX[-1])
                        if name == "B0":
                            wait_filled(act, ("CT", TILES - 1))
                        for t in range(TILES):
                            key = ("proj", name, t)
                            ps = wait_filled(act, key)
                            if name == "A0":
                                copy_out(key, AH[:, t, 0:5, :].rearrange("p h d -> p (h d)"), ps[:, 0:320])
                            elif name == "A1":
                                copy_out(key, CW[:, t, :], ps[:, 0:136])
                            elif name == "A2":
                                copy_out(key, AH[:, t, 7:15, :].rearrange("p h d -> p (h d)"), ps[:, :])
                            elif name in ("C0", "B0"):
                                copy_out(key, QK[:, t, :], ps[:, :])
                            elif name == "D0":
                                copy_out(key, DT[:, t, :], ps[:, :], HEAD ** -0.5 if t < 2 else 1.0)
                            elif name == "A3":
                                copy_out(key, G[:, t, 0:256], ps[:, 0:256])
                            else:
                                note(nc.scalar.activation(V[:, V_AT[name[0]], t, :], ps[:, 0:256], ACT.Copy))
                                y = Y_AT[name[0]]
                                copy_out(key, G[:, t, y:y + 256], ps[:, 256:512])
                    elif kind == "a_sq":
                        wait_projected(act, "A0")
                        wait_projected(act, "A1")
                        note(nc.scalar.activation(SQ[:, 0:1280].rearrange("p (t h d) -> p t h d", t=TILES, h=5),
                                                  head_view(0, 5), ACT.Square))
                        nc.scalar.activation(SQ[:, 1280:1792].rearrange("p (t n) -> p t n", t=TILES),
                                             CW[:, :, 0:KV_RANK], ACT.Square).then_inc(squares, 1)
                    elif kind == "ckvT":
                        act.wait_ge(h_lo_ready, 2 * TILES)
                        ps = wait_filled(act, step)
                        copy_out(step, CKT[:, :, :], ps[:, :].rearrange("p (t n) -> p t n", t=TILES))
                    elif kind == "kv_up":
                        ps = wait_filled(act, step)
                        kv = ps[:, :].rearrange("p (t n) -> p t n", t=TILES)
                        note(nc.scalar.activation(VA[:, :, :], kv[:, :, 64:128], ACT.Copy))
                        copy_out(step, AH[:, :, 5, :], kv[:, :, 0:64])
                        wait_copied(act, step)
                        act.wait_ge(var_ready, RSQ_AT["a"] + 1)
                        nc.scalar.activation(SQ[:, 0:256].rearrange("p (t n) -> p t n", t=TILES), AH[:, :, 5, :],
                                             ACT.Square).then_inc(squares, 1)
                    elif kind == "AT":
                        ps = wait_filled(act, (*step, 0))
                        copy_out((*step, 0), AT[:, 0:4, tok(step[1])], ps[:, :].rearrange("p (s n) -> p s n", s=4))
                    elif kind in ("CT", "BT"):
                        if kind == "BT" and step[1] == 0:
                            wait_filled(act, ("att_s", "C", TILES - 1, 1, 3))
                            wait_filled(act, ("att_s", "C", TILES - 1, 1, 2))
                        ps = wait_filled(act, step)
                        copy_out(step, QKT[:, :, tok(step[1])], ps[:, :].rearrange("p (s n) -> p s n", s=4))
                    elif kind == "idx":
                        i = IDX.index(step)
                        ps = wait_filled(act, step)
                        if i >= 2:
                            act.wait_ge(idx_added, i - 1)
                        n = (step[1] + 1) * P
                        drains(nc.scalar.activation(R[:, i % 2, 0:n], ps[:, 0:n], ACT.Relu), step)
                    elif kind == "c_sq":
                        wait_projected(act, "C0")
                        act.wait_ge(var_ready, RSQ_AT["k"] + 1)
                        nc.scalar.activation(SQ[:, :], QK[:, :, :].rearrange("p t n -> p (t n)"), ACT.Square) \
                            .then_inc(squares, 1)
                    elif kind == "att_s":
                        u = step[1:]
                        g, t, hp = u
                        i = ATT_S.index(u)
                        n = (t + 1) * P
                        scale = (HEAD if g == "A" else DIFF_HALF) ** -0.5
                        act.wait_ge(max_ready, i + 1)
                        for m in range(4):
                            nc.scalar.activation(L[:, i % 2, m, 0:n], L[:, i % 2, m, 0:n], ACT.Exp,
                                                 bias=NM[:, i % 2, m:m + 1], scale=scale,
                                                 accum_out=SUM[:, i % 2, m:m + 1]).then_inc(probs_ready, 1)
                    elif kind == "att_pv":
                        u = step[1:]
                        n = (u[1] + 1) * P
                        for m in maps_of(u[0]):
                            pt = PT_AT[(u, m)]
                            ps = wait_filled(act, (*step, m))
                            if pt >= 2:
                                act.wait_ge(pt_used, pt - 1)
                            copy_out((*step, m), PT[:, pt % 2, :, :].rearrange("p j n -> p (j n)")[:, 0:n],
                                     ps[:, 0:n])
                    elif kind == "gate":
                        y = Y_AT[step[1]]
                        i = GATES.index(step[1])
                        act.wait_ge(gate_clamped, i + 1)
                        link(nc.scalar.activation(GE[:, :, :], GE[:, :, :], ACT.Exp, scale=-1.0))
                        link(nc.scalar.activation(GE[:, :, :], GE[:, :, :], ACT.Ln, bias=1.0))
                        nc.scalar.activation(GE[:, :, :], GE[:, :, :], ACT.Exp, scale=-1.0).then_inc(sigmoid_ready, 1)
                    elif kind == "y_sq":
                        for u in [u for u in UNITS if u[0] == "C"]:
                            wait_copied(act, ("att_pv", *u))
                        nc.scalar.activation(SQY[:, :, :], YC[:, :, :], ACT.Square).then_inc(squares, 1)
                    elif kind == "b_sq":
                        act.wait_ge(centred, 1)
                        nc.scalar.activation(SQY[:, :, :], YB[:, :, :], ACT.Square).then_inc(squares, 1)
                    elif kind == "dz":
                        _, h, j = step
                        a = DAT[:, h % 2, D_AT[j]:D_AT[j] + (4 - j) * P]
                        ps = wait_filled(act, step)
                        if h == 0 and j == 3:
                            wait_filled(act, ("AT", TILES - 1, 1))
                        if h >= 2 and j == 3:
                            wait_filled(act, ('dpv', h - 2))
                        link(nc.scalar.activation(a, ps[:, 0:(4 - j) * P], ACT.Abs))
                        link(nc.scalar.activation(a, a, ACT.Exp, scale=-1.0))
                        nc.scalar.activation(a, a, ACT.Ln, bias=1.0).then_inc(softplus_log, 1)
                    elif kind == "da":
                        _, h, j = step
                        act.wait_ge(d_args, DA[(h, j)] + 1)
                        act.wait_ge(softplus_ready, DZ[(h, j)] + 1)
                        drains(nc.scalar.activation(DAT[:, h % 2, D_AT[j]:D_AT[j] + (4 - j) * P],
                                                    PS[TURN[("dz", h, j)][0]][:, 0:(4 - j) * P], ACT.Exp),
                               ("dz", h, j))
                    elif kind == "yT":
                        if step[1] == OUT_ORDER[0]:
                            wait_filled(act, ("proj", "A3", TILES - 1))
                        for j in range(2):
                            ps = wait_filled(act, (*step, j))
                            nc.scalar.activation(hT[0][:, 2 * OUT_ORDER.index(step[1]) + j, :], ps[:, :], ACT.Copy) \
                                .then_inc(h_hi_ready, 1)
                act.drain().then_inc(layer_done, 1)
                act.wait_ge(layer_cleared, l + 1)

        @block.vector
        def _(dve):
            v = nc.vector
            link, note, settle = chain(dve, setup_dve)
            two_pi = 2.0 * math.pi
            c1 = 6.28125
            c2 = float(np.float32(round((two_pi - c1) * 2 ** 20) / 2 ** 20))
            c3 = two_pi - c1 - c2
            pi = 3.1415925
            magic = 1.5 * 2 ** 23
            dve.wait_ge(const_in, 32)
            link(v.tensor_copy(POS[:, :], POS_I[:, :]))
            link(v.tensor_tensor(ANG[:, :, :], POS[:, :].unsqueeze(2).broadcast_to([P, TILES, FREQS]),
                                 const("freq").unsqueeze(1).broadcast_to([P, TILES, FREQS]), ALU.mult))
            link(v.tensor_scalar(TURNS_[:, :, :], ANG[:, :, :], 1.0 / two_pi, magic, ALU.mult, ALU.add))
            link(v.tensor_scalar(TURNS_[:, :, :], TURNS_[:, :, :], magic, None, ALU.subtract))
            for c in (c1, c2, c3):
                link(v.scalar_tensor_tensor(ANG[:, :, :], TURNS_[:, :, :], -c, ANG[:, :, :], ALU.mult, ALU.add))
            link(v.tensor_scalar(COS[:, :, :], ANG[:, :, :], pi / 2, -two_pi, ALU.is_gt, ALU.mult))
            link(v.scalar_tensor_tensor(TURNS_[:, :, :], ANG[:, :, :], math.pi / 2, COS[:, :, :], ALU.add, ALU.add))
            link(v.tensor_scalar(TURNS_[:, :, :], TURNS_[:, :, :], pi, -pi, ALU.min, ALU.max))
            note(v.tensor_scalar(ANG[:, :, :], ANG[:, :, :], pi, -pi, ALU.min, ALU.max))

            dve.wait_ge(tables_ready, 2)
            with dve.Fori(0, DEPTH) as l:
                link, note, settle = chain(dve, dve_step)

                def reduce_groups(use, src, lo, hi, n):
                    a = RSQ[use][0]
                    link(v.tensor_reduce(SS[:, a + lo:a + hi], src, op=ALU.add, axis=AX))
                    return v.tensor_scalar(VAR[:, a + lo:a + hi], SS[:, a + lo:a + hi], 1.0 / n, EPS, ALU.mult, ALU.add)

                def newton(use):
                    a, b = RSQ[use]
                    dve.wait_ge(rsq_guess, RSQ_AT[use] + 1)
                    link(v.tensor_tensor(NEWT[:, a:b], RS[:, a:b], RS[:, a:b], ALU.mult))
                    link(v.tensor_tensor(NEWT[:, a:b], NEWT[:, a:b], VAR[:, a:b], ALU.mult))
                    link(v.tensor_scalar(NEWT[:, a:b], NEWT[:, a:b], -0.5, 1.5, ALU.mult, ALU.add))
                    link(v.tensor_tensor(RS[:, a:b], RS[:, a:b], NEWT[:, a:b], ALU.mult))

                def rs(use, lo=0, hi=None):
                    a, b = RSQ[use]
                    return RS[:, a + lo:(b if hi is None else a + hi)]

                def rope(x1, x2, rot, heads, done):
                    f = rot.stop - rot.start
                    n = TILES * heads * f

                    def scratch(i):
                        return T[:, i, 0:n].rearrange("p (t h f) -> p t h f", t=TILES, h=heads)

                    cos = COS[:, :, rot].unsqueeze(2).broadcast_to([P, TILES, heads, f])
                    sin = SIN[:, :, rot].unsqueeze(2).broadcast_to([P, TILES, heads, f])
                    settle()
                    note(v.tensor_tensor(scratch(0), x1, sin, ALU.mult))
                    link(v.tensor_tensor(scratch(1), x2, sin, ALU.mult))
                    note(v.tensor_tensor(x1, x1, cos, ALU.mult))
                    link(v.tensor_tensor(x2, x2, cos, ALU.mult))
                    note(v.tensor_tensor(x1, x1, scratch(1), ALU.subtract))
                    v.tensor_tensor(x2, x2, scratch(0), ALU.add).then_inc(*done)

                for step in SCHEDULE:
                    kind = step[0]
                    if kind == "h_stats":
                        for t in range(2, TILES):
                            dve.wait_ge(x_in[t], 16)
                            link(v.tensor_tensor_reduce(out=G[:, t, :], in0=X[:, t, :], in1=X[:, t, :], scale=1.0,
                                                        scalar=0.0, op0=ALU.mult, op1=ALU.add,
                                                        accum_out=SS[:, t:t + 1]))
                        dve.wait_ge(squares, 2)
                        v.tensor_scalar(VAR[:, 0:4], SS[:, 0:4], 1.0 / D_MODEL, EPS, ALU.mult, ALU.add) \
                            .then_inc(var_ready, 1)
                    elif kind == "xn":
                        t = step[1]
                        if t == 0:
                            newton("h")
                        if t >= 2:
                            wait_filled(dve, ("xT", t - 2, 1))
                        v.tensor_scalar(XN[:, t % 2, :], X[:, t, :], RS[:, t:t + 1], None, ALU.mult) \
                            .then_inc(xn_ready, 1)
                    elif kind == "lam":
                        dve.wait_ge(vecs_in, 48)
                        for i in range(2):
                            v.tensor_tensor_reduce(out=YT[:, 32 * i:32 * i + 32], in0=vec(f"lam_q{i + 1}"),
                                                   in1=vec(f"lam_k{i + 1}"), scale=1.0, scalar=0.0, op0=ALU.mult,
                                                   op1=ALU.add, accum_out=LAM[:, i:i + 1]).then_inc(lam_sums, 1)
                        note(v.tensor_scalar(SG[:, :], vec("subln_g"), vec("one_minus"), None, ALU.mult))
                    elif kind == "xT":
                        t = step[1]
                        dve.wait_ge(vecs_in, 48)
                        for j in range(2):
                            ps = wait_filled(dve, (*step, j))
                            if t:
                                dve.wait_ge(h_lo_ready, 2 * t - 1 + j)
                            drains(v.tensor_tensor(H32[:, j, :, :],
                                                   ps[:, :].rearrange("p (s n) -> p s n", s=4),
                                                   NG[:, 4 * j:4 * j + 4].unsqueeze(2).broadcast_to([P, 4, P]),
                                                   ALU.mult), (*step, j))
                    elif kind == "a_sq":
                        dve.wait_ge(squares, 3)
                        note(reduce_groups("a", SQ[:, 0:1280].rearrange("p (g d) -> p g d", d=HEAD), 0, 20, HEAD))
                        reduce_groups("a", SQ[:, 1280:1792].rearrange("p (g d) -> p g d", d=KV_RANK), 20, 24,
                                      KV_RANK).then_inc(var_ready, 1)
                    elif kind == "a_norm":
                        newton("a")
                        ckv = CW[:, :, 0:KV_RANK]
                        link(v.tensor_tensor(ckv, ckv, rs("a", 20, 24).unsqueeze(2).broadcast_to([P, TILES, KV_RANK]),
                                             ALU.mult))
                        v.tensor_tensor(ckv, ckv, vec("kv_norm_g").unsqueeze(1).broadcast_to([P, TILES, KV_RANK]),
                                        ALU.mult).then_inc(cn_ready, 1)
                        link(v.tensor_tensor(head_view(0, 5), head_view(0, 5),
                                             rs("a", 0, 20).rearrange("p (t h) -> p t h", t=TILES).unsqueeze(3)
                                             .broadcast_to([P, TILES, 5, HEAD]), ALU.mult))
                        note(v.tensor_tensor(head_view(0, 4), head_view(0, 4),
                                             vec("q_norm_a").unsqueeze(1).unsqueeze(1)
                                             .broadcast_to([P, TILES, 4, HEAD]), ALU.mult))
                        note(v.tensor_scalar(CW[:, :, KV_RANK:], CW[:, :, KV_RANK:], (IDX_HEADS * HEAD) ** -0.5, None,
                                             ALU.mult))
                    elif kind == "kv_up":
                        dve.wait_ge(squares, 4)
                        reduce_groups("k", SQ[:, 0:256].rearrange("p (g d) -> p g d", d=HEAD), 0, 4, HEAD) \
                            .then_inc(var_ready, 1)
                    elif kind == "k_norm":
                        newton("k")
                        k = AH[:, :, 5, :]
                        link(v.tensor_tensor(k, k, rs("k").unsqueeze(2).broadcast_to([P, TILES, HEAD]), ALU.mult))
                        note(v.tensor_tensor(k, k, vec("k_norm_a").unsqueeze(1).broadcast_to([P, TILES, HEAD]), ALU.mult))
                    elif kind == "qi_rope":
                        wait_projected(dve, "A2")
                        rope(AH[:, :, 7:15, 0:8], AH[:, :, 7:15, 8:16], ROT_A, 8, (a_roped, 1))
                    elif kind == "a_rope":
                        dve.wait_ge(a_roped, 1)
                        rope(AH[:, :, 0:6, 0:8], AH[:, :, 0:6, 8:16], ROT_A, 6, (a_roped, 1))
                        dve.wait_ge(a_roped, 2)
                        v.tensor_copy(AH[:, :, 6, :], AH[:, :, 4, :]).then_inc(a_roped, 1)
                    elif kind == "c_rope":
                        q = QK[:, :, :].rearrange("p t (g d) -> p t g d", d=DIFF_HALF)
                        dve.wait_ge(a_roped, 2)
                        rope(q[:, :, :, 0:4], q[:, :, :, 4:8], ROT_C, 16, (c_roped, 1))
                    elif kind == "b_rope":
                        wait_projected(dve, "B0")
                        for i in range(2):
                            q = QK[:, :, 256 * i:256 * i + 256].rearrange("p t (h d) -> p t h d", d=HEAD)
                            dve.wait_ge(*((b_roped, 1) if i else (c_roped, 1)))
                            rope(q[:, :, :, 0:32], q[:, :, :, 32:64], ROT_B, HEADS, (b_roped, 1))
                        dve.wait_ge(b_roped, 2)
                        for t in range(TILES):
                            ins = v.tensor_tensor(KS[:, t, :, :], QK[:, t, 256:512].rearrange("p (h d) -> p h d", d=HEAD),
                                                  const("k_decay").unsqueeze(2).broadcast_to([P, HEADS, HEAD]), ALU.mult)
                            (note(ins) if t < TILES - 1 else ins.then_inc(ks_ready, 1))
                    elif kind == "c_sq":
                        dve.wait_ge(squares, 5)
                        reduce_groups("c", SQ[:, :].rearrange("p (g d) -> p g d", d=DIFF_HALF), 0, 64, DIFF_HALF) \
                            .then_inc(var_ready, 1)
                    elif kind == "c_norm":
                        newton("c")
                        q = QK[:, :, :].rearrange("p t n -> p (t n)").rearrange("p (g d) -> p g d", d=DIFF_HALF)
                        link(v.tensor_tensor(q, q, rs("c").unsqueeze(2).broadcast_to([P, 64, DIFF_HALF]), ALU.mult))
                        for i, name in enumerate(("q_norm_c", "k_norm_c")):
                            q = QK[:, :, 256 * i:256 * i + 256].rearrange("p t (g d) -> p t g d", d=DIFF_HALF)
                            note(v.tensor_tensor(q, q, vec(name).unsqueeze(1).unsqueeze(1)
                                                 .broadcast_to([P, TILES, 8, DIFF_HALF]), ALU.mult))
                    elif kind == "AT":
                        ps = wait_filled(dve, (*step, 1))
                        drains(v.tensor_copy(AT[:, 4:8, tok(step[1])], ps[:, :].rearrange("p (s n) -> p s n", s=4)),
                               (*step, 1))
                    elif kind == "idx":
                        _, t, h = step
                        i = IDX.index(step)
                        n = (t + 1) * P
                        s = WORK[:, WORK_AT[t]:WORK_AT[t] + n]
                        wait_copied(dve, step)
                        w_h = CW[:, t, KV_RANK + h:KV_RANK + h + 1]
                        if h == 0:
                            settle()
                            v.tensor_scalar(s, R[:, i % 2, 0:n], w_h, None, ALU.mult).then_inc(idx_added, 1)
                        else:
                            dve.wait_ge(idx_added, i)
                            v.scalar_tensor_tensor(s, R[:, i % 2, 0:n], w_h, s, ALU.mult, ALU.add) \
                                .then_inc(idx_added, 1)
                        if h == IDX_HEADS - 1:
                            dve.wait_ge(idx_added, i + 1)
                            a = WORK_AT[t] + n - CHUNK
                            link(v.memset(WORK[0:CHUNK, a:a + CHUNK], INVALID))
                    elif kind == "top":
                        _, t, r = step
                        s = WORK[:, WORK_AT[t]:WORK_AT[t] + (t + 1) * P]
                        link(v.max(M8[:, :], s))
                        link(v.match_replace(s, M8[:, :], s, TAKEN))
                        if r == TOPK // 8 - 1:
                            link(v.tensor_scalar(s, s, TAKEN, MASKED, ALU.not_equal, ALU.mult))
                    elif kind == "att_s":
                        u = step[1:]
                        g, t, hp = u
                        i = ATT_S.index(u)
                        lb = i % 2
                        n = (t + 1) * P
                        scale = (HEAD if g == "A" else DIFF_HALF) ** -0.5
                        if i >= 2:
                            prev = ("att_pv", *ATT_S[i - 2])
                            wait_filled(dve, (*prev, list(maps_of(prev[1]))[-1]))
                            wait_filled(dve, (*prev, list(maps_of(prev[1]))[-2]))
                        bias = WORK[:, WORK_AT[t]:WORK_AT[t] + n] if g == "A" and t else const("chunk_bias")[:, SEQ - n:]
                        for m in range(4):
                            ps = wait_filled(dve, (*step, m))
                            drains(v.tensor_tensor_reduce(out=L[:, lb, m, 0:n], in0=ps[:, 0:n], in1=bias, scale=1.0,
                                                          scalar=-3.0e38, op0=ALU.add, op1=ALU.max,
                                                          accum_out=MX[:, lb, m:m + 1]), (*step, m))
                        wait_copied(dve, (*step, 2))
                        wait_copied(dve, (*step, 3))
                        v.tensor_scalar(NM[:, lb, :], MX[:, lb, :], -scale, None, ALU.mult).then_inc(max_ready, 1)
                    elif kind == "att_pv":
                        u = step[1:]
                        g, t, hp = u
                        lb = ATT_S.index(u) % 2
                        b = TURN[step][0]
                        dve.wait_ge(probs_ready, probs_counts(u))
                        link(v.reciprocal(RINV[:, lb, :], SUM[:, lb, :]))
                        if g == "C":
                            dve.wait_ge(lam_exps, 1)
                            if u == ("C", 0, 0):
                                link(v.tensor_tensor(LAM[:, 4:5], LAM[:, 3:4], LAM[:, 2:3], ALU.subtract))
                                link(v.tensor_tensor(LAM[:, 5:6], LAM[:, 4:5], vec("lam_init"), ALU.subtract))
                            link(v.tensor_tensor(RHO[:, lb, :], SUM[:, lb, 0::2], RINV[:, lb, 1::2], ALU.mult))
                            link(v.tensor_scalar(RHO[:, lb, :], RHO[:, lb, :], LAM[:, 5:6], None, ALU.mult))
                            for i in range(2):
                                v.scalar_tensor_tensor(L[:, lb, 2 * i, 0:(t + 1) * P], L[:, lb, 2 * i + 1, 0:(t + 1) * P],
                                                       RHO[:, lb, i:i + 1], L[:, lb, 2 * i, 0:(t + 1) * P], ALU.mult,
                                                       ALU.add).then_inc(combined, 1)
                            dve.wait_ge(pt_used, PT_AT[(u, 2)] + 1)
                            drains(v.tensor_tensor(YC[:, t, 128 * hp:128 * hp + 128].rearrange("p (h d) -> p h d", h=2),
                                                   PS[b][:, 0:128].rearrange("p (h d) -> p h d", h=2),
                                                   RINV[:, lb, 0::2].unsqueeze(2).broadcast_to([P, 2, HEAD]), ALU.mult),
                                   step)
                        else:
                            dve.wait_ge(pt_used, PT_AT[(u, 3)] + 1)
                            drains(v.tensor_tensor(YT[:, :].rearrange("p (h d) -> p h d", h=4),
                                                   PS[b][:, 0:256].rearrange("p (h d) -> p h d", h=4),
                                                   RINV[:, lb, :].unsqueeze(2).broadcast_to([P, 4, HEAD]), ALU.mult),
                                   step)
                            wait_copied(dve, step)
                            dve.wait_ge(gate_ready, GATES.index("A") + 1)
                            v.tensor_tensor(G[:, t, 0:256], G[:, t, 0:256], YT[:, :], ALU.mult).then_inc(ya_ready, 1)
                    elif kind == "gate":
                        y = Y_AT[step[1]]
                        i = GATES.index(step[1])
                        wait_projected(dve, {"A": "A3", "B": "B1", "C": "C1", "D": "D1"}[step[1]])
                        if i:
                            dve.wait_ge(gate_ready, i)
                        v.tensor_scalar(GE[:, :, :], G[:, :, y:y + 256], -44.0, None, ALU.max).then_inc(gate_clamped, 1)
                    elif kind == "y_sq":
                        dve.wait_ge(squares, 6)
                        reduce_groups("y", SQY[:, :, :].rearrange("p t n -> p (t n)").rearrange("p (g d) -> p g d", d=HEAD), 0, 16, HEAD) \
                            .then_inc(var_ready, 1)
                    elif kind == "c_post":
                        newton("y")
                        y = YC.rearrange("p t (h d) -> p t h d", h=HEADS)
                        link(v.tensor_tensor(y, y, rs("y").rearrange("p (t h) -> p t h", t=TILES).unsqueeze(3)
                                             .broadcast_to([P, TILES, HEADS, HEAD]), ALU.mult))
                        v.tensor_tensor(y, y, SG[:, :].unsqueeze(1).unsqueeze(1)
                                        .broadcast_to([P, TILES, HEADS, HEAD]), ALU.mult).then_inc(y_normed, 1)
                    elif kind == "dz":
                        _, h, j = step
                        n = (4 - j) * P
                        dve.wait_ge(softplus_log, DZ[(h, j)] + 1)
                        if h >= 2 and j == 3:
                            dve.wait_ge(d_args, 4 * (h - 1))
                        if h == 0 and j == 3:
                            dve.wait_ge(idx_added, len(IDX))
                        v.scalar_tensor_tensor(DL[:, h % 2, D_AT[j]:D_AT[j] + n], PS[TURN[step][0]][:, 0:n], 0.0,
                                               DAT[:, h % 2, D_AT[j]:D_AT[j] + n], ALU.max, ALU.add) \
                            .then_inc(softplus_ready, 1)
                    elif kind == "dpv":
                        h = step[1]
                        y = Y_AT["D"] + 64 * h
                        ps = wait_filled(dve, step)
                        dve.wait_ge(gate_ready, GATES.index("D") + 1)
                        drains(v.tensor_tensor(G[:, :, y:y + 64], ps[:, 0:256].rearrange("p (t d) -> p t d", t=TILES),
                                               G[:, :, y:y + 64], ALU.mult), step)
                    elif kind == "bs":
                        t = step[1]
                        if t == 0:
                            dve.wait_ge(d_args, 16)
                        if t >= 2:
                            wait_filled(dve, ("by", t - 2))
                        for par in range(2):
                            ps = wait_filled(dve, (*step, par))
                            drains(v.tensor_tensor(SD[:, t % 2, par::2, :],
                                                   ps[:, 0:256].rearrange("p (h q) -> p h q", h=2),
                                                   const("decay").rearrange("p (h q) -> p h q", h=HEADS)[:, par::2, :],
                                                   ALU.mult), (*step, par))
                    elif kind == "bkv":
                        t = step[1]
                        ps = wait_filled(dve, step)
                        a = CONSTS["state_decay"][0]
                        if t == 0:
                            dve.wait_ge(states_zeroed, 1)
                        else:
                            wait_copied(dve, ("bkv", t - 1))
                        for h in range(HEADS):
                            rows = slice(64 * (h % 2), 64 * (h % 2) + 64)
                            kv = ps[rows, 64 * h:64 * h + 64]
                            new = STATE[rows, t, h // 2, rows]
                            if t == 0:
                                ins = v.tensor_copy(new, kv)
                            else:
                                ins = v.scalar_tensor_tensor(new, STATE[rows, t - 1, h // 2, rows],
                                                             C[rows, a + h // 2:a + h // 2 + 1], kv, ALU.mult, ALU.add)
                            (note(ins) if h < HEADS - 1 else drains(ins, step))
                    elif kind == "by":
                        t = step[1]
                        ps = wait_filled(dve, step)
                        if t == 0:
                            dve.wait_ge(ks_ready, 1)
                            wait_filled(dve, ("BT", TILES - 1))
                        drains(v.tensor_tensor(YB[:, t, :].rearrange("p (h d) -> p h d", h=HEADS),
                                               ps[:, 0:256].rearrange("p (h d) -> p h d", h=HEADS),
                                               const("q_decay").unsqueeze(2).broadcast_to([P, HEADS, HEAD]), ALU.mult),
                               step)
                    elif kind == "b_sq":
                        y = QK[:, :, :].rearrange("p t n -> p (t n)")[:, 0:1024].rearrange("p (g d) -> p g d", d=HEAD)
                        for t in range(TILES):
                            wait_copied(dve, ("by", t))
                        link(v.tensor_reduce(MU[:, :], y, op=ALU.add, axis=AX))
                        link(v.tensor_scalar(MU[:, :], MU[:, :], 1.0 / HEAD, None, ALU.mult))
                        v.tensor_tensor(y, y, MU[:, :].unsqueeze(2).broadcast_to([P, 16, HEAD]), ALU.subtract) \
                            .then_inc(centred, 1)
                        dve.wait_ge(squares, 7)
                        reduce_groups("b", SQY[:, :, :].rearrange("p t n -> p (t n)").rearrange("p (g d) -> p g d", d=HEAD), 0, 16, HEAD) \
                            .then_inc(var_ready, 1)
                    elif kind == "b_post":
                        newton("b")
                        y = QK[:, :, :].rearrange("p t n -> p (t n)")[:, 0:1024].rearrange("p (g d) -> p g d", d=HEAD)
                        link(v.tensor_tensor(y, y, rs("b").unsqueeze(2).broadcast_to([P, 16, HEAD]), ALU.mult))
                        v.tensor_tensor(YB[:, :, :], YB[:, :, :],
                                        vec("ret_norm_g").unsqueeze(1).broadcast_to([P, TILES, WIDTH]), ALU.mult) \
                            .then_inc(y_normed, 1)
                    elif kind == "yT":
                        n = OUT_ORDER.index(step[1])
                        for j in range(2):
                            ps = wait_filled(dve, (*step, j))
                            dve.wait_ge(h_hi_ready, 2 * TILES + 2 * n + j + 1)
                            drains(v.tensor_tensor(hT[1][:, 2 * n + j, :], ps[:, :], hT[0][:, 2 * n + j, :].bitcast(f32),
                                                   ALU.subtract), (*step, j))
                    elif kind == "slice" and SLICES[step[1]][1] == KT - 1:
                        name = NAMES[SLICES[step[1]][0]]
                        for t in range(TILES) if name[0] == "O" else ():
                            half = X[:, t, 512 * int(name[1]):512 * int(name[1]) + 512]
                            ps = wait_filled(dve, ("proj", name, t))
                            drains(v.tensor_tensor(half, ps[:, :], half, ALU.add), ("proj", name, t))
                dve.drain().then_inc(layer_done, 1)
                dve.wait_ge(layer_cleared, l + 1)

        @block.gpsimd
        def _(pool):
            p = nc.gpsimd
            with pool.Fori(0, DEPTH) as l:
                link, note, settle = chain(pool, pool_step)

                for step in SCHEDULE:
                    kind = step[0]
                    if kind == "split":
                        i = step[1]
                        n = COLS[SLICES[i][0]]
                        pool.wait_ge(w_hi_ready, i + 1)
                        p.tensor_tensor(WS[1][:, i % SPLIT, 0:n], raw(i), WS[0][:, i % SPLIT, 0:n].bitcast(f32),
                                        ALU.subtract).then_inc(w_lo_ready, 1)
                    elif kind == "xT":
                        t = step[1]
                        for j in range(2):
                            pool.wait_ge(h_hi_ready, 2 * t + j + 1)
                            p.tensor_tensor(hT[1][:, 4 * j:4 * j + 4, tok(t)], H32[:, j, :, :],
                                            hT[0][:, 4 * j:4 * j + 4, tok(t)].bitcast(f32), ALU.subtract) \
                                .then_inc(h_lo_ready, 1)
                    elif kind == "gate":
                        y = Y_AT[step[1]]
                        pool.wait_ge(sigmoid_ready, GATES.index(step[1]) + 1)
                        p.tensor_tensor(G[:, :, y:y + 256], G[:, :, y:y + 256], GE[:, :, :], ALU.mult) \
                            .then_inc(gate_ready, 1)
                    elif step == ("bkv", 0):
                        wait_filled(pool, ("BT", TILES - 1))
                        pool.wait_ge(ks_ready, 1)
                        p.memset(STATE[:, :, :, :], 0.0).then_inc(states_zeroed, 1)
                    elif kind in ("c_post", "b_post"):
                        y = Y_AT["C" if kind == "c_post" else "B"]
                        pool.wait_ge(y_normed, 1 if kind == "c_post" else 2)
                        pool.wait_ge(gate_ready, GATES.index("C" if kind == "c_post" else "B") + 1)
                        p.tensor_tensor(G[:, :, y:y + 256], G[:, :, y:y + 256],
                                        (YC if kind == "c_post" else YB)[:, :, :], ALU.mult).then_inc(y_ready, 1)
                    elif kind == "dz":
                        _, h, j = step
                        pool.wait_ge(softplus_ready, DZ[(h, j)] + 1)
                        d = DL[:, h % 2, D_AT[j]:D_AT[j] + P]
                        p.affine_select(out=d, in_=d, compare_op=ALU.is_gt, fill=0.0, base=0, pattern=[[1, P]],
                                        channel_multiplier=-1).then_inc(softplus_masked, 1)
                    elif kind == "da":
                        _, h, j = step
                        wait_copied(pool, ("dz", h, j))
                        d = DAT[:, h % 2, D_AT[j]:D_AT[j] + P]
                        p.affine_select(out=d, in_=d, compare_op=ALU.is_gt, fill=0.0, base=0, pattern=[[1, P]],
                                        channel_multiplier=-1).then_inc(d_masked, 1)
                pool.drain().then_inc(layer_done, 1)
                pool.wait_ge(layer_done, l * 4 + 4)
                pool.sem_inc(layer_over, 1)
                pool.sem_clear(in_layer)
                pool.sem_inc(layer_cleared, 1)


def constants():
    i = np.arange(P, dtype=np.float64)
    c = np.zeros((P, N_CONST), np.float64)

    def put(name, a):
        lo, hi = CONSTS[name]
        c[:, lo:hi] = np.asarray(a).reshape(P, hi - lo)

    log_gamma = np.log1p(-(2.0 ** (-5.0 - np.arange(HEADS))))
    put("ident", np.eye(P))
    seen = ~((i[None, :] < CHUNK) & (i[:, None] >= CHUNK))
    dist = np.abs(i[:, None] - i[None, :]) - (i[None, :] + 1)
    put("decay", np.stack([np.exp(g * dist) * seen * HEAD ** -0.5 for g in log_gamma], 1))
    put("tri", np.where(i[:, None] >= i[None, :], -1.0, 0.0))
    put("neg_ones", np.full((P, P), -1.0))
    bias = np.zeros((P, SEQ))
    bias[:CHUNK, SEQ - CHUNK:] = MASKED
    put("chunk_bias", bias)
    put("k_decay", np.exp(log_gamma[None, :] * (P - 1 - i)[:, None]) * HEAD ** -0.5)
    put("q_decay", np.exp(log_gamma[None, :] * (i + 1)[:, None]))
    put("state_decay", np.exp(log_gamma * P).reshape(2, 2)[:, (i >= 64).astype(int)].T)
    freq = []
    for theta, half, rot in ((ROPE_THETA, F_A, 16), (ROPE_THETA, F_C, 8), (RET_THETA, F_B, 64)):
        freq.append(np.float32(theta) ** (-np.arange(half, dtype=np.float32) * np.float32(2.0) / np.float32(rot)))
    put("freq", np.tile(np.concatenate(freq), (P, 1)))
    return c.astype(np.float32)


def kernel(**inputs):
    import concourse.bacc as bacc
    from concourse.bass_utils import run_bass_kernel_spmd

    a = {k: np.asarray(v) for k, v in inputs.items()}
    tiles = np.concatenate([np.arange(Y_AT[g], Y_AT[g] + WIDTH) for g in OUT_ORDER])
    parts = []
    for name, cols in GROUPS:
        if isinstance(cols, int):
            half = int(name[1])
            g = a["w_out"][:, tiles, 512 * half:512 * half + 512].reshape(DEPTH, KT, P, 512).transpose(0, 2, 1, 3)
        else:
            g = np.concatenate([a["w_in"][:, :, lo:hi] for lo, hi in cols], axis=2)
        parts.append(g.reshape(DEPTH, P, -1))
    lam_init = [0.8 - 0.6 * math.exp(-0.3 * l) for l in range(DEPTH)]
    rows = {"lam_init": np.array(lam_init, np.float32)[:, None],
            "one_minus": np.array([1.0 - v for v in lam_init], np.float32)[:, None]}
    arrays = {
        "x": np.ascontiguousarray(a["x"][0]),
        "pos": np.ascontiguousarray(a["positions"].reshape(TILES, P).T),
        "w": np.ascontiguousarray(np.concatenate(parts, axis=2)),
        "norm_g": np.ascontiguousarray(a["norm_g"]),
        "vecs": np.ascontiguousarray(np.concatenate([rows.get(n, a.get(n)) for n in VECS], axis=1)),
        "w_kv": np.ascontiguousarray(a["w_kv_up"]),
        "consts": constants(),
    }
    nc = bacc.Bacc("TRN2", target_bir_lowering=False, num_devices=1)
    args = [nc.dram_tensor(f"in_{n}", v.shape, mybir.dt.from_np(v.dtype), kind="ExternalInput").ap()
            for n, v in arrays.items()]
    out = nc.dram_tensor("out", (SEQ, D_MODEL), mybir.dt.float32, kind="ExternalOutput").ap()
    encoder(nc, *args, out)
    r = run_bass_kernel_spmd(nc, [{f"in_{n}": v for n, v in arrays.items()}], core_ids=[0])
    return r.results[0]["out"].reshape(1, SEQ, D_MODEL)
```

```python
import math
from contextlib import ExitStack

import numpy as np
import concourse.bass as bass
from concourse import mybir

SEQ, D_MODEL, DEPTH, CHUNK, P = 512, 1024, 2, 64, 128
HEAD, HEADS, WIDTH = 64, 4, 256
KV_RANK, IDX_HEADS, DIFF_HALF, TOPK = 128, 8, 32, 128
EPS = 1e-6
TILES = SEQ // P
KT = D_MODEL // P
ROPE_THETA, RET_THETA = 500000.0, 10000.0

F_A, F_C, F_B = 8, 4, 32
ROT_A, ROT_C, ROT_B = slice(0, 8), slice(8, 12), slice(12, 44)
FREQS = F_A + F_C + F_B

GROUPS = [
    ("A0", [(0, 256), (896, 960), (256, 384), (960, 968)]),
    ("A2", [(384, 896)]),
    ("C0", [(2248, 2760)]),
    ("C1", [(2760, 3272)]),
    ("D0", [(3272, 3784)]),
    ("A3", [(968, 1224)]),
    ("D1", [(3784, 4296)]),
    ("B0", [(1224, 1736)]),
    ("B1", [(1736, 2248)]),
    ("O0", 512),
    ("O1", 512),
]
NAMES = [n for n, _ in GROUPS]
COLS = [c if isinstance(c, int) else sum(b - a for a, b in c) for _, c in GROUPS]
OFFSETS = [KT * sum(COLS[:g]) for g in range(len(GROUPS) + 1)]
SLICES = [(g, k) for g in range(len(GROUPS)) for k in range(KT)]
RAW = 4
SPLIT = 3
PAIRS = len(SLICES) // 2
PER_SLOT = PAIRS // RAW

VECS = {}
for _name, _n in (("kv_norm_g", 128), ("q_norm_a", 64), ("k_norm_a", 64), ("ret_norm_g", 256),
                  ("q_norm_c", 32), ("k_norm_c", 32), ("lam_q1", 32), ("lam_k1", 32),
                  ("lam_q2", 32), ("lam_k2", 32), ("subln_g", 64), ("lam_init", 1), ("one_minus", 1)):
    _at = max((b for _, b in VECS.values()), default=0)
    VECS[_name] = (_at, _at + _n)
N_VEC = VECS["one_minus"][1]

CONSTS = {}
for _name, _n in (("ident", P), ("freq", FREQS), ("decay", HEADS * P), ("chunk_bias", SEQ),
                  ("k_decay", HEADS), ("q_decay", HEADS), ("state_decay", 2)):
    _at = max((b for _, b in CONSTS.values()), default=0)
    CONSTS[_name] = (_at, _at + _n)
N_CONST = CONSTS["state_decay"][1]
FIRST_CONSTS = CONSTS["freq"][1]

RSQ = {}
for _name, _n in (("h", 4), ("a", 24), ("k", 4), ("c", 64), ("y", 16), ("b", 16)):
    _at = max((b for _, b in RSQ.values()), default=0)
    RSQ[_name] = (_at, _at + _n)

MASKED = -1e30
INVALID = -3.0e38
TAKEN = -3.4e38
SLOT = ("slot",)
WORK_AT = {1: 0, 2: 256, 3: 640}
D_AT = {0: 0, 1: 512, 2: 896, 3: 1152}


EARLY_SLICES = (1, 1, 2, 1, 2, 1, 1, 2, 2, 2, 1, 1, 1, 6)
LATE_SLICES = (1, 1, 1, 2, 1)
C_STEPS_AT = (2, 4, 6, 9, 10, 16, 18)
BEFORE_V = (3, 2, 2, 2, 2, 3, 2, 3)
AFTER_V = (1, 3, 2, 2, 2, 2, 2, 2)
AFTER_C = (0, 0, 0, 0, 0, 0, 0, 0)
IN_HEADS = ((1, 1, 1, 1, 0),
            (1, 1, 1, 1, 0),
            (1, 1, 1, 1, 0))
GATE_AT = (1, 5)
GATED_AT = (2, 6)
TURNED_FIRST = (0, 1, 0, 0, 0, 0, 0)


def schedule():
    s = []
    sliced = [0]

    def slices(n):
        for i in range(sliced[0], sliced[0] + n):
            if i + 2 < len(SLICES):
                s.append(("split", i + 2))
            s.append(("slice", i))
        sliced[0] += n

    def group_end(name):
        return (NAMES.index(name) + 1) * KT - sliced[0]

    def weave(steps, name):
        cols = [COLS[g] for g, _ in SLICES[sliced[0]:sliced[0] + group_end(name)]]
        slots, done, at = steps.count(SLOT), 0, 0
        for step in steps:
            if step == SLOT:
                at += 1
                while sum(cols[:done]) * slots < sum(cols) * at:
                    slices(1)
                    done += 1
            else:
                s.append(step)

    s += [("xT", 0, 0), ("split", 0), ("xT", 0, 1), ("xT", 0, 2), ("split", 1), ("xT", 0, 3), ("xT", 1, 0), ("xT", 1, 1)]
    slices(EARLY_SLICES[0])
    s += [("xT", 1, 2)]
    slices(EARLY_SLICES[1])
    s += [("xT", 1, 3)]
    slices(EARLY_SLICES[2])
    s += [("h_stats",)]
    slices(EARLY_SLICES[3])
    s += [("rsq", "h"), ("h_rs",), ("lam",)]
    slices(EARLY_SLICES[4])
    s += [("rs_row",)]
    slices(EARLY_SLICES[5])
    s += [("a_sq",)]
    slices(EARLY_SLICES[6])
    s += [("rsq", "a")]
    slices(EARLY_SLICES[7])
    s += [("a_norm",)]
    slices(EARLY_SLICES[8])
    s += [("ckvT",)]
    slices(EARLY_SLICES[9])
    s += [("kv_up",)]
    slices(EARLY_SLICES[10])
    s += [("rsq", "k")]
    slices(EARLY_SLICES[11])
    s += [("k_norm",)]
    slices(EARLY_SLICES[12])
    s += [("qi_rope",), ("a_rope",)]
    slices(EARLY_SLICES[13])
    s += [("AT", t) for t in range(TILES)]
    slices(group_end("C0"))
    s += [("c_sq",)]
    top = [("top", t, r) for t in (1, 2, 3) for r in range(TOPK // 8)]
    idx = []
    between = {}
    c_steps = [[("rsq", "c")], [("c_norm", 0)], [("c_norm", 1)], [("c_rope", 0)], [("c_rope", 1)],
               [("CT", 0), ("CT", 1)], [("CT", 2), ("CT", 3)]]
    for n, steps in zip(C_STEPS_AT, c_steps):
        between.setdefault(n, []).extend(steps)
    for n, u in enumerate([("idx", t, h) for t in (1, 2, 3) for h in range(IDX_HEADS)]):
        idx += [u, SLOT] + between.get(n, [])
    weave(idx, "C1")

    def take(n):
        n = max(n, 0)
        out, top[:] = top[:n], top[n:]
        return out

    units = [("C", t, hp) for t in range(TILES) for hp in range(2)]
    att = [("att_s", *units[0]), ("att_e", *units[0]), SLOT] + take(2) + [SLOT, ("att_c", *units[0])]
    for i, u in enumerate(units):
        scores, turned = [("att_s", *units[i + 1])] if i + 1 < len(units) else [], [("att_t", *u, 0), ("att_t", *u, 2)]
        att += turned + scores if i < 7 and TURNED_FIRST[i] else scores + turned
        if i + 1 < len(units):
            att += [("att_e", *units[i + 1])]
        att += take(BEFORE_V[i]) + [SLOT]
        att += [("gate", g) for g, at in zip("CA", GATE_AT) if i == at]
        att += [("gated", g) for g, at in zip("CA", GATED_AT) if i == at]
        att += [("att_v", *u, 0), ("att_v", *u, 2)] + take(AFTER_V[i])
        if i + 1 < len(units):
            att += [("att_c", *units[i + 1])] + take(AFTER_C[i])
        att += [SLOT]
    weave(att, "D1")
    d = []
    for h in range(HEADS):
        a = ("A", h, 0)
        places = iter((*IN_HEADS, (0,) * 5)[h])
        d += take(len(top) - 16 * (3 - h))
        d += [("att_s", *a), ("dz", h, 3), ("dz", h, 2), ("dlo", h, 3), ("dlo", h, 2)] + take(next(places))
        d += [SLOT] + take(next(places))
        if h == 1:
            d += [("gated", "D")]
        if h:
            d += [("dpv", h - 1)]
        d += [("att_e", *a)] + take(next(places))
        if h == 2:
            d += [("rsq", "y")]
        if h > 1:
            d += [("b_rope", 2 * (h - 2))]
        d += [SLOT, ("da", h, 3), ("da", h, 2), ("dz", h, 1), ("dz", h, 0), ("dlo", h, 1), ("dlo", h, 0),
              ("att_t", *a, 0), ("att_t", *a, 1)]
        if h == 1:
            d += [("y_sq",)]
        if h == 2:
            d += [("c_post",)]
        if h == 3:
            d += [("b_rope", 3)]
        d += take(next(places)) + [SLOT, ("att_c", *a)]
        d += [("att_v", *a, 0), ("att_t", *a, 2), ("att_v", *a, 1), ("att_t", *a, 3)] + take(next(places))
        d += [SLOT, ("da", h, 1), ("da", h, 0)]
        if h == 0:
            d += [("gate", "D")]
        d += [("att_v", *a, 2), ("att_v", *a, 3)]
        if h == 2:
            d += [("b_rope", 1)]
    cut = [i for i, x in enumerate(d) if x == ("b_rope", 0)][0]
    weave(d[:cut], "B0")
    weave(d[cut:] + [("ks",), ("dpv", HEADS - 1)], "B1")
    assert not top
    s += [("BT", t) for t in range(TILES)]
    s += [("yT", "C", 0), ("yT", "C", 1), ("bs", 0), ("gate", "B"), ("bkv", 0), ("bs", 1), ("bkv", 1)]
    slices(LATE_SLICES[0])
    s += [("bs", 2), ("by", 0), ("bkv", 2), ("b_mu", 0), ("by", 1), ("yT", "D", 0), ("yT", "D", 1)]
    slices(LATE_SLICES[1])
    s += [("bs", 3), ("gated", "B"), ("b_mu", 1), ("by", 2), ("b_mu", 2), ("by", 3), ("b_mu", 3)]
    s += [("yT", "A", 0), ("yT", "A", 1)]
    slices(LATE_SLICES[2])
    s += [("gains",), ("b_sq",), ("rsq", "b")]
    slices(LATE_SLICES[3])
    s += [("b_post",)]
    s += [("yT", "B", 0)]
    slices(LATE_SLICES[4])
    s += [("yT", "B", 1)]
    slices(len(SLICES) - sliced[0])
    return s


SCHEDULE = schedule()

FREE_BANKS = (4, 5, 6, 7)
OUT_ORDER = ("C", "D", "A", "B")
MAPS = {"A": (0, 1, 2, 3), "C": (0, 2)}


def fills_of(step):
    k = step[0]
    if k == "slice" and SLICES[step[1]][1] == 0:
        return [("proj", NAMES[SLICES[step[1]][0]], t) for t in range(TILES)]
    if k == "AT":
        return [(*step, j) for j in range(2)]
    if k in ("CT", "BT", "ckvT", "kv_up", "dpv", "idx", "bkv", "by", "dz", "att_t", "rs_row", "xT", "yT"):
        return [step]
    if k == "bs":
        return [(*step, par) for par in range(2)]
    if k == "att_s":
        return [(*step, m) for m in range(4)]
    if k == "att_v" and step[-1] == 0:
        return [("att_o", *step[1:4])]
    return []


def turns():
    used = {b: 0 for b in range(8)}
    told = dict(used)
    order = list(FREE_BANKS)
    kept = {}
    out = {}
    for step in SCHEDULE:
        if step[0] == "da":
            order.append(kept.pop(("dz", *step[1:])))
        for key in fills_of(step):
            b = key[2] if key[0] == "proj" else order.pop(0)
            told[b] += key[0] != "att_o"
            out[key] = (b, used[b], told[b])
            used[b] += 1
            if key[0] in ("dz", "att_o"):
                kept[key] = b
            elif key[0] != "proj":
                order.append(b)
        if step[0] == "att_v" and step[-1] == MAPS[step[1]][-1]:
            order.append(kept.pop(("att_o", *step[1:4])))
    return out


TURN = turns()
UNITS = [s[1:] for s in SCHEDULE if s[0] == "att_s"]
PT_AT = {s[1:]: n for n, s in enumerate([s for s in SCHEDULE if s[0] == "att_t"])}
PV_AT = {s[1:]: n for n, s in enumerate([s for s in SCHEDULE if s[0] == "att_v"])}
assert list(PT_AT) == list(PV_AT)
GATES = [s[1] for s in SCHEDULE if s[0] == "gate"]
IDX = [s for s in SCHEDULE if s[0] == "idx"]
DZ = {s[1:]: n for n, s in enumerate([s for s in SCHEDULE if s[0] == "dz"])}
DA = {s[1:]: n for n, s in enumerate([s for s in SCHEDULE if s[0] == "da"])}
RSQ_AT = {s[1]: n for n, s in enumerate([s for s in SCHEDULE if s[0] == "rsq"])}
Y_AT = {"A": 0, "B": 256, "C": 512, "D": 768}
V_AT = {"C": 0, "D": 1, "B": 0}


def encoder(nc, x, pos, w, norm_g, vecs, w_kv, consts, signs, out):
    f32, f32r, i32 = mybir.dt.float32, mybir.dt.float32r, mybir.dt.int32
    ACT, ALU, AX = mybir.ActivationFunctionType, mybir.AluOpType, mybir.AxisListType.X
    ctx = ExitStack()
    with ctx:
        def sb(name, *shape, dt=f32):
            return ctx.enter_context(nc.sbuf_tensor(name, [P, *shape], dt))

        def sem(name):
            return ctx.enter_context(nc.semaphore(name))

        X = sb("X", TILES, D_MODEL)
        hT = [sb(f"hT_{part}", KT, SEQ, dt=f32r) for part in ("hi", "lo")]
        WR = sb("WR", RAW, 2 * 512)
        WS = [sb(f"WS_{part}", SPLIT, 512, dt=f32r) for part in ("hi", "lo")]
        AH = sb("AH", TILES, 15, HEAD)
        CW = sb("CW", TILES, KV_RANK + IDX_HEADS)
        VA = sb("VA", TILES, HEAD)
        AT = sb("AT", 8, SEQ)
        QK = sb("QK", TILES, 512)
        QKT = sb("QKT", 4, SEQ)
        V = sb("V", 2, TILES, WIDTH)
        G = sb("G", TILES, D_MODEL)
        L = sb("L", 2, 4, SEQ)
        PT = sb("PT", 2, TILES, P)
        DL = sb("DL", 1280)
        DS = [sb(f"DS_{part}", 1280, dt=f32r) for part in ("hi", "lo")]
        SIGNS = sb("SIGNS", 2, P, dt=f32r)
        WORK = sb("WORK", 1152)
        T = sb("T", 2, SEQ)
        C = sb("C", N_CONST)
        VEC = sb("VEC", N_VEC)
        NG = sb("NG", KT)
        WKV = sb("WKV", 2 * HEAD)
        COS = sb("COS", TILES, FREQS)
        SIN = sb("SIN", TILES, FREQS)
        SS = sb("SS", 128)
        VAR = sb("VAR", 128)
        RS = sb("RS", 128)
        NEWT = sb("NEWT", 128)
        M8 = sb("M8", 8)
        MX = sb("MX", 2, 4)
        NM = sb("NM", 2, 4)
        SUM = sb("SUM", 2, 4)
        RINV = sb("RINV", 2, 4)
        RHO = sb("RHO", 2, 2)
        LAM = sb("LAM", 8)
        SG = sb("SG", HEAD)
        MU = sb("MU", 16)
        YT = sb("YT", WIDTH)
        DT = AT[:, 4:8, :]
        DAT = AH[:, :, :, :].rearrange("p t h d -> p (t h d)")[:, 0:2560].rearrange("p (b n) -> p b n", b=2)
        YC = AH[:, :, :, :].rearrange("p t h d -> p (t h d)")[:, 2560:3584].rearrange("p (t n) -> p t n", t=TILES)
        SQ = L[:, :, :, :].rearrange("p a b n -> p (a b n)")[:, 2048:4096]
        SQY = T[:, :, :].rearrange("p a n -> p (a n)").rearrange("p (t n) -> p t n", t=TILES)
        SQY_HEADS = T[:, :, :].rearrange("p a n -> p (a n)").rearrange("p (g d) -> p g d", d=HEAD)
        H32 = PT
        CKT = PT[:, 0, :, :]
        R = DL[:, 0:2 * SEQ].rearrange("p (b n) -> p b n", b=2)
        RSB = V[:, 1, 0:2, :].rearrange("p t n -> p (t n)")
        SD = R.rearrange("p b (h q) -> p b h q", h=HEADS)
        GE = {g: (L[:, 0, :, :] if g == "B" else T[:, :, :]).rearrange("p a n -> p (a n)")[:, 0:1024]
              .rearrange("p (t n) -> p t n", t=TILES) for g in "ABCD"}
        KS = T[:, :, :].rearrange("p a n -> p (a n)").rearrange("p (t h d) -> p t h d", t=TILES, h=HEADS)
        STATE = QK[:, :, :].rearrange("p t n -> p (t n)")[:, 1024:1792].rearrange("p (t s n) -> p t s n", t=3, s=2)
        YB = QK[:, :, :].rearrange("p t n -> p (t n)")[:, 0:1024].rearrange("p (t n) -> p t n", t=TILES)
        SIGNS_RAW = V[:, 0, 0, :]
        early = SQ
        ANG, TURNS_ = (early[:, a:a + TILES * FREQS].rearrange("p (t f) -> p t f", t=TILES) for a in (0, 256))
        POS = early[:, 512:516]
        POS_I = early[:, 516:520].bitcast(i32)
        PS = [ctx.enter_context(nc.psum_tensor(f"PS{b}", [P, 512], f32)) for b in range(8)]

        def const(name):
            a, b = CONSTS[name]
            return C[:, a:b]

        def vec(name):
            a, b = VECS[name]
            return VEC[:, a:b]

        IDENT = const("ident")

        x_in = [[sem(f"x_in{j}_{t}") for t in range(TILES)] for j in range(2)]
        first_in = sem("first_in")
        const_in = sem("const_in")
        signs_in = sem("signs_in")
        signs_ready = sem("signs_ready")
        setup_dve = sem("setup_dve")
        tables_ready = sem("tables_ready")
        norm_in = sem("norm_in")
        weights_in = [sem(f"weights_in{i}") for i in range(RAW)]
        raw_free = sem("raw_free")
        layer_done = sem("layer_done")
        layer_cleared = sem("layer_cleared")
        layer_over = sem("layer_over")
        x_added = sem("x_added")
        stored = sem("stored")
        bank_filled = [sem(f"bank_filled{b}") for b in range(8)]
        bank_drained = [sem(f"bank_drained{b}") for b in range(8)]
        vecs_in = sem("vecs_in")
        w_hi_ready = sem("w_hi_ready")
        w_lo_ready = sem("w_lo_ready")
        slice_used = sem("slice_used")
        h_hi_ready = sem("h_hi_ready")
        h_lo_dve = sem("h_lo_dve")
        h_lo_pool = sem("h_lo_pool")
        h_rs_ready = sem("h_rs_ready")
        dve_step = sem("dve_step")
        act_step = sem("act_step")
        squares = sem("squares")
        var_ready = sem("var_ready")
        rsq_guess = sem("rsq_guess")
        lam_sums = sem("lam_sums")
        lam_exps = sem("lam_exps")
        cn_ready = sem("cn_ready")
        a_roped = sem("a_roped")
        c_roped = sem("c_roped")
        b_roped = sem("b_roped")
        ks_ready = sem("ks_ready")
        states_zeroed = sem("states_zeroed")
        idx_added = sem("idx_added")
        max_ready = sem("max_ready")
        probs_ready = sem("probs_ready")
        combined = sem("combined")
        pt_used = sem("pt_used")
        gate_clamped = sem("gate_clamped")
        sigmoid_ready = sem("sigmoid_ready")
        gate_ready = sem("gate_ready")
        softplus_log = sem("softplus_log")
        softplus_ready = sem("softplus_ready")
        softplus_masked = sem("softplus_masked")
        softplus_hi = sem("softplus_hi")
        softplus_split = sem("softplus_split")
        d_args = sem("d_args")
        d_masked = sem("d_masked")
        centred = sem("centred")
        yc_normed = sem("yc_normed")
        gains_ready = sem("gains_ready")
        yb_ready = sem("yb_ready")
        ya_ready = sem("ya_ready")
        yc_ready = sem("yc_ready")
        in_layer = range(bank_filled[0].num, yc_ready.num + 1)

        def tok(t, n=1):
            return slice(t * P, (t + n) * P)

        def wait_filled(e, key):
            b, _, f = TURN[key]
            e.wait_ge(bank_filled[b], f)
            return PS[b]

        def wait_copied(e, key):
            b, n, _ = TURN[key]
            e.wait_ge(bank_drained[b], n + 1)

        def drains(ins, key):
            ins.then_inc(bank_drained[TURN[key][0]], 1)

        def wait_projected(e, name):
            for t in range(TILES):
                wait_copied(e, ("proj", name, t))

        def wait_h_split(e, j, t):
            e.wait_ge((h_lo_dve, h_lo_pool)[t % 2], 2 * j + t // 2 + 1)

        def wait_slice_used(e, i):
            g, k = SLICES[i]
            if k == KT - 1:
                wait_filled(e, ("proj", NAMES[g], TILES - 1))
            else:
                e.wait_ge(slice_used, i - g + 1)

        def raw(i):
            n = COLS[SLICES[i][0]]
            return WR[:, i // 2 % RAW, (i % 2) * n:(i % 2 + 1) * n]

        def chain(e, s):
            count = [0]

            def note(ins):
                count[0] += 1
                ins.then_inc(s, 1)

            def settle():
                if count[0]:
                    e.wait_ge(s, count[0])

            def link(ins):
                note(ins)
                settle()
            return link, note, settle

        def head_view(a, b):
            return AH[:, :, a:b, :]

        def map_operands(kind, t, hp, m):
            n = (t + 1) * P
            if kind == "C":
                rows = slice(32 * m, 32 * m + 32)
                return QKT[rows, hp, tok(t)], QKT[rows, 2 + hp, 0:n], n
            base = 64 * (m % 2)
            rows = slice(base, base + 64)
            return AT[rows, m // 2, tok(t)], AT[rows, 3 if base == 0 else 2, 0:n], n

        def probs_counts(u):
            return 4 * (UNITS.index(u) + 1)

        C_UNITS = [u for u in UNITS if u[0] == "C"]
        SETUP = 11

        block = ctx.enter_context(nc.Block())

        @block.sync
        def _(sp):
            sp.dma_start(C[:, 0:FIRST_CONSTS], consts[:, 0:FIRST_CONSTS]).then_inc(first_in, 16)
            for t in range(TILES):
                sp.dma_start(X[:, t, 0:512], x[tok(t), 0:512]).then_inc(x_in[0][t], 16)
            sp.sem_inc(raw_free, RAW)
            with sp.Fori(0, DEPTH) as l:
                for j in range(PAIRS):
                    g, k = SLICES[2 * j]
                    n = COLS[g]
                    sp.wait_ge(raw_free, l * PAIRS + (j + 1))
                    sp.dma_start(WR[:, j % RAW, 0:2 * n],
                                 w[l][:, OFFSETS[g] + k * n:OFFSETS[g] + (k + 2) * n]).then_inc(weights_in[j % RAW], 16)
            for i in range(2 * TILES):
                t, half = i % TILES, slice(512 * (i // TILES), 512 * (i // TILES) + 512)
                sp.wait_ge(x_added, 2 * TILES * (DEPTH - 1) + i + 1)
                sp.dma_start(out[tok(t), half], X[:, t, half]).then_inc(stored, 16)
            sp.wait_ge(stored, 16 * 2 * TILES)

        @block.tensor
        def _(pe):
            def bank(key):
                b, n, _ = TURN[key]
                if n:
                    pe.wait_ge(bank_drained[b], n)
                return PS[b]

            def filled(ins, key):
                ins.then_inc(bank_filled[TURN[key][0]], 1)

            pe.wait_ge(first_in, 32)
            with pe.Fori(0, DEPTH) as l:
                for step in SCHEDULE:
                    kind = step[0]
                    if kind == "xT":
                        _, j, t = step
                        pe.wait_ge(x_in[j][t], 16)
                        ps = bank(step)
                        for i in range(4):
                            ins = pe.transpose(ps[:, tok(i)], X[:, t, tok(4 * j + i)], IDENT)
                        filled(ins, step)
                    elif kind == "slice":
                        i = step[1]
                        g, k = SLICES[i]
                        name, n = NAMES[g], COLS[g]
                        pe.wait_ge(w_lo_ready, i + 1)
                        if i % 2:
                            pe.sem_inc(raw_free, 1)
                        if name == "O0":
                            wait_copied(pe, ("yT", OUT_ORDER[k // 2], k % 2))
                        for t in range(TILES):
                            key = ("proj", name, t)
                            if i in (0, 4):
                                wait_h_split(pe, i // 4, t)
                            ps = bank(key) if k == 0 else PS[t]
                            for a, b in ((0, 0), (0, 1), (1, 0)):
                                first, last = (k, a, b) == (0, 0, 0), (k, a, b) == (KT - 1, 1, 0)
                                ws = WS[b][:, i % SPLIT, 0:n]
                                if name == "D0":
                                    ins = pe.matmul(ps[:, :], ws[:, tok(t)], hT[a][:, k, :], start=first, stop=last)
                                else:
                                    ins = pe.matmul(ps[:, 0:n], hT[a][:, k, tok(t)], ws, start=first, stop=last)
                            if k == KT - 1:
                                filled(ins, key)
                        if k < KT - 1:
                            ins.then_inc(slice_used, 1)
                    elif kind == "rs_row":
                        pe.wait_ge(h_rs_ready, 1)
                        ps = bank(step)
                        for t in range(TILES):
                            ins = pe.matmul(ps[:, tok(t)], RS[:, t:t + 1].broadcast_to([P, P]), IDENT, start=True,
                                            stop=True)
                        filled(ins, step)
                    elif kind == "ckvT":
                        pe.wait_ge(cn_ready, 1)
                        ps = bank(step)
                        for t in range(TILES):
                            ins = pe.transpose(ps[:, tok(t)], CW[:, t, 0:KV_RANK], IDENT)
                        filled(ins, step)
                    elif kind == "kv_up":
                        wait_copied(pe, ("ckvT",))
                        pe.wait_ge(vecs_in, 32)
                        ps = bank(step)
                        for t in range(TILES):
                            ins = pe.matmul(ps[:, tok(t)], CKT[:, t, :], WKV[:, :], start=True, stop=True)
                        filled(ins, step)
                    elif kind == "AT":
                        t = step[1]
                        pe.wait_ge(a_roped, 3)
                        for j in range(2):
                            ps = bank((*step, j))
                            for i, h in enumerate(((0, 2, 4, 5), (7, 9, 11, 13))[j]):
                                ins = pe.transpose(ps[:, tok(i)],
                                                   AH[:, t, h:h + 2, :].rearrange("p h d -> p (h d)"), IDENT)
                            filled(ins, (*step, j))
                    elif kind in ("CT", "BT"):
                        t = step[1]
                        pe.wait_ge(*((c_roped, 2) if kind == "CT" else (b_roped, 4)))
                        ps = bank(step)
                        for i in range(4):
                            ins = pe.transpose(ps[:, tok(i)], QK[:, t, tok(i)], IDENT)
                        filled(ins, step)
                    elif kind == "idx":
                        _, t, h = step
                        if h == 0:
                            for u in range(t + 1):
                                wait_copied(pe, ("AT", u, 0))
                                wait_copied(pe, ("AT", u, 1))
                        ps = bank(step)
                        rows = slice(64 * (h % 2), 64 * (h % 2) + 64)
                        filled(pe.matmul(ps[:, 0:(t + 1) * P], AT[rows, 4 + h // 2, tok(t)],
                                         AT[rows, 3 if h % 2 else 2, 0:(t + 1) * P], start=True, stop=True), step)
                    elif kind == "att_s":
                        _, g, t, hp = step
                        if g == "C":
                            wait_copied(pe, ("CT", t))
                            if t == hp == 0:
                                wait_projected(pe, "C1")
                        for m in range(4):
                            q, k, n = map_operands(g, t, hp, m)
                            ps = bank((*step, m))
                            filled(pe.matmul(ps[:, 0:n], q, k, start=True, stop=True), (*step, m))
                    elif kind == "att_t":
                        u, m = step[1:4], step[4]
                        g, t, hp = u
                        if g == "A":
                            pe.wait_ge(probs_ready, probs_counts(u))
                        else:
                            pe.wait_ge(combined, 2 * C_UNITS.index(u) + 1 + m // 2)
                        ps = bank(step)
                        for j in range(t + 1):
                            ins = pe.transpose(ps[:, tok(j)], L[:, UNITS.index(u) % 2, m, tok(j)], IDENT)
                        filled(ins, step)
                    elif kind == "att_v":
                        u, m = step[1:4], step[4]
                        g, t, hp = u
                        wait_copied(pe, ("att_t", *step[1:]))
                        i = MAPS[g].index(m)
                        if i == 0:
                            po = bank(("att_o", *u))
                        for j in range(t + 1):
                            v = VA[:, j, :] if g == "A" else V[:, V_AT["C"], j, (2 * hp + i) * 64:(2 * hp + i + 1) * 64]
                            ins = pe.matmul(po[:, 64 * i:64 * i + 64], PT[:, PV_AT[step[1:]] % 2, j, :], v,
                                            start=j == 0, stop=j == t)
                        ins.then_inc(pt_used, 1)
                    elif kind == "dz":
                        _, h, j = step
                        if h == 0 and j == 3:
                            wait_projected(pe, "D0")
                            pe.wait_ge(signs_ready, 1)
                        rows = slice(64 * (h % 2), 64 * (h % 2) + 64)
                        ps = bank(step)
                        filled(pe.matmul(ps[:, 0:(4 - j) * P], DT[rows, 2 + h // 2, tok(j)],
                                         DT[rows, h // 2, j * P:SEQ], start=True, stop=True), step)
                    elif kind == "da":
                        _, h, j = step
                        ps = PS[TURN[("dz", h, j)][0]]
                        pe.wait_ge(softplus_split, DZ[(h, j)] + 1)
                        for i in range(j, TILES):
                            at, n = (i - j) * P, (4 - i) * P
                            for part in DS:
                                ins = pe.matmul(ps[:, at:at + n], SIGNS[:, min(i - j, 1), :],
                                                part[:, D_AT[i]:D_AT[i] + n], start=False, stop=True,
                                                skip_group_check=True)
                        ins.then_inc(d_args, 1)
                    elif kind == "dpv":
                        h = step[1]
                        pe.wait_ge(d_masked, 4 * (h + 1))
                        if h == 0:
                            wait_projected(pe, "D1")
                        ps = bank(step)
                        for i in range(TILES):
                            for j in range(i + 1):
                                a = D_AT[j] + (i - j) * P
                                ins = pe.matmul(ps[:, 64 * i:64 * i + 64], DAT[:, h % 2, a:a + P],
                                                V[:, V_AT["D"], j, 64 * h:64 * h + 64], start=j == 0, stop=j == i)
                        filled(ins, step)
                    elif kind == "bs":
                        t = step[1]
                        wait_copied(pe, ("BT", t))
                        for par in range(2):
                            ps = bank((*step, par))
                            rows = slice(64 * par, 64 * par + 64)
                            for pair in range(2):
                                ins = pe.matmul(ps[:, tok(pair)], QKT[rows, 2 + pair, tok(t)], QKT[rows, pair, tok(t)],
                                                start=True, stop=True)
                            filled(ins, (*step, par))
                    elif kind == "bkv":
                        t = step[1]
                        pe.wait_ge(ks_ready, 1)
                        if t == 0:
                            wait_projected(pe, "B1")
                        ps = bank(step)
                        for h in range(HEADS):
                            r = 64 * (h % 2)
                            ins = pe.matmul(ps[r:r + 64, 64 * h:64 * h + 64], KS[:, t, h, :],
                                            V[:, V_AT["B"], t, 64 * h:64 * h + 64], start=True, stop=True)
                        filled(ins, step)
                    elif kind == "by":
                        t = step[1]
                        wait_copied(pe, ("bs", t, 0))
                        wait_copied(pe, ("bs", t, 1))
                        if t:
                            wait_copied(pe, ("bkv", t - 1))
                        ps = bank(step)
                        for pair in range(2):
                            if t:
                                pe.matmul(ps[:, tok(pair)], QKT[:, pair, tok(t)], STATE[:, t - 1, pair, :],
                                          start=True, stop=True)
                            for h in (2 * pair, 2 * pair + 1):
                                ins = pe.matmul(ps[:, 64 * h:64 * h + 64], SD[:, t % 2, h, :],
                                                V[:, V_AT["B"], t, 64 * h:64 * h + 64], start=t == 0, stop=True,
                                                skip_group_check=t > 0)
                        filled(ins, step)
                    elif kind == "yT":
                        _, g, j = step
                        if j == 0 and g == "D":
                            for h in range(HEADS):
                                wait_copied(pe, ("dpv", h))
                        elif j == 0 and g == "A":
                            pe.wait_ge(ya_ready, TILES)
                        elif j == 0 and g == "C":
                            pe.wait_ge(yc_ready, 1)
                        elif g == "B":
                            pe.wait_ge(yb_ready, j + 1)
                        ps = bank(step)
                        y = Y_AT[g] + j * P
                        for t in range(TILES):
                            ins = pe.transpose(ps[:, tok(t)], G[:, t, y:y + P], IDENT)
                        filled(ins, step)
                pe.drain().then_inc(layer_done, 1)
                pe.wait_ge(layer_cleared, l + 1)

        @block.scalar
        def _(act):
            act.dma_start(POS_I[:, :], pos).then_inc(first_in, 16)
            act.dma_start(NG[:, :], norm_g[0]).then_inc(norm_in, 16)
            act.dma_start(SIGNS_RAW, signs).then_inc(signs_in, 16)
            for t in range(TILES):
                act.dma_start(X[:, t, 512:1024], x[tok(t), 512:1024]).then_inc(x_in[1][t], 16)
            act.dma_start(C[:, FIRST_CONSTS:], consts[:, FIRST_CONSTS:]).then_inc(const_in, 16)
            act.wait_ge(setup_dve, SETUP)
            nc.scalar.activation(SIN[:, :, :], ANG[:, :, :], ACT.Sin).then_inc(tables_ready, 1)
            nc.scalar.activation(COS[:, :, :], TURNS_[:, :, :], ACT.Sin).then_inc(tables_ready, 1)
            act.preload_act_table_set("natural_log_exp_and_others")
            with act.Fori(0, DEPTH) as l:
                link, note, settle = chain(act, act_step)

                def scaled(dst, src, t):
                    return nc.scalar.activation(dst, src, ACT.Copy, scale=RS[:, t:t + 1])

                def copy_out(key, dst, src, scale=1.0):
                    drains(nc.scalar.activation(dst, src, ACT.Copy, scale=scale), key)

                for step in SCHEDULE:
                    kind = step[0]
                    if kind == "h_stats":
                        for t in range(2):
                            for j in range(2):
                                act.wait_ge(x_in[j][t], 16)
                            nc.scalar.activation(G[:, t, :], X[:, t, :], ACT.Square, accum_out=SS[:, t:t + 1]) \
                                .then_inc(squares, 1)
                    elif kind == "rsq":
                        a, b = RSQ[step[1]]
                        act.wait_ge(var_ready, RSQ_AT[step[1]] + 1)
                        link(nc.scalar.activation(RS[:, a:b], VAR[:, a:b], ACT.Ln))
                        nc.scalar.activation(RS[:, a:b], RS[:, a:b], ACT.Exp, scale=-0.5).then_inc(rsq_guess, 1)
                    elif kind == "lam":
                        act.wait_ge(lam_sums, 2)
                        nc.scalar.activation(LAM[:, 2:4], LAM[:, 0:2], ACT.Exp).then_inc(lam_exps, 1)
                    elif kind == "split":
                        i = step[1]
                        g, k = SLICES[i]
                        if i % 2 == 0:
                            act.wait_ge(weights_in[i // 2 % RAW], (l * PER_SLOT + (i // 2 // RAW + 1)) * 16)
                        if i >= SPLIT:
                            wait_slice_used(act, i - SPLIT)
                        nc.scalar.activation(WS[0][:, i % SPLIT, 0:COLS[g]], raw(i), ACT.Copy).then_inc(w_hi_ready, 1)
                    elif kind == "xT":
                        _, j, t = step
                        wait_copied(act, step)
                        if step == ("xT", 1, 1):
                            act.dma_start(VEC[:, :], vecs[l].partition_broadcast(P)).then_inc(vecs_in, 16)
                            act.dma_start(WKV[:, :], w_kv[l]).then_inc(vecs_in, 16)
                        if step == ("xT", 1, TILES - 1):
                            act.dma_start(NG[:, :], norm_g[l + 1]).then_inc(norm_in, 16)
                        nc.scalar.activation(hT[0][:, 4 * j:4 * j + 4, tok(t)], H32[:, t % 2, :, :], ACT.Copy) \
                            .then_inc(h_hi_ready, 1)
                    elif kind == "slice" and SLICES[step[1]][1] == KT - 1:
                        name = NAMES[SLICES[step[1]][0]]
                        if name[0] == "O" or name == "D0":
                            continue
                        if name == "A0":
                            act.wait_ge(h_rs_ready, 1)
                        if name == "C1":
                            act.wait_ge(signs_ready, 1)
                        if name == "D1":
                            wait_projected(act, "D0")
                        if name == "B0":
                            wait_filled(act, ("CT", TILES - 1))
                        if name == "B1":
                            act.wait_ge(pt_used, 2 * len(C_UNITS))
                        for t in range(TILES):
                            key = ("proj", name, t)
                            ps = wait_filled(act, key)
                            if name == "A0":
                                note(scaled(AH[:, t, 0:5, :].rearrange("p h d -> p (h d)"), ps[:, 0:320], t))
                                drains(scaled(CW[:, t, :], ps[:, 320:456], t), key)
                            elif name == "A2":
                                drains(scaled(AH[:, t, 7:15, :].rearrange("p h d -> p (h d)"), ps[:, :], t), key)
                            elif name in ("C0", "B0"):
                                drains(scaled(QK[:, t, :], ps[:, :], t), key)
                            elif name == "A3":
                                drains(scaled(G[:, t, 0:256], ps[:, 0:256], t), key)
                            else:
                                note(scaled(V[:, V_AT[name[0]], t, :], ps[:, 0:256], t))
                                y = Y_AT[name[0]]
                                drains(scaled(G[:, t, y:y + 256], ps[:, 256:512], t), key)
                    elif kind == "a_sq":
                        wait_projected(act, "A0")
                        settle()
                        note(nc.scalar.activation(SQ[:, 0:1280].rearrange("p (t h d) -> p t h d", t=TILES, h=5),
                                                  head_view(0, 5), ACT.Square))
                        nc.scalar.activation(SQ[:, 1280:1792].rearrange("p (t n) -> p t n", t=TILES),
                                             CW[:, :, 0:KV_RANK], ACT.Square).then_inc(squares, 1)
                    elif kind == "ckvT":
                        wait_h_split(act, 1, 2)
                        wait_h_split(act, 1, 3)
                        ps = wait_filled(act, step)
                        copy_out(step, CKT[:, :, :], ps[:, :].rearrange("p (t n) -> p t n", t=TILES))
                    elif kind == "kv_up":
                        ps = wait_filled(act, step)
                        kv = ps[:, :].rearrange("p (t n) -> p t n", t=TILES)
                        note(nc.scalar.activation(VA[:, :, :], kv[:, :, 64:128], ACT.Copy))
                        copy_out(step, AH[:, :, 5, :], kv[:, :, 0:64])
                        wait_copied(act, step)
                        act.wait_ge(var_ready, RSQ_AT["a"] + 1)
                        nc.scalar.activation(SQ[:, 0:256].rearrange("p (t n) -> p t n", t=TILES), AH[:, :, 5, :],
                                             ACT.Square).then_inc(squares, 1)
                    elif kind == "AT":
                        ps = wait_filled(act, (*step, 0))
                        copy_out((*step, 0), AT[:, 0:4, tok(step[1])], ps[:, :].rearrange("p (s n) -> p s n", s=4))
                    elif kind in ("CT", "BT"):
                        if kind == "BT" and step[1] == 0:
                            wait_filled(act, ("att_s", "C", TILES - 1, 1, 3))
                            wait_filled(act, ("att_s", "C", TILES - 1, 1, 2))
                        ps = wait_filled(act, step)
                        copy_out(step, QKT[:, :, tok(step[1])], ps[:, :].rearrange("p (s n) -> p s n", s=4))
                    elif kind == "idx":
                        i = IDX.index(step)
                        ps = wait_filled(act, step)
                        if i >= 2:
                            act.wait_ge(idx_added, i - 1)
                        n = (step[1] + 1) * P
                        drains(nc.scalar.activation(R[:, i % 2, 0:n], ps[:, 0:n], ACT.Relu), step)
                    elif kind == "c_sq":
                        wait_projected(act, "C0")
                        act.wait_ge(var_ready, RSQ_AT["k"] + 1)
                        nc.scalar.activation(SQ[:, :], QK[:, :, :].rearrange("p t n -> p (t n)"), ACT.Square) \
                            .then_inc(squares, 1)
                    elif kind == "att_e":
                        u = step[1:]
                        g, t, hp = u
                        i = UNITS.index(u)
                        n = (t + 1) * P
                        scale = (HEAD if g == "A" else DIFF_HALF) ** -0.5
                        act.wait_ge(max_ready, i + 1)
                        for m in range(4):
                            nc.scalar.activation(L[:, i % 2, m, 0:n], L[:, i % 2, m, 0:n], ACT.Exp,
                                                 bias=NM[:, i % 2, m:m + 1], scale=scale,
                                                 accum_out=SUM[:, i % 2, m:m + 1]).then_inc(probs_ready, 1)
                    elif kind == "att_t":
                        pt = PT_AT[step[1:]]
                        ps = wait_filled(act, step)
                        if pt >= 2:
                            act.wait_ge(pt_used, pt - 1)
                        n = (step[2] + 1) * P
                        copy_out(step, PT[:, pt % 2, :, :].rearrange("p j n -> p (j n)")[:, 0:n], ps[:, 0:n])
                    elif kind == "gate":
                        y = Y_AT[step[1]]
                        i = GATES.index(step[1])
                        act.wait_ge(gate_clamped, i + 1)
                        ge = GE[step[1]]
                        link(nc.scalar.activation(ge, ge, ACT.Exp, scale=-1.0))
                        link(nc.scalar.activation(ge, ge, ACT.Ln, bias=1.0))
                        nc.scalar.activation(ge, ge, ACT.Exp, scale=-1.0).then_inc(sigmoid_ready, 1)
                    elif kind == "y_sq":
                        for u in C_UNITS:
                            wait_copied(act, ("att_o", *u))
                        act.wait_ge(gate_ready, GATES.index("D") + 1)
                        nc.scalar.activation(SQY[:, :, :], YC[:, :, :], ACT.Square).then_inc(squares, 1)
                    elif kind == "b_sq":
                        act.wait_ge(centred, TILES)
                        nc.scalar.activation(SQY[:, :, :], YB[:, :, :], ACT.Square).then_inc(squares, 1)
                    elif kind == "dz":
                        _, h, j = step
                        a = DAT[:, h % 2, D_AT[j]:D_AT[j] + (4 - j) * P]
                        ps = wait_filled(act, step)
                        if h == 0 and j == 3:
                            wait_filled(act, ("AT", TILES - 1, 1))
                        if h >= 2 and j == 3:
                            wait_filled(act, ('dpv', h - 2))
                        link(nc.scalar.activation(a, ps[:, 0:(4 - j) * P], ACT.Abs))
                        link(nc.scalar.activation(a, a, ACT.Exp, scale=-1.0))
                        nc.scalar.activation(a, a, ACT.Ln, bias=1.0).then_inc(softplus_log, 1)
                    elif kind == "da":
                        _, h, j = step
                        act.wait_ge(d_args, DA[(h, j)] + 1)
                        act.wait_ge(softplus_ready, DZ[(h, j)] + 1)
                        drains(nc.scalar.activation(DAT[:, h % 2, D_AT[j]:D_AT[j] + (4 - j) * P],
                                                    PS[TURN[("dz", h, j)][0]][:, 0:(4 - j) * P], ACT.Exp),
                               ("dz", h, j))
                    elif kind == "yT":
                        _, g, j = step
                        if (g, j) == (OUT_ORDER[0], 0):
                            wait_filled(act, ("proj", "B1", TILES - 1))
                        ps = wait_filled(act, step)
                        nc.scalar.activation(hT[0][:, 2 * OUT_ORDER.index(g) + j, :], ps[:, :], ACT.Copy) \
                            .then_inc(h_hi_ready, 1)
                act.drain().then_inc(layer_done, 1)
                act.wait_ge(layer_cleared, l + 1)
            act.wait_ge(norm_in, 16 * (DEPTH + 1))

        @block.vector
        def _(dve):
            v = nc.vector
            link, note, settle = chain(dve, setup_dve)
            two_pi = 2.0 * math.pi
            c1 = 6.28125
            c2 = float(np.float32(round((two_pi - c1) * 2 ** 20) / 2 ** 20))
            c3 = two_pi - c1 - c2
            pi = 3.1415925
            magic = 1.5 * 2 ** 23
            dve.wait_ge(first_in, 32)
            link(v.tensor_copy(POS[:, :], POS_I[:, :]))
            link(v.tensor_tensor(ANG[:, :, :], POS[:, :].unsqueeze(2).broadcast_to([P, TILES, FREQS]),
                                 const("freq").unsqueeze(1).broadcast_to([P, TILES, FREQS]), ALU.mult))
            link(v.tensor_scalar(TURNS_[:, :, :], ANG[:, :, :], 1.0 / two_pi, magic, ALU.mult, ALU.add))
            link(v.tensor_scalar(TURNS_[:, :, :], TURNS_[:, :, :], magic, None, ALU.subtract))
            for c in (c1, c2, c3):
                link(v.scalar_tensor_tensor(ANG[:, :, :], TURNS_[:, :, :], -c, ANG[:, :, :], ALU.mult, ALU.add))
            link(v.tensor_scalar(COS[:, :, :], ANG[:, :, :], pi / 2, -two_pi, ALU.is_gt, ALU.mult))
            link(v.scalar_tensor_tensor(TURNS_[:, :, :], ANG[:, :, :], math.pi / 2, COS[:, :, :], ALU.add, ALU.add))
            link(v.tensor_scalar(TURNS_[:, :, :], TURNS_[:, :, :], pi, -pi, ALU.min, ALU.max))
            note(v.tensor_scalar(ANG[:, :, :], ANG[:, :, :], pi, -pi, ALU.min, ALU.max))

            with dve.Fori(0, DEPTH) as l:
                link, note, settle = chain(dve, dve_step)

                def reduce_groups(use, src, lo, hi, n):
                    a = RSQ[use][0]
                    link(v.tensor_reduce(SS[:, a + lo:a + hi], src, op=ALU.add, axis=AX))
                    return v.tensor_scalar(VAR[:, a + lo:a + hi], SS[:, a + lo:a + hi], 1.0 / n, EPS, ALU.mult, ALU.add)

                def newton(use, done=None):
                    a, b = RSQ[use]
                    dve.wait_ge(rsq_guess, RSQ_AT[use] + 1)
                    link(v.tensor_tensor(NEWT[:, a:b], RS[:, a:b], RS[:, a:b], ALU.mult))
                    link(v.tensor_tensor(NEWT[:, a:b], NEWT[:, a:b], VAR[:, a:b], ALU.mult))
                    link(v.tensor_scalar(NEWT[:, a:b], NEWT[:, a:b], -0.5, 1.5, ALU.mult, ALU.add))
                    last = v.tensor_tensor(RS[:, a:b], RS[:, a:b], NEWT[:, a:b], ALU.mult)
                    last.then_inc(done, 1) if done is not None else link(last)

                def rs(use, lo=0, hi=None):
                    a, b = RSQ[use]
                    return RS[:, a + lo:(b if hi is None else a + hi)]

                def rope(x1, x2, rot, heads, done, tiles=slice(0, TILES)):
                    f = rot.stop - rot.start
                    rows = tiles.stop - tiles.start
                    n = rows * heads * f

                    def scratch(i):
                        return T[:, i, 0:n].rearrange("p (t h f) -> p t h f", t=rows, h=heads)

                    cos = COS[:, tiles, rot].unsqueeze(2).broadcast_to([P, rows, heads, f])
                    sin = SIN[:, tiles, rot].unsqueeze(2).broadcast_to([P, rows, heads, f])
                    settle()
                    note(v.tensor_tensor(scratch(0), x1, sin, ALU.mult))
                    link(v.tensor_tensor(scratch(1), x2, sin, ALU.mult))
                    note(v.tensor_tensor(x1, x1, cos, ALU.mult))
                    link(v.tensor_tensor(x2, x2, cos, ALU.mult))
                    note(v.tensor_tensor(x1, x1, scratch(1), ALU.subtract))
                    v.tensor_tensor(x2, x2, scratch(0), ALU.add).then_inc(*done)

                for step in SCHEDULE:
                    kind = step[0]
                    if kind == "h_stats":
                        for t in range(2, TILES):
                            for j in range(2):
                                dve.wait_ge(x_in[j][t], 16)
                            link(v.tensor_tensor_reduce(out=G[:, t, :], in0=X[:, t, :], in1=X[:, t, :], scale=1.0,
                                                        scalar=0.0, op0=ALU.mult, op1=ALU.add,
                                                        accum_out=SS[:, t:t + 1]))
                        dve.wait_ge(squares, 2)
                        v.tensor_scalar(VAR[:, 0:4], SS[:, 0:4], 1.0 / D_MODEL, EPS, ALU.mult, ALU.add) \
                            .then_inc(var_ready, 1)
                    elif kind == "h_rs":
                        newton("h", h_rs_ready)
                    elif kind == "rs_row":
                        ps = wait_filled(dve, step)
                        drains(v.tensor_copy(RSB[:, :], ps[:, :]), step)
                    elif kind == "lam":
                        dve.wait_ge(const_in, 16)
                        dve.wait_ge(vecs_in, 32)
                        for i in range(2):
                            v.tensor_tensor_reduce(out=YT[:, 32 * i:32 * i + 32], in0=vec(f"lam_q{i + 1}"),
                                                   in1=vec(f"lam_k{i + 1}"), scale=1.0, scalar=0.0, op0=ALU.mult,
                                                   op1=ALU.add, accum_out=LAM[:, i:i + 1]).then_inc(lam_sums, 1)
                        note(v.tensor_scalar(SG[:, :], vec("subln_g"), vec("one_minus"), None, ALU.mult))
                    elif kind == "xT":
                        _, j, t = step
                        dve.wait_ge(norm_in, l * 16 + 16)
                        ps = wait_filled(dve, step)
                        if j or t >= 2:
                            wait_h_split(dve, *((j, t - 2) if t >= 2 else (0, t + 2)))
                        drains(v.tensor_tensor(H32[:, t % 2, :, :], ps[:, :].rearrange("p (s n) -> p s n", s=4),
                                               NG[:, 4 * j:4 * j + 4].unsqueeze(2).broadcast_to([P, 4, P]),
                                               ALU.mult), step)
                        if t % 2:
                            dve.wait_ge(h_hi_ready, TILES * j + t)
                            v.tensor_tensor(hT[1][:, 4 * j:4 * j + 4, tok(t - 1)], H32[:, 0, :, :],
                                            hT[0][:, 4 * j:4 * j + 4, tok(t - 1)].bitcast(f32), ALU.subtract) \
                                .then_inc(h_lo_dve, 1)
                    elif kind == "a_sq":
                        dve.wait_ge(squares, 3)
                        note(reduce_groups("a", SQ[:, 0:1280].rearrange("p (g d) -> p g d", d=HEAD), 0, 20, HEAD))
                        reduce_groups("a", SQ[:, 1280:1792].rearrange("p (g d) -> p g d", d=KV_RANK), 20, 24,
                                      KV_RANK).then_inc(var_ready, 1)
                    elif kind == "a_norm":
                        newton("a")
                        ckv = CW[:, :, 0:KV_RANK]
                        link(v.tensor_tensor(ckv, ckv, rs("a", 20, 24).unsqueeze(2).broadcast_to([P, TILES, KV_RANK]),
                                             ALU.mult))
                        v.tensor_tensor(ckv, ckv, vec("kv_norm_g").unsqueeze(1).broadcast_to([P, TILES, KV_RANK]),
                                        ALU.mult).then_inc(cn_ready, 1)
                        link(v.tensor_tensor(head_view(0, 5), head_view(0, 5),
                                             rs("a", 0, 20).rearrange("p (t h) -> p t h", t=TILES).unsqueeze(3)
                                             .broadcast_to([P, TILES, 5, HEAD]), ALU.mult))
                        note(v.tensor_tensor(head_view(0, 4), head_view(0, 4),
                                             vec("q_norm_a").unsqueeze(1).unsqueeze(1)
                                             .broadcast_to([P, TILES, 4, HEAD]), ALU.mult))
                        note(v.tensor_scalar(CW[:, :, KV_RANK:], CW[:, :, KV_RANK:], (IDX_HEADS * HEAD) ** -0.5, None,
                                             ALU.mult))
                    elif kind == "kv_up":
                        dve.wait_ge(squares, 4)
                        reduce_groups("k", SQ[:, 0:256].rearrange("p (g d) -> p g d", d=HEAD), 0, 4, HEAD) \
                            .then_inc(var_ready, 1)
                    elif kind == "k_norm":
                        newton("k")
                        k = AH[:, :, 5, :]
                        link(v.tensor_tensor(k, k, rs("k").unsqueeze(2).broadcast_to([P, TILES, HEAD]), ALU.mult))
                        note(v.tensor_tensor(k, k, vec("k_norm_a").unsqueeze(1).broadcast_to([P, TILES, HEAD]), ALU.mult))
                    elif kind == "qi_rope":
                        wait_projected(dve, "A2")
                        dve.wait_ge(tables_ready, 2)
                        rope(AH[:, :, 7:15, 0:8], AH[:, :, 7:15, 8:16], ROT_A, 8, (a_roped, 1))
                    elif kind == "a_rope":
                        dve.wait_ge(a_roped, 1)
                        rope(AH[:, :, 0:6, 0:8], AH[:, :, 0:6, 8:16], ROT_A, 6, (a_roped, 1))
                        dve.wait_ge(a_roped, 2)
                        v.tensor_copy(AH[:, :, 6, :], AH[:, :, 4, :]).then_inc(a_roped, 1)
                    elif kind == "c_rope":
                        tiles = slice(2 * step[1], 2 * step[1] + 2)
                        q = QK[:, tiles, :].rearrange("p t (g d) -> p t g d", d=DIFF_HALF)
                        dve.wait_ge(*((c_roped, 1) if step[1] else (a_roped, 2)))
                        rope(q[:, :, :, 0:4], q[:, :, :, 4:8], ROT_C, 16, (c_roped, 1), tiles)
                    elif kind == "b_rope":
                        i, tiles = step[1] // 2, slice(2 * (step[1] % 2), 2 * (step[1] % 2) + 2)
                        if step[1] == 0:
                            wait_projected(dve, "B0")
                            dve.wait_ge(var_ready, RSQ_AT["y"] + 1)
                        else:
                            dve.wait_ge(b_roped, step[1])
                        q = QK[:, tiles, 256 * i:256 * i + 256].rearrange("p t (h d) -> p t h d", d=HEAD)
                        rope(q[:, :, :, 0:32], q[:, :, :, 32:64], ROT_B, HEADS, (b_roped, 1), tiles)
                    elif kind == "ks":
                        dve.wait_ge(b_roped, 4)
                        for t in range(TILES):
                            ins = v.tensor_tensor(KS[:, t, :, :], QK[:, t, 256:512].rearrange("p (h d) -> p h d", d=HEAD),
                                                  const("k_decay").unsqueeze(2).broadcast_to([P, HEADS, HEAD]), ALU.mult)
                            (note(ins) if t < TILES - 1 else ins.then_inc(ks_ready, 1))
                    elif kind == "c_sq":
                        dve.wait_ge(squares, 5)
                        reduce_groups("c", SQ[:, :].rearrange("p (g d) -> p g d", d=DIFF_HALF), 0, 64, DIFF_HALF) \
                            .then_inc(var_ready, 1)
                    elif kind == "c_norm":
                        half = step[1]
                        tiles = slice(2 * half, 2 * half + 2)
                        if half == 0:
                            newton("c")
                        q = QK[:, tiles, :].rearrange("p t n -> p (t n)").rearrange("p (g d) -> p g d", d=DIFF_HALF)
                        link(v.tensor_tensor(q, q, rs("c", 32 * half, 32 * half + 32).unsqueeze(2)
                                             .broadcast_to([P, 32, DIFF_HALF]), ALU.mult))
                        for i, name in enumerate(("q_norm_c", "k_norm_c")):
                            q = QK[:, tiles, 256 * i:256 * i + 256].rearrange("p t (g d) -> p t g d", d=DIFF_HALF)
                            note(v.tensor_tensor(q, q, vec(name).unsqueeze(1).unsqueeze(1)
                                                 .broadcast_to([P, 2, 8, DIFF_HALF]), ALU.mult))
                    elif kind == "AT":
                        ps = wait_filled(dve, (*step, 1))
                        drains(v.tensor_copy(AT[:, 4:8, tok(step[1])], ps[:, :].rearrange("p (s n) -> p s n", s=4)),
                               (*step, 1))
                    elif kind == "idx":
                        _, t, h = step
                        i = IDX.index(step)
                        n = (t + 1) * P
                        s = WORK[:, WORK_AT[t]:WORK_AT[t] + n]
                        wait_copied(dve, step)
                        w_h = CW[:, t, KV_RANK + h:KV_RANK + h + 1]
                        if h == 0:
                            settle()
                            v.tensor_scalar(s, R[:, i % 2, 0:n], w_h, None, ALU.mult).then_inc(idx_added, 1)
                        else:
                            dve.wait_ge(idx_added, i)
                            v.scalar_tensor_tensor(s, R[:, i % 2, 0:n], w_h, s, ALU.mult, ALU.add) \
                                .then_inc(idx_added, 1)
                        if h == IDX_HEADS - 1:
                            dve.wait_ge(idx_added, i + 1)
                            a = WORK_AT[t] + n - CHUNK
                            link(v.memset(WORK[0:CHUNK, a:a + CHUNK], INVALID))
                    elif kind == "top":
                        _, t, r = step
                        s = WORK[:, WORK_AT[t]:WORK_AT[t] + (t + 1) * P]
                        link(v.max(M8[:, :], s))
                        link(v.match_replace(s, M8[:, :], s, TAKEN))
                        if r == TOPK // 8 - 1:
                            link(v.tensor_scalar(s, s, TAKEN, MASKED, ALU.not_equal, ALU.mult))
                    elif kind == "att_s":
                        u = step[1:]
                        g, t, hp = u
                        i = UNITS.index(u)
                        lb = i % 2
                        n = (t + 1) * P
                        scale = (HEAD if g == "A" else DIFF_HALF) ** -0.5
                        if i >= 2:
                            for m in MAPS[UNITS[i - 2][0]][-2:]:
                                wait_filled(dve, ("att_t", *UNITS[i - 2], m))
                        bias = WORK[:, WORK_AT[t]:WORK_AT[t] + n] if g == "A" and t else const("chunk_bias")[:, SEQ - n:]
                        for m in range(4):
                            ps = wait_filled(dve, (*step, m))
                            drains(v.tensor_tensor_reduce(out=L[:, lb, m, 0:n], in0=ps[:, 0:n], in1=bias, scale=1.0,
                                                          scalar=-3.0e38, op0=ALU.add, op1=ALU.max,
                                                          accum_out=MX[:, lb, m:m + 1]), (*step, m))
                        wait_copied(dve, (*step, 2))
                        wait_copied(dve, (*step, 3))
                        v.tensor_scalar(NM[:, lb, :], MX[:, lb, :], -scale, None, ALU.mult).then_inc(max_ready, 1)
                    elif kind == "att_c":
                        u = step[1:]
                        g, t, hp = u
                        lb = UNITS.index(u) % 2
                        n = (t + 1) * P
                        dve.wait_ge(probs_ready, probs_counts(u))
                        link(v.reciprocal(RINV[:, lb, :], SUM[:, lb, :]))
                        if g == "C":
                            dve.wait_ge(lam_exps, 1)
                            if u == ("C", 0, 0):
                                link(v.tensor_tensor(LAM[:, 4:5], LAM[:, 3:4], LAM[:, 2:3], ALU.subtract))
                                link(v.tensor_tensor(LAM[:, 5:6], LAM[:, 4:5], vec("lam_init"), ALU.subtract))
                            link(v.tensor_tensor(RHO[:, lb, :], SUM[:, lb, 0::2], RINV[:, lb, 1::2], ALU.mult))
                            link(v.tensor_scalar(RHO[:, lb, :], RHO[:, lb, :], LAM[:, 5:6], None, ALU.mult))
                            for i in range(2):
                                v.scalar_tensor_tensor(L[:, lb, 2 * i, 0:n], L[:, lb, 2 * i + 1, 0:n],
                                                       RHO[:, lb, i:i + 1], L[:, lb, 2 * i, 0:n], ALU.mult,
                                                       ALU.add).then_inc(combined, 1)
                    elif kind == "att_v" and step[-1] == MAPS[step[1]][-1]:
                        u = step[1:4]
                        g, t, hp = u
                        lb = UNITS.index(u) % 2
                        out_key = ("att_o", *u)
                        po = PS[TURN[out_key][0]]
                        dve.wait_ge(pt_used, PV_AT[step[1:]] + 1)
                        if g == "C":
                            drains(v.tensor_tensor(YC[:, t, 128 * hp:128 * hp + 128].rearrange("p (h d) -> p h d", h=2),
                                                   po[:, 0:128].rearrange("p (h d) -> p h d", h=2),
                                                   RINV[:, lb, 0::2].unsqueeze(2).broadcast_to([P, 2, HEAD]), ALU.mult),
                                   out_key)
                        else:
                            drains(v.tensor_tensor(YT[:, :].rearrange("p (h d) -> p h d", h=4),
                                                   po[:, 0:256].rearrange("p (h d) -> p h d", h=4),
                                                   RINV[:, lb, :].unsqueeze(2).broadcast_to([P, 4, HEAD]), ALU.mult),
                                   out_key)
                            wait_copied(dve, out_key)
                            dve.wait_ge(gate_ready, GATES.index("A") + 1)
                            v.tensor_tensor(G[:, t, 0:256], G[:, t, 0:256], YT[:, :], ALU.mult).then_inc(ya_ready, 1)
                    elif kind == "gate":
                        y = Y_AT[step[1]]
                        i = GATES.index(step[1])
                        wait_projected(dve, {"A": "A3", "B": "B1", "C": "C1", "D": "D1"}[step[1]])
                        if i:
                            dve.wait_ge(gate_ready, i)
                        if step[1] == "C":
                            dve.wait_ge(c_roped, 2)
                        elif step[1] == "B":
                            for m in (2, 3):
                                wait_filled(dve, ("att_t", "A", TILES - 1, 0, m))
                        v.tensor_scalar(GE[step[1]], G[:, :, y:y + 256], -44.0, None, ALU.max).then_inc(gate_clamped, 1)
                    elif kind == "y_sq":
                        dve.wait_ge(squares, 6)
                        reduce_groups("y", SQY_HEADS, 0, 16, HEAD) \
                            .then_inc(var_ready, 1)
                    elif kind == "c_post":
                        newton("y")
                        y = YC.rearrange("p t (h d) -> p t h d", h=HEADS)
                        link(v.tensor_tensor(y, y, rs("y").rearrange("p (t h) -> p t h", t=TILES).unsqueeze(3)
                                             .broadcast_to([P, TILES, HEADS, HEAD]), ALU.mult))
                        v.tensor_tensor(y, y, SG[:, :].unsqueeze(1).unsqueeze(1)
                                        .broadcast_to([P, TILES, HEADS, HEAD]), ALU.mult).then_inc(yc_normed, 1)
                    elif kind == "dz":
                        _, h, j = step
                        n = (4 - j) * P
                        dve.wait_ge(softplus_log, DZ[(h, j)] + 1)
                        if h and j == 3:
                            dve.wait_ge(d_args, 4 * h)
                        if h == 0 and j == 3:
                            dve.wait_ge(idx_added, len(IDX))
                        v.scalar_tensor_tensor(DL[:, D_AT[j]:D_AT[j] + n], PS[TURN[step][0]][:, 0:n], 0.0,
                                               DAT[:, h % 2, D_AT[j]:D_AT[j] + n], ALU.max, ALU.add) \
                            .then_inc(softplus_ready, 1)
                    elif kind == "dlo":
                        _, h, j = step
                        n = (4 - j) * P
                        dve.wait_ge(softplus_hi, DZ[(h, j)] + 1)
                        v.tensor_tensor(DS[1][:, D_AT[j]:D_AT[j] + n], DL[:, D_AT[j]:D_AT[j] + n],
                                        DS[0][:, D_AT[j]:D_AT[j] + n].bitcast(f32), ALU.subtract) \
                            .then_inc(softplus_split, 1)
                    elif kind == "dpv":
                        h = step[1]
                        y = Y_AT["D"] + 64 * h
                        ps = wait_filled(dve, step)
                        dve.wait_ge(gate_ready, GATES.index("D") + 1)
                        drains(v.tensor_tensor(G[:, :, y:y + 64], ps[:, 0:256].rearrange("p (t d) -> p t d", t=TILES),
                                               G[:, :, y:y + 64], ALU.mult), step)
                    elif kind == "bs":
                        t = step[1]
                        if t == 0:
                            dve.wait_ge(d_args, 16)
                        if t >= 2:
                            wait_filled(dve, ("by", t - 2))
                        for par in range(2):
                            ps = wait_filled(dve, (*step, par))
                            drains(v.tensor_tensor(SD[:, t % 2, par::2, :],
                                                   ps[:, 0:256].rearrange("p (h q) -> p h q", h=2),
                                                   const("decay").rearrange("p (h q) -> p h q", h=HEADS)[:, par::2, :],
                                                   ALU.mult), (*step, par))
                    elif kind == "bkv":
                        t = step[1]
                        ps = wait_filled(dve, step)
                        a = CONSTS["state_decay"][0]
                        if t == 0:
                            dve.wait_ge(states_zeroed, 1)
                        else:
                            wait_copied(dve, ("bkv", t - 1))
                        for h in range(HEADS):
                            rows = slice(64 * (h % 2), 64 * (h % 2) + 64)
                            kv = ps[rows, 64 * h:64 * h + 64]
                            new = STATE[rows, t, h // 2, rows]
                            if t == 0:
                                ins = v.tensor_copy(new, kv)
                            else:
                                ins = v.scalar_tensor_tensor(new, STATE[rows, t - 1, h // 2, rows],
                                                             C[rows, a + h // 2:a + h // 2 + 1], kv, ALU.mult, ALU.add)
                            (note(ins) if h < HEADS - 1 else drains(ins, step))
                    elif kind == "by":
                        t = step[1]
                        ps = wait_filled(dve, step)
                        if t == 0:
                            dve.wait_ge(ks_ready, 1)
                            wait_filled(dve, ("BT", TILES - 1))
                        drains(v.tensor_tensor(YB[:, t, :].rearrange("p (h d) -> p h d", h=HEADS),
                                               ps[:, 0:256].rearrange("p (h d) -> p h d", h=HEADS),
                                               const("q_decay").unsqueeze(2).broadcast_to([P, HEADS, HEAD]), ALU.mult),
                               step)
                    elif kind == "b_mu":
                        t = step[1]
                        y = YB[:, t, :].rearrange("p (h d) -> p h d", h=HEADS)
                        mu = MU[:, 4 * t:4 * t + 4]
                        wait_copied(dve, ("by", t))
                        link(v.tensor_reduce(mu, y, op=ALU.add, axis=AX))
                        link(v.tensor_scalar(mu, mu, 1.0 / HEAD, None, ALU.mult))
                        v.tensor_tensor(y, y, mu.unsqueeze(2).broadcast_to([P, HEADS, HEAD]), ALU.subtract) \
                            .then_inc(centred, 1)
                    elif kind == "b_sq":
                        dve.wait_ge(squares, 7)
                        reduce_groups("b", SQY_HEADS, 0, 16, HEAD) \
                            .then_inc(var_ready, 1)
                    elif kind == "b_post":
                        newton("b")
                        dve.wait_ge(gains_ready, 1)
                        for j in range(2):
                            y = YB[:, :, j * P:(j + 1) * P].rearrange("p t (h d) -> p t h d", h=2)
                            link(v.tensor_tensor(y, y, rs("b").rearrange("p (t h) -> p t h", t=TILES)[:, :, 2 * j:2 * j + 2]
                                                 .unsqueeze(3).broadcast_to([P, TILES, 2, HEAD]), ALU.mult))
                            g = G[:, :, Y_AT["B"] + j * P:Y_AT["B"] + (j + 1) * P]
                            v.tensor_tensor(g, g, YB[:, :, j * P:(j + 1) * P], ALU.mult).then_inc(yb_ready, 1)
                    elif kind == "yT":
                        k = 2 * OUT_ORDER.index(step[1]) + step[2]
                        ps = wait_filled(dve, step)
                        dve.wait_ge(h_hi_ready, 2 * TILES + k + 1)
                        drains(v.tensor_tensor(hT[1][:, k, :], ps[:, :], hT[0][:, k, :].bitcast(f32), ALU.subtract), step)
                    elif kind == "slice" and SLICES[step[1]][1] == KT - 1:
                        name = NAMES[SLICES[step[1]][0]]
                        if name == "D0":
                            wait_copied(dve, IDX[-1])
                            wait_copied(dve, ("rs_row",))
                            for t in range(TILES):
                                ps = wait_filled(dve, ("proj", name, t))
                                drains(v.scalar_tensor_tensor(DT[:, t, :], ps[:, :], HEAD ** -0.5 if t < 2 else 1.0,
                                                              RSB[:, :], ALU.mult, ALU.mult), ("proj", name, t))
                        for t in range(TILES) if name[0] == "O" else ():
                            half = X[:, t, 512 * int(name[1]):512 * int(name[1]) + 512]
                            ps = wait_filled(dve, ("proj", name, t))
                            drains(v.tensor_tensor(half, ps[:, :], half, ALU.add), ("proj", name, t))
                            wait_copied(dve, ("proj", name, t))
                            dve.sem_inc(x_added, 1)
                dve.drain().then_inc(layer_done, 1)
                dve.wait_ge(layer_cleared, l + 1)

        @block.gpsimd
        def _(pool):
            p = nc.gpsimd
            pool.wait_ge(signs_in, 16)
            p.tensor_copy(SIGNS[:, :, :], SIGNS_RAW.rearrange("p (a n) -> p a n", a=2)).then_inc(signs_ready, 1)
            with pool.Fori(0, DEPTH) as l:
                for step in SCHEDULE:
                    kind = step[0]
                    if kind == "split":
                        i = step[1]
                        n = COLS[SLICES[i][0]]
                        pool.wait_ge(w_hi_ready, i + 1)
                        p.tensor_tensor(WS[1][:, i % SPLIT, 0:n], raw(i), WS[0][:, i % SPLIT, 0:n].bitcast(f32),
                                        ALU.subtract).then_inc(w_lo_ready, 1)
                    elif kind == "xT":
                        _, j, t = step
                        if t % 2:
                            pool.wait_ge(h_hi_ready, TILES * j + t + 1)
                            p.tensor_tensor(hT[1][:, 4 * j:4 * j + 4, tok(t)], H32[:, 1, :, :],
                                            hT[0][:, 4 * j:4 * j + 4, tok(t)].bitcast(f32), ALU.subtract) \
                                .then_inc(h_lo_pool, 1)
                    elif kind == "gated":
                        y = Y_AT[step[1]]
                        pool.wait_ge(sigmoid_ready, GATES.index(step[1]) + 1)
                        p.tensor_tensor(G[:, :, y:y + 256], G[:, :, y:y + 256], GE[step[1]], ALU.mult) \
                            .then_inc(gate_ready, 1)
                    elif step == ("bkv", 0):
                        wait_filled(pool, ("BT", TILES - 1))
                        pool.wait_ge(ks_ready, 1)
                        p.memset(STATE[:, :, :, :], 0.0).then_inc(states_zeroed, 1)
                    elif kind == "c_post":
                        y = Y_AT["C"]
                        pool.wait_ge(yc_normed, 1)
                        pool.wait_ge(gate_ready, GATES.index("C") + 1)
                        p.tensor_tensor(G[:, :, y:y + 256], G[:, :, y:y + 256], YC[:, :, :], ALU.mult) \
                            .then_inc(yc_ready, 1)
                    elif kind == "gains":
                        y = Y_AT["B"]
                        pool.wait_ge(gate_ready, GATES.index("B") + 1)
                        p.tensor_tensor(G[:, :, y:y + 256], G[:, :, y:y + 256],
                                        vec("ret_norm_g").unsqueeze(1).broadcast_to([P, TILES, WIDTH]), ALU.mult) \
                            .then_inc(gains_ready, 1)
                    elif kind == "dz":
                        _, h, j = step
                        pool.wait_ge(softplus_ready, DZ[(h, j)] + 1)
                        d = DL[:, D_AT[j]:D_AT[j] + P]
                        p.affine_select(out=d, in_=d, compare_op=ALU.is_gt, fill=0.0, base=0, pattern=[[1, P]],
                                        channel_multiplier=-1).then_inc(softplus_masked, 1)
                        pool.wait_ge(softplus_masked, DZ[(h, j)] + 1)
                        n = (4 - j) * P
                        p.tensor_copy(DS[0][:, D_AT[j]:D_AT[j] + n], DL[:, D_AT[j]:D_AT[j] + n]) \
                            .then_inc(softplus_hi, 1)
                    elif kind == "da":
                        _, h, j = step
                        wait_copied(pool, ("dz", h, j))
                        d = DAT[:, h % 2, D_AT[j]:D_AT[j] + P]
                        p.affine_select(out=d, in_=d, compare_op=ALU.is_gt, fill=0.0, base=0, pattern=[[1, P]],
                                        channel_multiplier=-1).then_inc(d_masked, 1)
                pool.drain().then_inc(layer_done, 1)
                pool.wait_ge(layer_done, l * 4 + 4)
                pool.sem_inc(layer_over, 1)
                pool.sem_clear(in_layer)
                pool.sem_inc(layer_cleared, 1)


def constants():
    i = np.arange(P, dtype=np.float64)
    c = np.zeros((P, N_CONST), np.float64)

    def put(name, a):
        lo, hi = CONSTS[name]
        c[:, lo:hi] = np.asarray(a).reshape(P, hi - lo)

    log_gamma = np.log1p(-(2.0 ** (-5.0 - np.arange(HEADS))))
    put("ident", np.eye(P))
    seen = ~((i[None, :] < CHUNK) & (i[:, None] >= CHUNK))
    dist = np.abs(i[:, None] - i[None, :]) - (i[None, :] + 1)
    put("decay", np.stack([np.exp(g * dist) * seen * HEAD ** -0.5 for g in log_gamma], 1))
    bias = np.zeros((P, SEQ))
    bias[:CHUNK, SEQ - CHUNK:] = MASKED
    put("chunk_bias", bias)
    put("k_decay", np.exp(log_gamma[None, :] * (P - 1 - i)[:, None]) * HEAD ** -0.5)
    put("q_decay", np.exp(log_gamma[None, :] * (i + 1)[:, None]))
    put("state_decay", np.exp(log_gamma * P).reshape(2, 2)[:, (i >= 64).astype(int)].T)
    freq = []
    for theta, half, rot in ((ROPE_THETA, F_A, 16), (ROPE_THETA, F_C, 8), (RET_THETA, F_B, 64)):
        freq.append(np.float32(theta) ** (-np.arange(half, dtype=np.float32) * np.float32(2.0) / np.float32(rot)))
    put("freq", np.tile(np.concatenate(freq), (P, 1)))
    return c.astype(np.float32)


def signs():
    i = np.arange(P)
    return np.concatenate([np.where(i[:, None] >= i[None, :], -1.0, 0.0), np.full((P, P), -1.0)], 1).astype(np.float32)


def kernel(**inputs):
    import concourse.bacc as bacc
    from concourse.bass_utils import run_bass_kernel_spmd

    a = {k: np.asarray(v) for k, v in inputs.items()}
    tiles = np.concatenate([np.arange(Y_AT[g], Y_AT[g] + WIDTH) for g in OUT_ORDER])
    parts = []
    for name, cols in GROUPS:
        if isinstance(cols, int):
            half = int(name[1])
            g = a["w_out"][:, tiles, 512 * half:512 * half + 512].reshape(DEPTH, KT, P, 512).transpose(0, 2, 1, 3)
        else:
            g = np.concatenate([a["w_in"][:, :, lo:hi] for lo, hi in cols], axis=2)
            g = g.reshape(DEPTH, KT, P, -1).transpose(0, 2, 1, 3)
        parts.append(g.reshape(DEPTH, P, -1))
    lam_init = [0.8 - 0.6 * math.exp(-0.3 * l) for l in range(DEPTH)]
    rows = {"lam_init": np.array(lam_init, np.float32)[:, None],
            "one_minus": np.array([1.0 - v for v in lam_init], np.float32)[:, None]}
    arrays = {
        "x": np.ascontiguousarray(a["x"][0]),
        "pos": np.ascontiguousarray(a["positions"].reshape(TILES, P).T),
        "w": np.ascontiguousarray(np.concatenate(parts, axis=2)),
        "norm_g": np.ascontiguousarray(np.concatenate([a["norm_g"], a["norm_g"][:1]])
                                       .reshape(DEPTH + 1, KT, P).transpose(0, 2, 1)),
        "vecs": np.ascontiguousarray(np.concatenate([rows.get(n, a.get(n)) for n in VECS], axis=1)),
        "w_kv": np.ascontiguousarray(a["w_kv_up"]),
        "consts": constants(),
        "signs": signs(),
    }
    nc = bacc.Bacc("TRN2", target_bir_lowering=False, num_devices=1)
    args = [nc.dram_tensor(f"in_{n}", v.shape, mybir.dt.from_np(v.dtype), kind="ExternalInput").ap()
            for n, v in arrays.items()]
    out = nc.dram_tensor("out", (SEQ, D_MODEL), mybir.dt.float32, kind="ExternalOutput").ap()
    encoder(nc, *args, out)
    r = run_bass_kernel_spmd(nc, [{f"in_{n}": v for n, v in arrays.items()}], core_ids=[0])
    return r.results[0]["out"].reshape(1, SEQ, D_MODEL)
```
